# Optimizing a Trainium2 kernel written in Bass

```python
import math
import jax, jax.numpy as jnp
from jax import lax
import numpy as np

D_MODEL = 2048
BATCH = 1
SEQ = 256
DEPTH = 1

MIX_WIDTH = D_MODEL // 2
N_BRANCHES = 3
EPS = 1e-6
CHUNK = 128
GM_WIDTH = MIX_WIDTH
GM_GROUP_CH = 128
GM_GROUPS = GM_WIDTH // GM_GROUP_CH
S5_WIDTH = MIX_WIDTH
S5_GROUP_CH = 16
S5_GROUPS = S5_WIDTH // S5_GROUP_CH
S5_STATE = 64
DT_MIN = 1e-3
DT_MAX = 1e-1
SB_WIDTH = MIX_WIDTH
SB_HEAD_DIM = 128
SB_HEADS = SB_WIDTH // SB_HEAD_DIM
SB_BLOCK = 128
PROJ_COLS = 2 * GM_WIDTH + S5_WIDTH + 3 * SB_WIDTH + N_BRANCHES * D_MODEL
D_FF = 4 * D_MODEL


def rmsnorm(x, g):
    xf = x.astype(jnp.float32)
    y = xf * lax.rsqrt(jnp.mean(xf * xf, axis=-1, keepdims=True) + EPS)
    return (y * g.astype(jnp.float32)).astype(x.dtype)

def gmlp_mixer(uv, norm_g, w_s, b_s):
    bsz, seq, _ = uv.shape
    z = jax.nn.gelu(uv)
    u, v = jnp.split(z, 2, axis=-1)
    v = rmsnorm(v, norm_g)
    v = v.reshape(bsz, seq // CHUNK, CHUNK, GM_GROUPS, GM_GROUP_CH)
    w = jnp.tril(w_s)
    mixed = jnp.einsum('gts,bcsgh->bctgh', w, v) + jnp.transpose(b_s)[None, None, :, :, None]
    return u * mixed.reshape(bsz, seq, GM_WIDTH)

def s5_mixer(xin, lam_re, lam_im, log_dt, b_re, b_im, c_re, c_im, d, w_glu, b_glu):
    f32 = jnp.float32
    bsz, seq, _ = xin.shape
    u = xin.astype(f32).reshape(bsz, seq, S5_GROUPS, S5_GROUP_CH)
    lam_re = lam_re.astype(f32)
    lam_im = lam_im.astype(f32)
    b_re = b_re.astype(f32)
    b_im = b_im.astype(f32)
    dt = jnp.exp(log_dt.astype(f32))[:, None]
    mag = jnp.exp(lam_re * dt)
    ab_re = mag * jnp.cos(lam_im * dt)
    ab_im = mag * jnp.sin(lam_im * dt)
    den = lam_re * lam_re + lam_im * lam_im
    n_re = ab_re - 1.0
    n_im = ab_im
    k_re = (n_re * lam_re + n_im * lam_im) / den
    k_im = (n_im * lam_re - n_re * lam_im) / den
    bb_re = k_re[..., None] * b_re - k_im[..., None] * b_im
    bb_im = k_re[..., None] * b_im + k_im[..., None] * b_re
    bu_re = jnp.einsum('blgh,gph->blgp', u, bb_re)
    bu_im = jnp.einsum('blgh,gph->blgp', u, bb_im)
    a_re = jnp.broadcast_to(ab_re, bu_re.shape)
    a_im = jnp.broadcast_to(ab_im, bu_im.shape)

    def combine(e_i, e_j):
        ar_i, ai_i, br_i, bi_i = e_i
        ar_j, ai_j, br_j, bi_j = e_j
        return (ar_j * ar_i - ai_j * ai_i,
                ar_j * ai_i + ai_j * ar_i,
                ar_j * br_i - ai_j * bi_i + br_j,
                ar_j * bi_i + ai_j * br_i + bi_j)

    _, _, s_re, s_im = lax.associative_scan(combine, (a_re, a_im, bu_re, bu_im), axis=1)
    y = (jnp.einsum('blgp,ghp->blgh', s_re, c_re.astype(f32))
         - jnp.einsum('blgp,ghp->blgh', s_im, c_im.astype(f32)))
    y = y.reshape(bsz, seq, S5_WIDTH) + d.astype(f32) * xin.astype(f32)
    g = jax.nn.gelu(y)
    out = g * jax.nn.sigmoid(g @ w_glu.astype(f32) + b_glu.astype(f32))
    return out.astype(xin.dtype)

def stick_breaking_attention(q, k, v):
    f32 = jnp.float32
    seq = q.shape[2]
    scale = SB_HEAD_DIM ** -0.5
    outs = []
    for blk in range(seq // SB_BLOCK):
        t0 = blk * SB_BLOCK
        t1 = t0 + SB_BLOCK
        qb = q[:, :, t0:t1].astype(f32)
        kb = k[:, :, :t1].astype(f32)
        vb = v[:, :, :t1].astype(f32)
        z = jnp.einsum('bhtd,bhsd->bhts', qb, kb) * scale
        mask = jnp.arange(t1)[None, :] < jnp.arange(t0, t1)[:, None]
        log_1m = jnp.where(mask, jax.nn.log_sigmoid(-z), 0.0)
        after = lax.cumsum(log_1m, axis=3, reverse=True) - log_1m
        w = jnp.where(mask, jnp.exp(jax.nn.log_sigmoid(z) + after), 0.0)
        outs.append(jnp.einsum('bhts,bhsd->bhtd', w, vb))
    return jnp.concatenate(outs, axis=2).astype(q.dtype)

def first_inputs(seed: int = 0) -> dict:
    key = jax.random.key(seed)
    ks = jax.random.split(key, 32)

    def nrm(k, shape, scale):
        return jax.random.normal(k, shape, jnp.float32) * scale

    x = nrm(ks[0], (BATCH, SEQ, D_MODEL), 1.0)
    norm1_g = 1.0 + nrm(ks[1], (DEPTH, D_MODEL), 0.05)
    w_in = nrm(ks[2], (DEPTH, D_MODEL, PROJ_COLS), D_MODEL ** -0.5)
    b_gate = nrm(ks[3], (DEPTH, N_BRANCHES, D_MODEL), 0.1)
    gm_norm_g = 1.0 + nrm(ks[4], (DEPTH, GM_WIDTH), 0.05)
    gm_w_s = nrm(ks[5], (DEPTH, GM_GROUPS, CHUNK, CHUNK), CHUNK ** -0.5)
    gm_b_s = 1.0 + nrm(ks[6], (DEPTH, GM_GROUPS, CHUNK), 0.1)
    s5_lambda_re = -0.5 + nrm(ks[7], (DEPTH, S5_GROUPS, S5_STATE), 0.01)
    s5_lambda_im = (math.pi * jnp.arange(S5_STATE, dtype=jnp.float32))[None, None, :] \
        + nrm(ks[8], (DEPTH, S5_GROUPS, S5_STATE), 0.01)
    s5_log_dt = jax.random.uniform(ks[9], (DEPTH, S5_GROUPS), jnp.float32,
                                   math.log(DT_MIN), math.log(DT_MAX))
    s5_b_re = nrm(ks[10], (DEPTH, S5_GROUPS, S5_STATE, S5_GROUP_CH), (2 * S5_GROUP_CH) ** -0.5)
    s5_b_im = nrm(ks[11], (DEPTH, S5_GROUPS, S5_STATE, S5_GROUP_CH), (2 * S5_GROUP_CH) ** -0.5)
    s5_c_re = nrm(ks[12], (DEPTH, S5_GROUPS, S5_GROUP_CH, S5_STATE), (2 * S5_STATE) ** -0.5)
    s5_c_im = nrm(ks[13], (DEPTH, S5_GROUPS, S5_GROUP_CH, S5_STATE), (2 * S5_STATE) ** -0.5)
    s5_d = nrm(ks[14], (DEPTH, S5_WIDTH), 1.0)
    s5_w_glu = nrm(ks[15], (DEPTH, S5_WIDTH, S5_WIDTH), S5_WIDTH ** -0.5)
    s5_b_glu = nrm(ks[16], (DEPTH, S5_WIDTH), 0.02)
    w_branch = nrm(ks[17], (DEPTH, N_BRANCHES, MIX_WIDTH, D_MODEL), MIX_WIDTH ** -0.5)
    w_out = nrm(ks[18], (DEPTH, D_MODEL, D_MODEL), D_MODEL ** -0.5)
    norm2_g = 1.0 + nrm(ks[19], (DEPTH, D_MODEL), 0.05)
    w_mlp_in = nrm(ks[20], (DEPTH, D_MODEL, D_FF), D_MODEL ** -0.5)
    w_mlp_out = nrm(ks[21], (DEPTH, D_FF, D_MODEL), D_FF ** -0.5)
    final_g = 1.0 + nrm(ks[22], (D_MODEL,), 0.05)
    return {"x": x, "norm1_g": norm1_g, "w_in": w_in, "b_gate": b_gate,
            "gm_norm_g": gm_norm_g, "gm_w_s": gm_w_s, "gm_b_s": gm_b_s,
            "s5_lambda_re": s5_lambda_re, "s5_lambda_im": s5_lambda_im, "s5_log_dt": s5_log_dt,
            "s5_b_re": s5_b_re, "s5_b_im": s5_b_im, "s5_c_re": s5_c_re, "s5_c_im": s5_c_im,
            "s5_d": s5_d, "s5_w_glu": s5_w_glu, "s5_b_glu": s5_b_glu,
            "w_branch": w_branch, "w_out": w_out, "norm2_g": norm2_g,
            "w_mlp_in": w_mlp_in, "w_mlp_out": w_mlp_out, "final_g": final_g}

def first_block(x, norm1_g, w_in, b_gate, gm_norm_g, gm_w_s, gm_b_s,
              s5_lambda_re, s5_lambda_im, s5_log_dt, s5_b_re, s5_b_im, s5_c_re, s5_c_im,
              s5_d, s5_w_glu, s5_b_glu, w_branch, w_out, norm2_g,
              w_mlp_in, w_mlp_out, final_g):
    bsz, seq, _ = x.shape
    o_a = 2 * GM_WIDTH
    o_b = o_a + S5_WIDTH
    o_c = o_b + 3 * SB_WIDTH
    for l in range(DEPTH):
        h = rmsnorm(x, norm1_g[l])
        proj = h @ w_in[l]
        uv = proj[..., :o_a]
        s5_in = proj[..., o_a:o_b]
        qkv = proj[..., o_b:o_c].reshape(bsz, seq, 3, SB_HEADS, SB_HEAD_DIM)
        qkv = jnp.transpose(qkv, (2, 0, 3, 1, 4))
        gates = jax.nn.sigmoid(proj[..., o_c:].reshape(bsz, seq, N_BRANCHES, D_MODEL) + b_gate[l])

        y_a = gmlp_mixer(uv, gm_norm_g[l], gm_w_s[l], gm_b_s[l])
        y_b = s5_mixer(s5_in, s5_lambda_re[l], s5_lambda_im[l], s5_log_dt[l],
                       s5_b_re[l], s5_b_im[l], s5_c_re[l], s5_c_im[l],
                       s5_d[l], s5_w_glu[l], s5_b_glu[l])
        y_c = stick_breaking_attention(qkv[0], qkv[1], qkv[2])
        y_c = jnp.transpose(y_c, (0, 2, 1, 3)).reshape(bsz, seq, SB_WIDTH)

        ys = jnp.stack([y_a, y_b, y_c], axis=2)
        br = jnp.einsum('blnw,nwd->blnd', ys, w_branch[l])
        merged = jnp.sum(gates * br, axis=2)
        x = x + merged @ w_out[l]
        h2 = rmsnorm(x, norm2_g[l])
        x = x + jnp.square(jax.nn.relu(h2 @ w_mlp_in[l])) @ w_mlp_out[l]
    return rmsnorm(x, final_g)


CHUNK_2 = 64

D_A = 768
K_A = 31
POOL_WINDOWS = (2, 4, 8, 16)
N_POOL_GROUPS = 4
POOL_GROUP = 128
D_B = N_POOL_GROUPS * POOL_GROUP
D_C = 768
K_C = 3
D_IN = 2 * D_A + D_B + 3 * D_C
N_BRANCH = 3
D_FF_2 = 4 * D_MODEL


def rmsnorm_2(x, g):
    xf = x.astype(jnp.float32)
    y = xf * lax.rsqrt(jnp.mean(xf * xf, axis=-1, keepdims=True) + EPS)
    return (y * g.astype(jnp.float32)).astype(x.dtype)

def layernorm(x, g, b):
    xf = x.astype(jnp.float32)
    mu = jnp.mean(xf, axis=-1, keepdims=True)
    xc = xf - mu
    var = jnp.mean(xc * xc, axis=-1, keepdims=True)
    y = xc * lax.rsqrt(var + EPS) * g.astype(jnp.float32) + b.astype(jnp.float32)
    return y.astype(x.dtype)

def causal_dwconv(u, w):
    k, c = w.shape
    return lax.conv_general_dilated(
        u, w[:, None, :].astype(u.dtype), window_strides=(1,), padding=[(k - 1, 0)],
        dimension_numbers=("NWC", "WIO", "NWC"), feature_group_count=c)

def multiscale_pool(u, w_grp, scale):
    b, s, _ = u.shape
    ug = u.reshape(b, s, N_POOL_GROUPS, POOL_GROUP).astype(jnp.float32)
    cs = jnp.cumsum(ug, axis=1)
    pos = jnp.arange(1, s + 1, dtype=jnp.float32)
    means = []
    for gi, w in enumerate(POOL_WINDOWS):
        c = cs[:, :, gi]
        lag = jnp.pad(c, ((0, 0), (w, 0), (0, 0)))[:, :s]
        cnt = jnp.minimum(pos, float(w))[None, :, None]
        means.append((c - lag) / cnt)
    pooled = (jnp.stack(means, axis=2) - ug).astype(u.dtype)
    mixed = jnp.einsum("bsgc,gcd->bsgd", pooled, w_grp)
    return mixed.reshape(b, s, D_B) * scale

def second_inputs(seed: int = 0) -> dict:
    key = jax.random.key(seed)
    ks = jax.random.split(key, 24)
    f32 = jnp.float32
    nrm = lambda k, shape, scale: jax.random.normal(k, shape, f32) * scale
    L, D = DEPTH, D_MODEL
    return {
        "x": jax.random.normal(ks[0], (BATCH, SEQ, D), f32),
        "g_mix": 1.0 + nrm(ks[1], (L, D), 0.02),
        "w_in": nrm(ks[2], (L, D, D_IN), D ** -0.5),
        "w_gate": nrm(ks[3], (L, D, N_BRANCH * D), D ** -0.5),
        "b_gate": nrm(ks[4], (L, N_BRANCH * D), 0.01),
        "b_glu": nrm(ks[5], (L, 2 * D_A), 0.01),
        "w_dw_a": nrm(ks[6], (L, K_A, D_A), K_A ** -0.5),
        "b_dw_a": nrm(ks[7], (L, D_A), 0.01),
        "ln_g_a": 1.0 + nrm(ks[8], (L, D_A), 0.02),
        "ln_b_a": nrm(ks[9], (L, D_A), 0.01),
        "w_a_out": nrm(ks[10], (L, D_A, D), D_A ** -0.5),
        "w_pool_grp": nrm(ks[11], (L, N_POOL_GROUPS, POOL_GROUP, POOL_GROUP), POOL_GROUP ** -0.5),
        "pool_scale": 1.0 + nrm(ks[12], (L, D_B), 0.02),
        "w_b_out": nrm(ks[13], (L, D_B, D), D_B ** -0.5),
        "w_dw_c": nrm(ks[14], (L, K_C, D_C), K_C ** -0.5),
        "w_c_out": nrm(ks[15], (L, D_C, D), D_C ** -0.5),
        "w_o": nrm(ks[16], (L, D, D), D ** -0.5),
        "g_mlp": 1.0 + nrm(ks[17], (L, D), 0.02),
        "w_up": nrm(ks[18], (L, D, D_FF_2), D ** -0.5),
        "w_down": nrm(ks[19], (L, D_FF_2, D), 0.5 * D_FF_2 ** -0.5),
        "g_final": 1.0 + nrm(ks[20], (D,), 0.02),
    }

def second_block(x, g_mix, w_in, w_gate, b_gate, b_glu, w_dw_a, b_dw_a, ln_g_a, ln_b_a, w_a_out,
              w_pool_grp, pool_scale, w_b_out, w_dw_c, w_c_out, w_o, g_mlp, w_up, w_down, g_final):
    b, s, d = x.shape
    for l in range(DEPTH):
        h = rmsnorm_2(x, g_mix[l])
        z = h @ w_in[l]
        za = z[..., : 2 * D_A] + b_glu[l]
        zb = z[..., 2 * D_A: 2 * D_A + D_B]
        zc = z[..., 2 * D_A + D_B:]

        ua = za[..., :D_A] * jax.nn.sigmoid(za[..., D_A:])
        va = causal_dwconv(ua, w_dw_a[l]) + b_dw_a[l]
        va = jax.nn.silu(layernorm(va, ln_g_a[l], ln_b_a[l]))
        ya = va @ w_a_out[l]

        yb = multiscale_pool(zb, w_pool_grp[l], pool_scale[l]) @ w_b_out[l]

        gb, gc, xv = zc[..., :D_C], zc[..., D_C: 2 * D_C], zc[..., 2 * D_C:]
        yc = (gb * causal_dwconv(gc * xv, w_dw_c[l])) @ w_c_out[l]

        gates = jax.nn.sigmoid(h @ w_gate[l] + b_gate[l]).reshape(b, s, N_BRANCH, d)
        merged = gates[:, :, 0] * ya + gates[:, :, 1] * yb + gates[:, :, 2] * yc
        x = x + merged @ w_o[l]

        h2 = rmsnorm_2(x, g_mlp[l])
        x = x + jnp.square(jax.nn.relu(h2 @ w_up[l])) @ w_down[l]
    return rmsnorm_2(x, g_final)


_first_inputs = second_inputs


def second_inputs(seed=0):
    import zlib

    import numpy as np

    out = dict(_first_inputs(seed))
    spreads = {}
    factors = {'g_mix': 2.92,
     'b_gate': 22.136,
     'b_glu': 64.0,
     'b_dw_a': 40.641,
     'ln_g_a': 64.0,
     'ln_b_a': 64.0,
     'pool_scale': 33.347,
     'g_mlp': 19.592,
     'g_final': 8.278}
    for name, (base, spread) in spreads.items():
        noise = np.random.default_rng([zlib.crc32(name.encode()), seed]).standard_normal(out[name].shape)
        drawn = base * np.exp(spread * noise) if base else spread * noise
        out[name] = __import__('jax').numpy.asarray(drawn.astype(out[name].dtype))
    for name, factor in factors.items():
        out[name] = (out[name] * factor).astype(out[name].dtype)
    return out


_narrow_inputs = second_inputs


def second_inputs(seed=0):

    out = dict(_narrow_inputs(seed))
    wider = {'ln_g_a': 6.17, 'ln_b_a': 12.0, 'pool_scale': 3.31, 'g_final': 3.24}
    for name, times in wider.items():
        mean = out[name].mean()
        out[name] = (mean + times * (out[name] - mean)).astype(out[name].dtype)
    return out


def setup_inputs(seed=0):
    out = dict(first_inputs(seed))
    for name, value in second_inputs(seed + 1).items():
        if name != "x":
            out[name + "_2"] = value
    return out


def reference(
    x, norm1_g, w_in, b_gate, gm_norm_g, gm_w_s, gm_b_s, s5_lambda_re, s5_lambda_im, s5_log_dt,
    s5_b_re, s5_b_im, s5_c_re, s5_c_im, s5_d, s5_w_glu, s5_b_glu, w_branch, w_out, norm2_g,
    w_mlp_in, w_mlp_out, final_g, g_mix_2, w_in_2, w_gate_2, b_gate_2, b_glu_2, w_dw_a_2,
    b_dw_a_2, ln_g_a_2, ln_b_a_2, w_a_out_2, w_pool_grp_2, pool_scale_2, w_b_out_2, w_dw_c_2,
    w_c_out_2, w_o_2, g_mlp_2, w_up_2, w_down_2, g_final_2,
):
    x = first_block(
        x, norm1_g, w_in, b_gate, gm_norm_g, gm_w_s, gm_b_s, s5_lambda_re, s5_lambda_im,
        s5_log_dt, s5_b_re, s5_b_im, s5_c_re, s5_c_im, s5_d, s5_w_glu, s5_b_glu, w_branch,
        w_out, norm2_g, w_mlp_in, w_mlp_out, final_g,
    )
    return second_block(
        x, g_mix_2, w_in_2, w_gate_2, b_gate_2, b_glu_2, w_dw_a_2, b_dw_a_2, ln_g_a_2, ln_b_a_2,
        w_a_out_2, w_pool_grp_2, pool_scale_2, w_b_out_2, w_dw_c_2, w_c_out_2, w_o_2, g_mlp_2,
        w_up_2, w_down_2, g_final_2,
    )


_drawn_inputs = setup_inputs


def setup_inputs(seed=0):
    import zlib

    import numpy as np

    out = dict(_drawn_inputs(seed))
    spreads = {}
    factors = {'gm_norm_g': 3.339,
     's5_lambda_re': 64.0,
     's5_lambda_im': 30.184,
     's5_log_dt': 30.168,
     's5_b_re': 42.136,
     's5_b_im': 42.216,
     's5_c_re': 41.984,
     's5_c_im': 41.72,
     's5_b_glu': 29.852}
    for name, (base, spread) in spreads.items():
        noise = np.random.default_rng([zlib.crc32(name.encode()), seed]).standard_normal(out[name].shape)
        drawn = base * np.exp(spread * noise) if base else spread * noise
        out[name] = __import__('jax').numpy.asarray(drawn.astype(out[name].dtype))
    for name, factor in factors.items():
        out[name] = (out[name] * factor).astype(out[name].dtype)
    return out
```

```python
from collections import deque
from contextlib import ExitStack

import numpy as np
import concourse.bass as bass
from concourse import mybir

F32 = mybir.dt.float32
F32R = mybir.dt.float32r
I32 = mybir.dt.int32
ALU = mybir.AluOpType
ACT = mybir.ActivationFunctionType

P = 128
D = 2048
L = 256
EPS = 1e-6
NRAW = 4
NSPL = 4
POOL_W = (2, 4, 8, 16)
PI_DOWN = 3.1415925
NV = 11


class Queue:

    def __init__(self, sem):
        self.sem, self.n, self.items = sem, 0, []

    def __call__(self, fn, *waits, inc=True):
        self.items.append((fn, list(flat(waits)), (self.sem, 1) if inc else None))
        self.n += inc
        return (self.sem, self.n)

    def now(self):
        return (self.sem, self.n)

    def play(self, eng):
        seen = {}
        for fn, waits, inc in self.items:
            for sem, val in waits:
                if seen.get(sem.name, 0) < val:
                    eng.wait_ge(sem, val)
                    seen[sem.name] = val
            ins = fn(eng)
            if inc:
                ins.then_inc(*inc)


def flat(waits):
    for w in waits:
        if isinstance(w, list):
            yield from flat(w)
        elif w is not None and w[1] > 0:
            yield w


def consts():
    c = np.zeros((P, 3 * P + 2), np.float32)
    i = np.arange(P)
    c[:, 0:P] = np.eye(P)
    c[:, P:2 * P] = i[:, None] >= i[None, :]
    c[:, 2 * P:3 * P] = 1.0
    c[i, 3 * P + (i // 16) % 2] = 1.0
    s, t = np.arange(L)[:, None], np.arange(L)[None, :]
    m = np.zeros((P, 4, 2, L), np.float32)
    for g, w in enumerate(POOL_W):
        band = ((s <= t) & (s > t - w)) / np.minimum(t + 1, w).astype(np.float64) - (s == t)
        m[:, g] = band.astype(np.float32).reshape(2, P, L).transpose(1, 0, 2)
    return c, m


def build(nc, a, out, upto=99):
    ctx = ExitStack()

    def sem(name):
        return ctx.enter_context(nc.semaphore(name))

    T, A, V, G, S = (Queue(sem("q_" + n)) for n in ("tensor", "scalar", "vector", "pool", "sync"))

    def sb(name, shape, dt=F32, to=ctx):
        return to.enter_context(nc.sbuf_tensor(name, shape, dt))

    dma_count = {}

    def dma(name, dst, src, *waits):
        if name not in dma_count:
            dma_count[name] = [sem("d_" + name), 0]
        rec = dma_count[name]
        rec[1] += 16
        s = rec[0]
        S.items.append((lambda e: e.dma_start(dst, src).then_inc(s, 16), list(flat(waits)), None))
        return (s, rec[1])

    def row(ap, n):
        return ap.rearrange("(a n) -> a n", a=1).to_broadcast([P, n])

    def everything():
        return [q.now() for q in (T, A, V, G)]

    X = sb("X", [P, 2, D])
    XTH, XTL = sb("XTH", [P, 16, L], F32R), sb("XTL", [P, 16, L], F32R)
    RAW = [sb(f"RAW{i}", [P, 2, 512]) for i in range(NRAW)]
    WH = [sb(f"WH{i}", [P, 2, 512], F32R) for i in range(NSPL)]
    WL = [sb(f"WL{i}", [P, 2, 512], F32R) for i in range(NSPL)]
    YAH, YAL = sb("YAH", [P, 8, L], F32R), sb("YAL", [P, 8, L], F32R)
    CST = sb("CST", [P, 3 * P + 2])
    VEC = sb("VEC", [P, 94])
    DWT = sb("DWT", [P, 6, 34])
    ST = sb("ST", [P, 96])
    GB = [sb(f"GB{i}", [P, 512]) for i in range(2)]
    IDENT, TRI, ONES, PAR = CST[:, 0:P], CST[:, P:2 * P], CST[:, 2 * P:3 * P], CST[:, 3 * P:3 * P + 2]
    ACC = ctx.enter_context(nc.psum_tensor("ACC", [P, 4, 512], F32))
    TB = [ctx.enter_context(nc.psum_tensor(f"TB{i}", [P, 512], F32)) for i in range(4)]

    st_used = [0]

    def stat(n):
        st_used[0] += n
        return ST[:, st_used[0] - n:st_used[0]]

    bank_free = [[] for _ in TB]
    bank_next = [0]

    def bank():
        i = bank_next[0] % 4
        bank_next[0] += 1
        assert bank_free[i] is not None
        free, bank_free[i] = bank_free[i], None
        return i, TB[i], free

    def bank_done(i, *evs):
        bank_free[i] = list(evs)

    side = deque()

    def side_step():
        while side:
            try:
                next(side[0])
                return
            except StopIteration:
                side.popleft()

    def side_drain(gen):
        while gen in side:
            side_step()

    w_in1, w_in2 = a["w_in"][0], a["w_in_2"][0]
    wg2 = a["w_gate_2"][0]
    wbr = [a["w_branch"][0, n] for n in range(3)]
    plan = []

    def planned(w, nk, c0, n=512):
        plan.append((w, nk, c0, n))

    def plan_branch(gate, g0, w, nk, wide):
        if wide:
            for c in range(4):
                planned(gate, 16, g0 + 512 * c)
            for c in range(4):
                planned(w, nk, 512 * c)
        else:
            for c in range(4):
                planned(gate, 16, g0 + 512 * c)
                planned(w, nk, 512 * c)

    def plan_mlp(wi, wo):
        for j in range(9):
            if j < 8:
                for b in range(2):
                    planned(wi, 16, 1024 * j + 512 * b)
            if j > 0:
                for c in range(4):
                    planned(wo[1024 * (j - 1):1024 * j, :], 8, 512 * c)

    GATE0 = 6144
    for c in (4, 5, 2, 3, 0, 1):
        planned(w_in1, 16, 512 * c)
    plan_branch(w_in1, GATE0, wbr[0], 8, False)
    for c in range(6, 12):
        planned(w_in1, 16, 512 * c)
    for c in range(2):
        planned(a["s5_w_glu"][0], 8, 512 * c)
    plan_branch(w_in1, GATE0 + 2 * D, wbr[2], 8, True)
    plan_branch(w_in1, GATE0 + D, wbr[1], 8, True)
    for c in range(4):
        planned(a["w_out"][0], 16, 512 * c)
    plan_mlp(a["w_mlp_in"][0], a["w_mlp_out"][0])
    ZC0 = 2048
    for c in range(3):
        planned(w_in2, 16, 512 * c)
    for c in range(5):
        planned(w_in2, 16, ZC0 + 512 * c, 512 if c < 4 else 256)
    planned(w_in2, 16, 1536)
    plan_branch(wg2, D, a["w_b_out_2"][0], 4, False)
    plan_branch(wg2, 2 * D, a["w_c_out_2"][0], 6, False)
    plan_branch(wg2, 0, a["w_a_out_2"][0], 6, True)
    for c in range(4):
        planned(a["w_o_2"][0], 16, 512 * c)
    plan_mlp(a["w_up_2"][0], a["w_down_2"][0])

    units = [(w, 2 * i, c0, n) for w, nk, c0, n in plan for i in range(nk // 2)]
    landed, split, used = {}, {}, {}
    sent, cut = [0], [0]

    def send(upto_u):
        while sent[0] < min(upto_u, len(units)):
            u = sent[0]
            w, k, c0, n = units[u]
            src = w[k * P:(k + 2) * P, c0:c0 + n].rearrange("(t p) n -> p t n", p=P)
            landed[u] = dma(f"raw{u % NRAW}", RAW[u % NRAW][:, :, 0:n], src, split.get(u - NRAW))
            sent[0] += 1

    def cut_units(upto_u):
        while cut[0] < min(upto_u, len(units)):
            u = cut[0]
            send(u + 1)
            n = units[u][3]
            r, h, l = (b[:, :, 0:n] for b in (RAW[u % NRAW], WH[u % NSPL], WL[u % NSPL]))
            ev = A(lambda e, h=h, r=r: e.activation(h, r, ACT.Copy), landed[u], used.get(u - NSPL))
            split[u] = V(lambda e, l=l, r=r, h=h: e.tensor_tensor(l, r, h, ALU.subtract),
                         ev, used.get(u - NSPL))
            cut[0] += 1
            send(u + 1 + NRAW)

    acc_free = [[], []]
    at = {"unit": 0, "block": 0}

    def product(w, nk, c0, xh, xl, ready, n=512, rate=1):
        s = at["block"] % 2
        pw, pk, pc, pn = plan[at["block"]]
        assert (pk, pc, pn) == (nk, c0, n) and pw.tensor.name == w.tensor.name
        at["block"] += 1
        ev = None
        for i in range(nk // 2):
            u = at["unit"]
            at["unit"] += 1
            cut_units(u + NSPL - 1)
            h, l = WH[u % NSPL], WL[u % NSPL]

            def mm(e, i=i, h=h, l=l):
                for half in range(2):
                    for t in range(2):
                        k = 2 * i + t
                        xs = slice(half * P, half * P + P)
                        for m, (p, q) in enumerate(((xh, h), (xh, l), (xl, h))):
                            ins = e.matmul(ACC[:, 2 * s + half, 0:n], p[:, k, xs], q[:, t, 0:n],
                                           start=(k == 0 and m == 0), stop=(k == nk - 1 and m == 2))
                return ins

            ev = used[u] = T(mm, split[u], ready[i] if ready else None, acc_free[s] if i == 0 else None)
            for _ in range(rate):
                side_step()
        return s, ev

    def turn(src, kts, yh, yl, *waits, free=None, gain=None):
        evs = []
        for k in range(0, kts, 2):
            b, t, bf = bank()

            def tr(e, k=k, t=t):
                for m in range(2):
                    for half in range(2):
                        ins = e.transpose(t[:, m * L + half * P:m * L + half * P + P], src(k + m, half), IDENT)
                return ins

            ev = T(tr, bf, *waits)
            tv = t[:, :].rearrange("p (m t) -> p m t", m=2)
            if gain is None:
                e1 = A(lambda e, k=k, tv=tv: e.activation(yh[:, k:k + 2, :], tv, ACT.Copy), ev, free)
                e2 = V(lambda e, k=k, tv=tv: e.tensor_tensor(yl[:, k:k + 2, :], tv, yh[:, k:k + 2, :], ALU.subtract),
                       e1, free)
            else:
                for m in range(2):
                    e1 = A(lambda e, k=k + m, tv=tv[:, m, :]: e.activation(yh[:, k, :], tv, ACT.Copy, scale=gain(k)),
                           ev, free)
                for m in range(2):
                    e2 = V(lambda e, k=k + m, tv=tv[:, m, :]: e.scalar_tensor_tensor(
                        out=yl[:, k, :], in0=tv, scalar=gain(k), in1=yh[:, k, :], op0=ALU.mult, op1=ALU.subtract),
                        e1, free)
            bank_done(b, e2)
            evs.append(e2)
        return evs

    def rms(x, width, n, *waits):
        ss, rs = stat(n), stat(n)
        junk = ACC[:, :, :].rearrange("p b n -> p (b n)")[:, 0:width]
        ev = None
        for i in range(n):
            ev = A(lambda e, i=i: e.activation(junk, x(i), ACT.Square, accum_out=ss[:, i:i + 1]),
                   *waits, acc_free, ev)
        acc_free[0], acc_free[1] = [ev], [ev]
        return rs, finish_rms(ss, rs, width, ev)

    def finish_rms(ss, rs, width, *waits):
        ev = V(lambda e: e.tensor_scalar(ss, ss, 1.0 / width, EPS, ALU.mult, ALU.add), *waits)
        ev = A(lambda e: e.activation(ss, ss, ACT.Sqrt), ev)
        return V(lambda e: e.reciprocal(rs, ss), ev)

    def normed(x, dst, gcol, *waits, free=None, dfree=None):
        rs, ev = rms(lambda i: x[:, i, :], D, 2, *waits)
        e0 = A(lambda e: e.activation(dst[:, 0, :], x[:, 0, :], ACT.Copy, scale=rs[:, 0:1]), ev, dfree)
        e1 = V(lambda e: e.tensor_scalar(dst[:, 1, :], x[:, 1, :], rs[:, 1:2], None, ALU.mult), ev, dfree)
        return turn(lambda k, half: dst[:, half, k * P:k * P + P], 16, XTH, XTL, e0, e1, free=free,
                    gain=lambda k: VEC[:, gcol + k:gcol + k + 1])

    gb_used = [0]
    gb_free = [None, None]

    def gate_branch(gate, g0, bias, w, nk, ready, yready, merged, SG, first, mfree, wide, rate=1, last=None):
        res = []

        def do_gate(c):
            i = gb_used[0] % 2
            gb_used[0] += 1
            eb = dma(f"gb{i}", GB[i][:, :], row(bias[512 * c:512 * c + 512], 512), gb_free[i])
            s, ev = product(gate, 16, g0 + 512 * c, XTH, XTL, ready if c == 0 else None, rate=rate)
            sg = SG[:, :, 512 * c:512 * c + 512] if wide else SG
            for half in range(2):
                e1 = V(lambda e, half=half: e.tensor_tensor(sg[:, half, :], ACC[:, 2 * s + half, :], GB[i][:, :],
                                                            ALU.add), ev, eb, sg_free[c if wide else 0])
            acc_free[s] = [e1]
            gb_free[i] = e1
            return A(lambda e: e.activation(sg, sg, ACT.Sigmoid), e1), ev

        def do_branch(c, es):
            s, ev = product(w, nk, 512 * c, YAH, YAL, yready() if c == 0 else None, rate=rate)
            sg = SG[:, :, 512 * c:512 * c + 512] if wide else SG
            m = merged[:, :, 512 * c:512 * c + 512]
            av = ACC[:, 2 * s:2 * s + 2, :]
            if first:
                e1 = V(lambda e: e.tensor_tensor(m, av, sg, ALU.mult), ev, es, mfree)
                acc_free[s] = [e1]
                sg_free[c if wide else 0] = e1
            else:
                e0 = V(lambda e: e.tensor_tensor(sg, av, sg, ALU.mult), ev, es)
                acc_free[s] = [e0]
                e1 = G(lambda e: e.tensor_tensor(m, m, sg, ALU.add), e0, mfree)
                sg_free[c if wide else 0] = e1
            res.append(e1)
            if last:
                last(c, e1, gates_done)
            return ev

        sg_free = [everything() if c == 0 else None for c in range(4)]
        gates_done = None
        if wide:
            es = []
            for c in range(4):
                e, gates_done = do_gate(c)
                es.append(e)
            for c in range(4):
                ev = do_branch(c, es[c])
        else:
            for c in range(4):
                e, gates_done = do_gate(c)
                ev = do_branch(c, e)
        return res, ev, gates_done

    def residual_product(w, x, ready, xready):
        evs = []
        for c in range(4):
            s, ev = product(w, 16, 512 * c, XTH, XTL, ready if c == 0 else [ready[-1]] * 8)
            xv = x[:, :, 512 * c:512 * c + 512]
            e1 = V(lambda e, s=s, xv=xv: e.tensor_tensor(xv, xv, ACC[:, 2 * s:2 * s + 2, :], ALU.add), ev, xready)
            acc_free[s] = [e1]
            evs.append(e1)
        return evs, ev

    def mlp(tag, wi, wo, x, ready, xready):
        evs = []
        with ExitStack() as sc:
            fence = everything()
            YBH, YBL = sb("YBH" + tag, [P, 8, L], F32R, sc), sb("YBL" + tag, [P, 8, L], F32R, sc)
            HB = [sb(f"HB{i}" + tag, [P, 2, 512], F32, sc) for i in range(2)]
            hb_free = [fence, fence]
            Y = [(YAH, YAL), (YBH, YBL)]
            y_free = [fence, fence]
            hready = {}
            for j in range(9):
                if j < 8:
                    hready[j] = []
                    for b in range(2):
                        s, ev = product(wi, 16, 1024 * j + 512 * b, XTH, XTL, ready if j + b == 0 else None)
                        hb = HB[b]
                        e1 = A(lambda e, s=s, hb=hb: e.activation(hb[:, :, :], ACC[:, 2 * s:2 * s + 2, :], ACT.Relu),
                               ev, hb_free[b])
                        acc_free[s] = [e1]
                        e2 = A(lambda e, hb=hb: e.activation(hb[:, :, :], hb[:, :, :], ACT.Square), e1)
                        yh, yl = Y[j % 2]
                        hready[j] += turn(lambda k, half, hb=hb: hb[:, half, k * P:k * P + P], 4,
                                          yh[:, 4 * b:4 * b + 4, :], yl[:, 4 * b:4 * b + 4, :], e2, free=y_free[j % 2])
                        hb_free[b] = T.now()
                    xlast = ev
                if j > 0:
                    wj = wo[1024 * (j - 1):1024 * j, :]
                    yh, yl = Y[(j - 1) % 2]
                    evs = []
                    for c in range(4):
                        s, ev = product(wj, 8, 512 * c, yh, yl, hready[j - 1] if c == 0 else None)
                        xv = x[:, :, 512 * c:512 * c + 512]
                        e1 = V(lambda e, s=s, xv=xv: e.tensor_tensor(xv, xv, ACC[:, 2 * s:2 * s + 2, :], ALU.add),
                               ev, xready)
                        acc_free[s] = [e1]
                        evs.append(e1)
                    y_free[(j - 1) % 2] = ev
        return evs, xlast

    x0 = a["x"][0].rearrange("(h p) n -> p h n", p=P)
    ld_x = dma("x", X[:, :, :], x0)
    ld_c = dma("cst", CST[:, :], a["cst"])

    one = ExitStack()
    XIN = sb("XIN", [P, 2, 1024], to=one)
    s5 = ExitStack()
    CT = sb("CT", [P, 2, 8, P], to=s5)
    SS = sb("SS", [P, 2, 16, L], to=s5)
    AP = sb("AP", [P, 3, 32, 16], to=s5)
    TMP = sb("TMP", [P, 2, 2, 256], to=s5)
    PR = sb("PR", [P, 24, 32], to=s5)
    VG = sb("VG", [P, 2, 1024], to=s5)
    UG = sb("UG", [P, 2, 512], to=s5)
    WS = sb("WS", [P, 8, P], to=s5)
    SGA = sb("SGA", [P, 2, 512], to=s5)
    VST = sb("VST", [94, P], to=s5)
    S5ST = sb("S5ST", [32, 3, P], to=s5)
    LDT = sb("LDT", [32, 2], to=s5)
    pool = SS[:, :, :, :].rearrange("p a j t -> p (a j t)")
    BRI = pool[:, 0:1024].rearrange("p (a j h) -> p a j h", a=2, j=32)
    EX = pool[:, 1024:3072].rearrange("p (a j g h) -> p a j g h", a=2, j=32, g=2)
    CRI = pool[:, 3072:4096].rearrange("p (a q s) -> p a q s", a=2, q=8)
    CX = pool[:, 4096:6144].rearrange("p (a q g s) -> p a q g s", a=2, q=8, g=2)
    GW = pool[:, 6144:7168].rearrange("p (g s) -> p g s", g=8)
    DB = pool[:, 7168:8192]
    DWS = VG[:, :, :].rearrange("p a n -> p (a n)")[0:34, 0:768]
    GMG = UG[:, :, :].rearrange("p a n -> p (a n)")

    r0 = 0
    for name, n in (("norm1_g", 16), ("norm2_g", 16), ("g_mix_2", 16), ("g_mlp_2", 16), ("gm_b_s", 8),
                    ("ln_g_a_2", 6), ("ln_b_a_2", 6), ("b_dw_a_2", 6), ("pool_scale_2", 4)):
        v = a[name]
        src = v[0] if name == "gm_b_s" else v[0].rearrange("(r p) -> r p", p=P)
        ld_v = dma("vec", VST[r0:r0 + n, :], src)
        r0 += n
    V_N1, V_N2, V_MIX, V_MLP, V_GB, V_LG, V_LB, V_DB, V_PS = 0, 16, 32, 48, 64, 72, 78, 84, 90
    dma("s5p", S5ST[:, 0, :], a["s5_lambda_re"][0].rearrange("(j g) p -> j (g p)", g=2))
    dma("s5p", S5ST[:, 1, :], a["s5_lambda_im"][0].rearrange("(j g) p -> j (g p)", g=2))
    ld_s = dma("s5p", LDT[:, :], a["s5_log_dt"][0].rearrange("(j g) -> j g", g=2))
    send(NRAW)
    dma("dw", DWS[0:31, :], a["w_dw_a_2"][0])
    ld_dw = dma("dw", DWS[31:34, :], a["w_dw_c_2"][0])
    for i, n in enumerate(("s5_b_re", "s5_b_im")):
        ld_b = dma("s5b", BRI[:, i, :, :], a[n][0].rearrange("(j g) p h -> (g p) j h", g=2))
    for i, n in enumerate(("s5_c_re", "s5_c_im")):
        ld_cc = dma("s5c", CRI[:, i, :, :], a[n][0].rearrange("(q g) h p -> (g h) q p", q=8))
    ld_gw = dma("gw", GW, a["gm_w_s"][0].rearrange("g t s -> t g s"))
    ld_d = dma("sd", DB, row(a["s5_d"][0], 1024))
    ld_gmg = dma("gmg", GMG, row(a["gm_norm_g"][0], 1024))

    b, t, bf = bank()
    ev = T(lambda e, t=t: e.transpose(t[:, 0:94], VST[:, :], IDENT[0:94, 0:94]), ld_v, ld_c, bf)
    ev_vec = V(lambda e, t=t: e.tensor_copy(VEC[:, :], t[:, 0:94]), ev)
    bank_done(b, ev_vec)

    ready = normed(X, X, V_N1, ld_x, ev_vec)
    ev_x_read = T.now()

    ev = V(lambda e: e.tensor_copy(S5ST[:, 2, :].rearrange("j (g p) -> j g p", g=2),
                                   LDT[:, :].unsqueeze(2).to_broadcast([32, 2, 64])), ld_s)
    b, t, bf = bank()

    def tr3(e, t=t):
        for i in range(3):
            ins = e.transpose(t[:, 32 * i:32 * i + 32], S5ST[:, i, :], IDENT[0:32, 0:32])
        return ins

    ev = T(tr3, ev, bf)
    pr = lambda i: PR[:, i, :]
    ev = V(lambda e, t=t: e.tensor_copy(PR[:, 0:3, :], t[:, 0:96].rearrange("p (i j) -> p i j", i=3)), ev)
    bank_done(b, ev)

    def vtt(o, x, y, op, *w):
        return V(lambda e: e.tensor_tensor(o, x, y, op), *w)

    def vts(o, x, s1, s2, o1, o2, *w):
        return V(lambda e: e.tensor_scalar(o, x, s1, s2, o1, o2), *w)

    def vstt(o, x, s, y, o1, o2, *w):
        return V(lambda e: e.scalar_tensor_tensor(out=o, in0=x, scalar=s, in1=y, op0=o1, op1=o2), *w)

    ev = A(lambda e: e.activation(pr(3), pr(2), ACT.Exp), ev)
    ev = vtt(pr(4), pr(0), pr(3), ALU.mult, ev)
    ev_m = A(lambda e: e.activation(pr(5), pr(4), ACT.Exp), ev)
    ev = vtt(pr(6), pr(1), pr(3), ALU.mult, ev)
    MAGIC = 12582912.0
    ev = vts(pr(7), pr(6), 1.0 / (2 * np.pi), MAGIC, ALU.mult, ALU.add, ev)
    ev = vts(pr(7), pr(7), MAGIC, None, ALU.subtract, ALU.bypass, ev)
    c1 = 6.28125
    c2 = float(np.float32(np.float32((2 * np.pi - c1) * 2 ** 21).astype(np.int64) // 2048 * 2048 / 2 ** 21)) \
        if False else 0.0019350051879882812
    c3 = 2 * np.pi - c1 - c2
    ev = vstt(pr(8), pr(7), -c1, pr(6), ALU.mult, ALU.add, ev)
    ev = vstt(pr(8), pr(7), -c2, pr(8), ALU.mult, ALU.add, ev)
    ev = vstt(pr(8), pr(7), -c3, pr(8), ALU.mult, ALU.add, ev)
    ev = vts(pr(8), pr(8), PI_DOWN, -PI_DOWN, ALU.min, ALU.max, ev)
    ev_sn = A(lambda e: e.activation(pr(9), pr(8), ACT.Sin), ev)
    ev = A(lambda e: e.activation(pr(10), pr(8), ACT.Abs), ev)
    ev = vts(pr(10), pr(10), -1.0, float(np.pi / 2), ALU.mult, ALU.add, ev)
    ev = A(lambda e: e.activation(pr(10), pr(10), ACT.Sin), ev)
    ev_are = vtt(AP[:, 0, :, 0], pr(5), pr(10), ALU.mult, ev, ev_m)
    ev_aim = vtt(AP[:, 2, :, 0], pr(5), pr(9), ALU.mult, ev_sn)
    ar, ai = AP[:, 0, :, 0], AP[:, 2, :, 0]
    e1 = vtt(pr(13), pr(0), pr(0), ALU.mult)
    e2 = vtt(pr(14), pr(1), pr(1), ALU.mult)
    e1 = vtt(pr(13), pr(13), pr(14), ALU.add, e2)
    e1 = V(lambda e: e.reciprocal(pr(14), pr(13)), e1)
    e2 = vts(pr(15), ar, 1.0, None, ALU.subtract, ALU.bypass, ev_are)
    e3 = vtt(pr(16), pr(15), pr(0), ALU.mult, e2)
    e4 = vtt(pr(17), ai, pr(1), ALU.mult, ev_aim)
    e5 = vtt(pr(18), ai, pr(0), ALU.mult, e4)
    e6 = vtt(pr(21), pr(15), pr(1), ALU.mult, e5)
    e3 = vtt(pr(19), pr(16), pr(17), ALU.add, e6)
    e4 = vtt(pr(20), pr(18), pr(21), ALU.subtract, e6)
    e3 = vtt(pr(19), pr(19), pr(14), ALU.mult, e4)
    ev_k = vtt(pr(20), pr(20), pr(14), ALU.mult, e4)

    ev_ez = G(lambda e: e.memset(EX, 0.0))
    kre = pr(19).unsqueeze(2).to_broadcast([P, 32, 16])
    kim = pr(20).unsqueeze(2).to_broadcast([P, 32, 16])
    t0 = TMP[:, 0, :, :].rearrange("p a (j h) -> p (a j) h", h=16)
    t1 = TMP[:, 1, :, :].rearrange("p a (j h) -> p (a j) h", h=16)
    ev_e = ev_ez
    for i in range(2):
        e1 = G(lambda e, i=i: e.tensor_tensor(t0, BRI[:, i, :, :], kre, ALU.mult), ev_k, ld_b, ev_e)
        e2 = G(lambda e, i=i: e.tensor_tensor(t1, BRI[:, 1 - i, :, :], kim, ALU.mult), ev_k, ld_b, ev_e)
        for g in range(2):
            q = slice(64 * g, 64 * g + 64)
            ev_e = V(lambda e, i=i, g=g, q=q: e.tensor_tensor(EX[q, i, :, g, :], t0[q], t1[q],
                                                              ALU.subtract if i == 0 else ALU.add), e1, e2, ev_ez)
    for i in range(2):
        for g in range(2):
            if i == 0:
                ev_c = V(lambda e, g=g: e.tensor_scalar(CX[:, 0, :, g, :], CRI[:, 0, :, :], PAR[:, g:g + 1], None,
                                                        ALU.mult), ld_cc, ld_c)
            else:
                ev_c = V(lambda e, g=g: e.tensor_scalar(CX[:, 1, :, g, :], CRI[:, 1, :, :], PAR[:, g:g + 1], -1.0,
                                                        ALU.mult, ALU.mult), ld_cc, ld_c)
    u0 = TMP[:, 0, :, :].rearrange("p a n -> p (a n)")
    u1 = TMP[:, 1, :, :].rearrange("p a n -> p (a n)")
    ev = [ev_aim, ev_e]
    for n in (1, 2, 4, 8):
        re, im = AP[:, 0, :, 0:n], AP[:, 2, :, 0:n]
        mr = AP[:, 0, :, n - 1:n].to_broadcast([P, 32, n])
        mi = AP[:, 2, :, n - 1:n].to_broadcast([P, 32, n])
        v0 = u0[:, 0:32 * n].rearrange("p (j n) -> p j n", n=n)
        v1 = u1[:, 0:32 * n].rearrange("p (j n) -> p j n", n=n)
        e1 = vtt(v0, re, mr, ALU.mult, ev)
        e1 = vtt(v1, im, mi, ALU.mult, ev)
        e1 = vtt(AP[:, 0, :, n:2 * n], v0, v1, ALU.subtract, e1)
        e2 = vtt(v0, re, mi, ALU.mult, e1)
        e2 = vtt(v1, im, mr, ALU.mult, e1)
        ev = vtt(AP[:, 2, :, n:2 * n], v0, v1, ALU.add, e2)
    ev_ap = vts(AP[:, 1, :, :], AP[:, 2, :, :], -1.0, None, ALU.mult, ALU.bypass, ev)

    ev_gw = G(lambda e: e.affine_select(out=GW, in_=GW, compare_op=ALU.is_ge, fill=0.0, base=0,
                                        pattern=[[0, 8], [-1, P]], channel_multiplier=1), ld_gw)
    for g4 in range(2):
        b, t, bf = bank()

        def tr4(e, t=t, g4=g4):
            for g in range(4):
                ins = e.transpose(t[:, g * P:g * P + P], GW[:, 4 * g4 + g, :], IDENT)
            return ins

        ev = T(tr4, ev_gw, bf)
        ev_ws = V(lambda e, t=t, g4=g4: e.tensor_copy(WS[:, 4 * g4:4 * g4 + 4, :],
                                                      t[:, :].rearrange("p (g s) -> p g s", g=4)), ev)
        bank_done(b, ev_ws)
    b, t, bf = bank()

    def tr6(e, t=t):
        for c in range(6):
            ins = e.transpose(t[:, 34 * c:34 * c + 34], DWS[:, c * P:c * P + P], IDENT[0:34, 0:34])
        return ins

    ev_dw_t = T(tr6, ld_dw, bf)
    ev_dw = V(lambda e, t=t: e.tensor_copy(DWT[:, :, :], t[:, 0:204].rearrange("p (c k) -> p c k", c=6)), ev_dw_t)
    bank_done(b, ev_dw)
    BT = X[:, 0, :].rearrange("p (a q s) -> p a q s", a=2, q=8)
    UT = X[:, 1, :].rearrange("p (q t) -> p q t", q=8)

    def s5_turn(src, dst, *waits):
        for i in range(2):
            for q4 in range(2):
                b, t, bf = bank()

                def tr(e, t=t, i=i, q4=q4):
                    for q in range(4):
                        ins = e.transpose(t[:, q * P:q * P + P], src(i, 4 * q4 + q), IDENT)
                    return ins

                ev = T(tr, bf, *waits)
                ev = A(lambda e, t=t, i=i, q4=q4: e.activation(
                    dst[:, i, 4 * q4:4 * q4 + 4, :], t[:, :].rearrange("p (q s) -> p q s", q=4), ACT.Copy), ev)
                bank_done(b, ev)
        return ev

    ev_s5 = {}

    def s5_run():
        ev_bt = s5_turn(lambda i, q: EX[:, i, 4 * q:4 * q + 4, :, :].rearrange("p j g h -> p (j g h)"), BT, ev_e, ev_x_read)
        yield
        ev_ct = s5_turn(lambda i, q: CX[:, i, q, :, :].rearrange("p g s -> p (g s)"), CT, ev_c)
        yield
        for k in range(0, 8, 2):
            b, t, bf = bank()

            def tr(e, t=t, k=k):
                for m in range(2):
                    for half in range(2):
                        ins = e.transpose(t[:, m * L + half * P:m * L + half * P + P],
                                          XIN[:, half, (k + m) * P:(k + m) * P + P], IDENT)
                return ins

            ev = T(tr, bf, ev_s5["in"])
            ev_u = A(lambda e, t=t, k=k: e.activation(UT[:, k:k + 2, :], t[:, :].rearrange("p (m t) -> p m t", m=2),
                                                      ACT.Copy), ev)
            bank_done(b, ev_u)
        yield
        for half in range(2):
            ev_dx = G(lambda e, half=half: e.tensor_tensor(XIN[:, half, :], XIN[:, half, :], DB, ALU.mult),
                      ld_d, T.now(), ev_s5["in"])
        yield
        ev_free = [ev_dx, ev_ct, ev_bt, ev_e, ev_c, ev_ws, ev_gw]
        Sv = SS[:, :, :, :].rearrange("p a j (c i) -> p a j c i", i=16)
        for r in range(2):
            for jj in range(16):
                j = 16 * r + jj
                q, i = j // 4, j % 4
                b, t, bf = bank()
                rows = slice(32 * i, 32 * i + 32)

                def mm(e, t=t, q=q, rows=rows):
                    for ri in range(2):
                        ins = e.matmul(t[:, ri * L:ri * L + L], BT[rows, ri, q, :], UT[rows, q, :],
                                       start=True, stop=True)
                    return ins

                ev = T(mm, bf, ev_bt, ev_u)
                ev_bu = A(lambda e, t=t, jj=jj: e.activation(SS[:, :, jj, :], t[:, :].rearrange("p (a t) -> p a t", a=2),
                                                             ACT.Copy), ev, ev_free)
                bank_done(b, ev_bu)
                if jj % 4 == 3:
                    yield
            if r == 1:
                ev_s5["x_free"] = T.now()
            parts = [(V, 0, NV, 0), (G, NV, 16, NV * 16)]
            last = {}

            def step(k, dst, src, rr, ii, shape, j0, j1, tk):
                n = 1
                for d in shape[1:]:
                    n *= d
                tv = []
                for z in range(2):
                    f = TMP[:, z, :, tk:tk + n]
                    tv.append(f if len(shape) == 2 else f.rearrange("p a (j c) -> p a j c", c=shape[2]))
                Q = parts[k][0]
                w = [last.get(k), ev_bu, ev_ap]
                Q(lambda e: e.tensor_tensor(tv[0], src, rr, ALU.mult), w)
                e1 = Q(lambda e: e.tensor_tensor(tv[1], src[:, ::-1], ii, ALU.mult), w)
                e1 = Q(lambda e: e.tensor_tensor(dst, dst, tv[0], ALU.add), e1)
                last[k] = Q(lambda e: e.tensor_tensor(dst, dst, tv[1], ALU.add), e1)

            def coef(j0, j1, p, n):
                js = slice(16 * r + j0, 16 * r + j1)
                if n is None:
                    return (AP[:, 0, js, p].unsqueeze(1).to_broadcast([P, 2, j1 - j0]), AP[:, 1:3, js, p])
                rr = AP[:, 0, js, p].unsqueeze(1).unsqueeze(3).to_broadcast([P, 2, j1 - j0, n])
                ii = AP[:, 1:3, js, p].unsqueeze(3).to_broadcast([P, 2, j1 - j0, n])
                return rr, ii

            for i in range(1, 16):
                for k, (Q, j0, j1, tk) in enumerate(parts):
                    rr, ii = coef(j0, j1, 0, 16)
                    step(k, Sv[:, :, j0:j1, :, i], Sv[:, :, j0:j1, :, i - 1], rr, ii, (2, j1 - j0, 16), j0, j1, tk)
                yield
            for c in range(1, 16):
                for k, (Q, j0, j1, tk) in enumerate(parts):
                    rr, ii = coef(j0, j1, 15, None)
                    step(k, Sv[:, :, j0:j1, c, 15], Sv[:, :, j0:j1, c - 1, 15], rr, ii, (2, j1 - j0), j0, j1, tk)
                if c % 3 == 0:
                    yield
            for i in range(15):
                for k, (Q, j0, j1, tk) in enumerate(parts):
                    rr, ii = coef(j0, j1, i, 15)
                    step(k, Sv[:, :, j0:j1, 1:16, i], Sv[:, :, j0:j1, 0:15, 15], rr, ii, (2, j1 - j0, 15), j0, j1, tk)
                yield
            for half in range(2):
                b, t, bf = bank()

                def mm(e, t=t, half=half, r=r):
                    for jj in range(16):
                        j = 16 * r + jj
                        q, i = j // 4, j % 4
                        for ri in range(2):
                            ins = e.matmul(t[:, 32 * jj:32 * jj + 32], SS[:, ri, jj, half * P:half * P + P],
                                           CT[:, ri, q, 32 * i:32 * i + 32], start=(ri == 0), stop=(ri == 1))
                    return ins

                ev = T(mm, bf, [last[0], last[1]], ev_ct)
                ev_y = V(lambda e, t=t, half=half, r=r: e.tensor_tensor(
                    XIN[:, half, 512 * r:512 * r + 512], t[:, :], XIN[:, half, 512 * r:512 * r + 512], ALU.add), ev, ev_dx)
                bank_done(b, ev_y)
            ev_free = [ev_y, ev]
            yield
        ev_s5["y"] = A(lambda e: e.activation(XIN[:, :, :], XIN[:, :, :], ACT.Gelu_apprx_tanh), ev_y)

    for c in range(2):
        s, ev = product(w_in1, 16, 512 * (4 + c), XTH, XTL, ready if c == 0 else None)
        e1 = A(lambda e, s=s, c=c: e.activation(XIN[:, :, 512 * c:512 * c + 512], ACC[:, 2 * s:2 * s + 2, :], ACT.Copy), ev)
        acc_free[s] = [e1]
        ev_s5["in"] = e1
    s5_gen = s5_run()
    side.append(s5_gen)

    ssv = stat(4)
    for c in range(2):
        s, ev = product(w_in1, 16, 512 * (2 + c), XTH, XTL, None)
        e1 = A(lambda e, s=s, c=c: e.activation(VG[:, :, 512 * c:512 * c + 512], ACC[:, 2 * s:2 * s + 2, :],
                                                ACT.Gelu_apprx_tanh), ev, ev_dw_t)
        for half in range(2):
            e1 = A(lambda e, s=s, c=c, half=half: e.activation(
                ACC[:, 2 * s + half, :], VG[:, half, 512 * c:512 * c + 512], ACT.Square,
                accum_out=ssv[:, 2 * c + half:2 * c + half + 1]), e1)
        acc_free[s] = [e1]
    ssh, rsv = stat(2), stat(2)
    e1 = vtt(ssh, ssv[:, 0:2], ssv[:, 2:4], ALU.add, e1)
    e1 = finish_rms(ssh, rsv, 1024, e1)
    for half in range(2):
        ev_vn = vstt(VG[:, half, :], VG[:, half, :], rsv[:, half:half + 1], GMG, ALU.mult, ALU.mult, e1, ld_gmg)
    ya = []
    ug_free = ev_vn
    for c in range(2):
        s, ev = product(w_in1, 16, 512 * c, XTH, XTL, None)
        ev_ug = A(lambda e, s=s: e.activation(UG[:, :, :], ACC[:, 2 * s:2 * s + 2, :], ACT.Gelu_apprx_tanh), ev, ug_free)
        acc_free[s] = [ev_ug]
        for half in range(2):
            b, t, bf = bank()

            def mm(e, t=t, half=half, c=c):
                for g in range(4):
                    ins = e.matmul(t[:, g * P:g * P + P], WS[:, 4 * c + g, :],
                                   VG[:, half, (4 * c + g) * P:(4 * c + g) * P + P], start=True, stop=True)
                return ins

            ev = T(mm, bf, ev_vn, ev_ws)
            for g in range(4):
                ug = UG[:, half, g * P:g * P + P]
                e1 = vstt(ug, t[:, g * P:g * P + P], VEC[:, V_GB + 4 * c + g:V_GB + 4 * c + g + 1], ug,
                          ALU.add, ALU.mult, ev, ev_ug)
            bank_done(b, e1)
        ya += turn(lambda k, half: UG[:, half, k * P:k * P + P], 4, YAH[:, 4 * c:4 * c + 4, :], YAL[:, 4 * c:4 * c + 4, :], e1)
        ug_free = T.now()

    bg1 = a["b_gate"][0]

    def merged_free():
        while "x_free" not in ev_s5:
            side_step()
        return ev_s5["x_free"]

    class Late(list):
        pass

    xf = []
    res, ev_ya, _ = None, None, None
    xf.append(merged_free())
    res, ev_ya, _ = gate_branch(w_in1, GATE0, bg1[0], wbr[0], 8, None, lambda: ya, X, SGA[:, :, :], True, xf, False)
    side_drain(s5_gen)
    fence = everything()
    s5.close()

    QKV = sb("QKV", [P, 2, 3072], to=one)
    QT = sb("QT", [P, 8, L], to=one)
    KT = sb("KT", [P, 8, L], to=one)
    SG = sb("SG", [P, 2, D], to=one)
    BGL = sb("BGL", [P, 1024], to=one)
    ld_bgl = dma("bgl", BGL[:, :], row(a["s5_b_glu"][0], 1024), fence)
    for c in range(6):
        s, ev = product(w_in1, 16, 512 * (6 + c), XTH, XTL, None)
        e1 = A(lambda e, s=s, c=c: e.activation(QKV[:, :, 512 * c:512 * c + 512], ACC[:, 2 * s:2 * s + 2, :], ACT.Copy),
               ev, fence)
        acc_free[s] = [e1]
        if c == 0:
            gt = turn(lambda k, half: XIN[:, half, k * P:k * P + P], 8, YAH, YAL, ev_s5["y"], free=ev_ya)
    ev_qkv = e1

    ev_at = {}
    HW = 384
    pool2 = QKV[:, :, 0:D]
    ZSb, SPb = QKV[:, 0, 0:4 * HW], QKV[:, 1, 0:4 * HW]

    def attention():
        for src, dst in ((0, QT), (1024, KT)):
            for h in range(0, 8, 2):
                b, t, bf = bank()

                def tr(e, t=t, src=src, h=h):
                    for m in range(2):
                        for half in range(2):
                            ins = e.transpose(t[:, m * L + half * P:m * L + half * P + P],
                                              QKV[:, half, src + (h + m) * P:src + (h + m) * P + P], IDENT)
                    return ins

                ev = T(tr, bf, ev_qkv)
                ev_t = A(lambda e, t=t, dst=dst, h=h: e.activation(
                    dst[:, h:h + 2, :], t[:, :].rearrange("p (m t) -> p m t", m=2), ACT.Copy), ev, fence)
                bank_done(b, ev_t)
                yield
        free = [ev]
        for hg in range(2):
            for hh in range(4):
                h = 4 * hg + hh
                b, t, bf = bank()

                def mm(e, t=t, h=h):
                    e.matmul(t[:, 0:L], KT[:, h, 0:P], QT[:, h, :], start=True, stop=True)
                    return e.matmul(t[:, L:HW], KT[:, h, P:L], QT[:, h, P:L], start=True, stop=True)

                ev = T(mm, bf, ev_t)
                ev_z = A(lambda e, t=t, hh=hh: e.activation(ZSb[:, hh * HW:hh * HW + HW], t[:, 0:HW], ACT.Copy,
                                                            scale=128.0 ** -0.5), ev, free)
                bank_done(b, ev_z)
            yield
            e1 = A(lambda e: e.activation(SPb, ZSb, ACT.Abs), ev_z, free)
            e1 = A(lambda e: e.activation(SPb, SPb, ACT.Exp, scale=-1.0), e1)
            e1 = A(lambda e: e.activation(SPb, SPb, ACT.Ln, bias=1.0), e1)
            yield
            e1 = vstt(SPb, ZSb, 0.0, SPb, ALU.max, ALU.add, e1)
            yield
            for buf, fill in ((SPb, 0.0), (ZSb, -1e30)):
                for d in (0, 2):
                    v = buf.rearrange("p (h b c) -> p h b c", h=4, b=3)[:, :, d, :]
                    ev_m = G(lambda e, v=v, fill=fill: e.affine_select(
                        out=v, in_=v, compare_op=ALU.is_gt, fill=fill, base=0, pattern=[[0, 4], [1, P]],
                        channel_multiplier=-1), e1)
            yield
            for hh in range(4):
                sp = SPb[:, hh * HW:hh * HW + HW]
                b, t, bf = bank()

                def mm(e, t=t, sp=sp):
                    e.matmul(t[:, 0:P], TRI, sp[:, 0:P], start=True, stop=True)
                    e.matmul(t[:, P:L], TRI, sp[:, P:L], start=True, stop=False)
                    e.matmul(t[:, P:L], ONES, sp[:, L:HW], start=False, stop=True)
                    return e.matmul(t[:, L:HW], TRI, sp[:, L:HW], start=True, stop=True)

                ev = T(mm, bf, ev_m)
                zs = ZSb[:, hh * HW:hh * HW + HW]
                e2 = vtt(zs, zs, t[:, 0:HW], ALU.subtract, ev, ev_m)
                bank_done(b, e2)
            yield
            e2 = A(lambda e: e.activation(ZSb, ZSb, ACT.Exp), e2)
            yield
            for hp in range(2):
                b, t, bf = bank()

                def mm(e, t=t, hp=hp, hg=hg):
                    for m in range(2):
                        hh = 2 * hp + m
                        vc = D + (4 * hg + hh) * P
                        w = ZSb[:, hh * HW:hh * HW + HW]
                        e.matmul(t[:, m * L:m * L + P], QKV[:, 0, vc:vc + P], w[:, 0:P], start=True, stop=True)
                        e.matmul(t[:, m * L + P:m * L + L], QKV[:, 0, vc:vc + P], w[:, P:L], start=True, stop=False)
                        ins = e.matmul(t[:, m * L + P:m * L + L], QKV[:, 1, vc:vc + P], w[:, L:HW],
                                       start=False, stop=True)
                    return ins

                ev = T(mm, bf, e2)
                k = 4 * hg + 2 * hp
                tv = t[:, :].rearrange("p (m t) -> p m t", m=2)
                e3 = A(lambda e, k=k, tv=tv: e.activation(YAH[:, k:k + 2, :], tv, ACT.Copy), ev, ev_at["free"])
                e4 = vtt(YAL[:, k:k + 2, :], tv, YAH[:, k:k + 2, :], ALU.subtract, e3, ev_at["free"])
                bank_done(b, e4)
                ev_at.setdefault("y", []).append(e4)
            free = [ev, e2]
            yield

    at_gen = attention()
    for c in range(2):
        s, ev = product(a["s5_w_glu"][0], 8, 512 * c, YAH, YAL, gt if c == 0 else None)
        sg = SG[:, :, 512 * c:512 * c + 512]
        for half in range(2):
            e1 = vtt(sg[:, half, :], ACC[:, 2 * s + half, :], BGL[:, 512 * c:512 * c + 512], ALU.add, ev, ld_bgl, fence)
        acc_free[s] = [e1]
        e1 = A(lambda e, sg=sg: e.activation(sg, sg, ACT.Sigmoid), e1)
        xi = XIN[:, :, 512 * c:512 * c + 512]
        ev_yb = G(lambda e, xi=xi, sg=sg: e.tensor_tensor(xi, xi, sg, ALU.mult), e1, gt)
    ev_at["free"] = ev
    side.append(at_gen)

    def yc_ready():
        side_drain(at_gen)
        return ev_at["y"]

    res, ev_yc, _ = gate_branch(w_in1, GATE0 + 2 * D, bg1[2], wbr[2], 8, None, yc_ready, X, SG, False, res, True)
    yb = []

    def turn_yb():
        yb.extend(turn(lambda k, half: XIN[:, half, k * P:k * P + P], 8, YAH, YAL, ev_yb, free=ev_yc))
        yield

    yb_gen = turn_yb()
    side.append(yb_gen)

    def yb_ready():
        side_drain(yb_gen)
        return yb

    mready = []

    def turn_merged(c, ev, gates_done):
        mready.extend(turn(lambda k, half: X[:, half, 512 * c + k * P:512 * c + k * P + P], 4,
                           XTH[:, 4 * c:4 * c + 4, :], XTL[:, 4 * c:4 * c + 4, :], ev, free=gates_done))

    gate_branch(w_in1, GATE0 + D, bg1[1], wbr[1], 8, None, yb_ready, X, SG, False, res, True, last=turn_merged)
    ld_x = dma("x", X[:, :, :], x0, T.now(), everything())
    fence = everything()
    one.close()
    xr, ev_xt = residual_product(a["w_out"][0], X, mready, ld_x)

    def normed_to_xt(tag, gcol, ready_x, xt_free):
        with ExitStack() as sc:
            HS = sb("HS" + tag, [P, 2, D], F32, sc)
            return normed(X, HS, gcol, ready_x, free=xt_free, dfree=everything())

    ready = normed_to_xt("n2", V_N2, xr, ev_xt)
    xr, ev_xt = mlp("1", a["w_mlp_in"][0], a["w_mlp_out"][0], X, ready, xr)

    def final(gain, dst, sc, tag, xr):
        FG = sb("FG" + tag, [P, D], F32, sc)
        ld = dma("fg" + tag, FG[:, :], row(gain, D), everything())
        rs, ev = rms(lambda i: X[:, i, :], D, 2, xr)
        return [vstt(dst[:, h, :], X[:, h, :], rs[:, h:h + 1], FG[:, :], ALU.mult, ALU.mult, ev, ld) for h in range(2)]

    with ExitStack() as sc:
        xr = final(a["final_g"], X, sc, "1", xr)

    ready = normed_to_xt("m", V_MIX, xr, ev_xt)
    two = ExitStack()
    fence = everything()
    MG = sb("MG", [P, 2, D], to=two)
    ZA = MG[:, :, :].rearrange("p a n -> p (a n)")[:, 0:3072].rearrange("p (a n) -> p a n", a=2)
    ZB = MG[:, :, :].rearrange("p a n -> p (a n)")[:, 3072:4096].rearrange("p (a n) -> p a n", a=2)
    ZCb = sb("ZCb", [P, 2 * 2304], to=two)
    ZC = ZCb[:, :].rearrange("p (a n) -> p a n", a=2)
    SG2 = ZCb[:, 0:2 * D].rearrange("p (a n) -> p a n", a=2)
    UA = sb("UA", [P, 6, 30 + L], to=two)
    CA = sb("CA", [P, 6, L], to=two)
    VT = sb("VT", [P, 2, 768], to=two)
    PC = sb("PC", [P, 6, 2 + L], to=two)
    GBT = sb("GBT", [P, 6, L], to=two)
    PM = sb("PM", [P, 4, 2, L], to=two)
    PT = sb("PT", [P, 4, L], to=two)
    WG = sb("WG", [P, 4, P], to=two)
    BG = VT[:, :, :].rearrange("p a n -> p (a n)")
    ld_bg = dma("bglu2", BG, row(a["b_glu_2"][0], 1536), fence)
    ld_pm = dma("pm", PM[:, :, :, :], a["pmat"], fence)
    ld_wg = dma("wgrp", WG[:, :, :], a["w_pool_grp_2"][0].rearrange("g c d -> c g d"), fence)
    ev_pad = G(lambda e: e.memset(UA[:, :, 0:30], 0.0), fence)
    ev_pad = G(lambda e: e.memset(PC[:, :, 0:2], 0.0), fence)

    for c in range(3):
        s, ev = product(w_in2, 16, 512 * c, XTH, XTL, ready if c == 0 else None)
        for half in range(2):
            e1 = vtt(ZA[:, half, 512 * c:512 * c + 512], ACC[:, 2 * s + half, :], BG[:, 512 * c:512 * c + 512], ALU.add,
                     ev, ld_bg, fence)
        acc_free[s] = [e1]
    e1 = A(lambda e: e.activation(ZA[:, :, 768:1536], ZA[:, :, 768:1536], ACT.Sigmoid), e1)
    ev_ua = G(lambda e: e.tensor_tensor(ZA[:, :, 0:768], ZA[:, :, 0:768], ZA[:, :, 768:1536], ALU.mult), e1)

    def plain_turn(src, k0, n, dst, *waits):
        b, t, bf = bank()

        def tr(e):
            for m in range(n):
                for half in range(2):
                    ins = e.transpose(t[:, m * L + half * P:m * L + half * P + P], src(k0 + m, half), IDENT)
            return ins

        ev = T(tr, bf, *waits)
        ev = A(lambda e: e.activation(dst, t[:, 0:n * L].rearrange("p (m t) -> p m t", m=n), ACT.Copy), ev, fence)
        bank_done(b, ev)
        return ev

    ya2 = []
    va = {}

    def conv_a():
        for k in range(0, 6, 2):
            ev_t = plain_turn(lambda k, half: ZA[:, half, k * P:k * P + P], k, 2, UA[:, k:k + 2, 30:30 + L], ev_ua)
        va["za_read"] = T.now()
        yield
        prev = [None] * 6
        for k in range(31):
            for c in range(6):
                tap = DWT[:, c, k:k + 1]
                if k == 0:
                    prev[c] = vts(CA[:, c, :], UA[:, c, 0:L], tap, VEC[:, V_DB + c:V_DB + c + 1], ALU.mult, ALU.add,
                                  ev_t, ev_pad, fence)
                else:
                    prev[c] = vstt(CA[:, c, :], UA[:, c, k:k + L], tap, CA[:, c, :], ALU.mult, ALU.add, prev[c])
                if c == 2:
                    yield
            yield
        for half in range(2):
            for c0, n in ((0, 4), (4, 2)):
                b, t, bf = bank()

                def tr(e, t=t, c0=c0, n=n, half=half):
                    for m in range(n):
                        ins = e.transpose(t[:, m * P:m * P + P], CA[:, c0 + m, half * P:half * P + P], IDENT)
                    return ins

                ev = T(tr, bf, prev)
                e1 = A(lambda e, t=t, c0=c0, n=n, half=half: e.activation(
                    VT[:, half, c0 * P:(c0 + n) * P], t[:, 0:n * P], ACT.Copy), ev, acc_bg)
                bank_done(b, e1)
            yield
        e1 = [e1]
        for half in range(2):
            bs, mv, rs = stat(12), stat(2), stat(1)
            for q in range(2):
                e2 = V(lambda e, half=half, q=q, bs=bs: e.bn_stats(bs[:, 6 * q:6 * q + 6],
                                                                   VT[:, half, 384 * q:384 * q + 384]), e1)
            e2 = V(lambda e, bs=bs, mv=mv: e.bn_aggr(mv, bs.rearrange("p (q s) -> p q s", q=2)), e2)
            e2 = vts(rs, mv[:, 1:2], EPS, None, ALU.add, ALU.bypass, e2)
            e2 = A(lambda e, rs=rs: e.activation(rs, rs, ACT.Sqrt), e2)
            e2 = V(lambda e, rs=rs: e.reciprocal(rs, rs), e2)
            ev_ln = vts(VT[:, half, :], VT[:, half, :], mv[:, 0:1], rs, ALU.subtract, ALU.mult, e2)
            yield
        for k in range(0, 6, 2):
            b, t, bf = bank()

            def tr(e, t=t, k=k):
                for m in range(2):
                    for half in range(2):
                        ins = e.transpose(t[:, m * L + half * P:m * L + half * P + P],
                                          VT[:, half, (k + m) * P:(k + m) * P + P], IDENT)
                return ins

            ev = T(tr, bf, ev_ln)
            for m in range(2):
                e1 = vts(CA[:, k + m, :], t[:, m * L:m * L + L], VEC[:, V_LG + k + m:V_LG + k + m + 1],
                         VEC[:, V_LB + k + m:V_LB + k + m + 1], ALU.mult, ALU.add, ev)
            bank_done(b, e1)
            e1 = A(lambda e, k=k: e.activation(UA[:, k:k + 2, 0:L], CA[:, k:k + 2, :], ACT.Sigmoid), e1)
            va["v"] = vtt(CA[:, k:k + 2, :], CA[:, k:k + 2, :], UA[:, k:k + 2, 0:L], ALU.mult, e1)
            yield

    def place(src, n, free, *waits):
        evs = []
        for k in range(0, n, 2):
            e1 = A(lambda e, k=k: e.activation(YAH[:, k:k + 2, :], src[:, k:k + 2, :], ACT.Copy), free, *waits)
            evs.append(vtt(YAL[:, k:k + 2, :], src[:, k:k + 2, :], YAH[:, k:k + 2, :], ALU.subtract, e1, free))
        return evs

    acc_bg = e1
    va_gen = conv_a()
    side.append(va_gen)

    for c in range(5):
        n = 512 if c < 4 else 256
        s, ev = product(w_in2, 16, ZC0 + 512 * c, XTH, XTL, None, n=n)
        e1 = A(lambda e, s=s, c=c, n=n: e.activation(ZC[:, :, 512 * c:512 * c + n], ACC[:, 2 * s:2 * s + 2, 0:n], ACT.Copy),
               ev, fence)
        acc_free[s] = [e1]
    ev_zc = e1
    ev_p = G(lambda e: e.tensor_tensor(ZC[:, :, 768:1536], ZC[:, :, 768:1536], ZC[:, :, 1536:2304], ALU.mult), ev_zc)
    vc = {}

    def conv_c():
        for k in range(0, 6, 2):
            ev_g = plain_turn(lambda k, half: ZC[:, half, k * P:k * P + P], k, 2, GBT[:, k:k + 2, :], ev_zc)
            yield
        for k in range(0, 6, 2):
            ev_t = plain_turn(lambda k, half: ZC[:, half, 768 + k * P:768 + k * P + P], k, 2, PC[:, k:k + 2, 2:2 + L], ev_p)
            yield
        vc["read"] = [T.now(), ev_p]
        o = WGC
        for c in range(6):
            e1 = vts(o[:, c, :], PC[:, c, 0:L], DWT[:, c, 31:32], None, ALU.mult, ALU.bypass, ev_t, ev_pad)
            e1 = vstt(o[:, c, :], PC[:, c, 1:1 + L], DWT[:, c, 32:33], o[:, c, :], ALU.mult, ALU.add, e1)
            e1 = vstt(o[:, c, :], PC[:, c, 2:2 + L], DWT[:, c, 33:34], o[:, c, :], ALU.mult, ALU.add, e1)
            yield
        vc["v"] = G(lambda e: e.tensor_tensor(GBT[:, :, :], GBT[:, :, :], o[:, :, :], ALU.mult), e1, ev_g)

    WGC = sb("WGC", [P, 6, L], to=two)
    s, ev = product(w_in2, 16, 1536, XTH, XTL, None)
    e1 = A(lambda e, s=s: e.activation(ZB, ACC[:, 2 * s:2 * s + 2, :], ACT.Copy), ev, fence)
    acc_free[s] = [e1]
    vc_gen = conv_c()
    side.appendleft(vc_gen)
    side_drain(vc_gen)

    yb2 = []
    for g in range(0, 4, 2):
        b, t, bf = bank()

        def mm(e, t=t, g=g):
            for m in range(2):
                for half in range(2):
                    ins = e.matmul(t[:, m * L:m * L + L], ZB[:, half, (g + m) * P:(g + m) * P + P], PM[:, g + m, half, :],
                                   start=(half == 0), stop=(half == 1))
            return ins

        ev = T(mm, bf, e1, ld_pm)
        e2 = A(lambda e, t=t, g=g: e.activation(PT[:, g:g + 2, :], t[:, :].rearrange("p (m t) -> p m t", m=2), ACT.Copy),
               ev, fence)
        bank_done(b, e2)
    zb_read = T.now()
    for g in range(0, 4, 2):
        b, t, bf = bank()

        def mm(e, t=t, g=g):
            for m in range(2):
                ins = e.matmul(t[:, m * L:m * L + L], WG[:, g + m, :], PT[:, g + m, :], start=True, stop=True)
            return ins

        ev = T(mm, bf, e2, ld_wg)
        for m in range(2):
            sc_ = VEC[:, V_PS + g + m:V_PS + g + m + 1]
            e3 = A(lambda e, t=t, g=g, m=m, sc_=sc_: e.activation(YAH[:, g + m, :], t[:, m * L:m * L + L], ACT.Copy,
                                                                  scale=sc_), ev, fence)
        for m in range(2):
            sc_ = VEC[:, V_PS + g + m:V_PS + g + m + 1]
            e4 = vstt(YAL[:, g + m, :], t[:, m * L:m * L + L], sc_, YAH[:, g + m, :], ALU.mult, ALU.subtract, e3, fence)
        bank_done(b, e4)
        yb2.append(e4)

    bg2 = a["b_gate_2"][0].rearrange("(n d) -> n d", n=3)
    while "za_read" not in va:
        side_step()
    mfree = [va["za_read"], zb_read, vc["read"]]
    SGB = SG2[:, :, 0:512]
    res, ev_b, _ = gate_branch(wg2, D, bg2[1], a["w_b_out_2"][0], 4, None, lambda: yb2, MG, SGB, True, mfree, False)
    yc2 = place(GBT, 6, ev_b, vc["v"])
    res, ev_c2, _ = gate_branch(wg2, 2 * D, bg2[2], a["w_c_out_2"][0], 6, None, lambda: yc2, MG, SGB, False, res, False)

    def ya2_ready():
        side_drain(va_gen)
        return place(CA, 6, ev_c2, va["v"])

    mready2 = []

    def turn_merged2(c, ev, gates_done):
        mready2.extend(turn(lambda k, half: MG[:, half, 512 * c + k * P:512 * c + k * P + P], 4,
                            XTH[:, 4 * c:4 * c + 4, :], XTL[:, 4 * c:4 * c + 4, :], ev, free=gates_done))

    gate_branch(wg2, 0, bg2[0], a["w_a_out_2"][0], 6, None, ya2_ready, MG, SG2, False, res, True, last=turn_merged2)
    two.close()
    xr, ev_xt = residual_product(a["w_o_2"][0], X, mready2, xr)
    ready = normed_to_xt("n4", V_MLP, xr, ev_xt)
    xr, ev_xt = mlp("2", a["w_up_2"][0], a["w_down_2"][0], X, ready, xr)
    with ExitStack() as sc:
        evs = final(a["g_final_2"], X, sc, "2", xr)
    st = dma("out", out[0].rearrange("(h p) n -> p h n", p=P), X[:, :, :], evs)
    assert at["block"] == len(plan) and at["unit"] == len(units)
    S.items.append((lambda e: e.wait_ge(*st), [], None))

    block = ctx.enter_context(nc.Block())

    @block.sync
    def _(eng):
        S.play(eng)

    @block.tensor
    def _(eng):
        T.play(eng)

    @block.scalar
    def _(eng):
        A.play(eng)

    @block.vector
    def _(eng):
        V.play(eng)

    @block.gpsimd
    def _(eng):
        G.play(eng)

    ctx.close()


_INS = ["x", "norm1_g", "w_in", "b_gate", "gm_norm_g", "gm_w_s", "gm_b_s", "s5_lambda_re", "s5_lambda_im", "s5_log_dt",
        "s5_b_re", "s5_b_im", "s5_c_re", "s5_c_im", "s5_d", "s5_w_glu", "s5_b_glu", "w_branch", "w_out", "norm2_g",
        "w_mlp_in", "w_mlp_out", "final_g", "g_mix_2", "w_in_2", "w_gate_2", "b_gate_2", "b_glu_2", "w_dw_a_2",
        "b_dw_a_2", "ln_g_a_2", "ln_b_a_2", "w_a_out_2", "w_pool_grp_2", "pool_scale_2", "w_b_out_2", "w_dw_c_2",
        "w_c_out_2", "w_o_2", "g_mlp_2", "w_up_2", "w_down_2", "g_final_2"]


def kernel(**inputs):
    import numpy as _np
    import concourse.bacc as _bacc
    from concourse import mybir as _mybir
    from concourse.bass_utils import run_bass_kernel_spmd as _run

    nc = _bacc.Bacc("TRN2", target_bir_lowering=False, num_devices=1)
    arrays, aps = {}, {}
    cst, pmat = consts()
    for name in _INS + ["cst", "pmat"]:
        v = {"cst": cst, "pmat": pmat}.get(name)
        v = _np.ascontiguousarray(inputs[name] if v is None else v)
        arrays[f"in_{name}_dram"] = v
        aps[name] = nc.dram_tensor(f"in_{name}_dram", v.shape, _mybir.dt.from_np(v.dtype), kind="ExternalInput").ap()
    out = nc.dram_tensor("out_0_dram", (1, L, D), F32, kind="ExternalOutput").ap()
    build(nc, aps, out)
    r = _run(nc, [arrays], core_ids=[0])
    return r.results[0]["out_0_dram"]
```

```python
from collections import deque
from contextlib import ExitStack

import numpy as np
import concourse.bass as bass
from concourse import mybir

F32 = mybir.dt.float32
F32R = mybir.dt.float32r
I32 = mybir.dt.int32
ALU = mybir.AluOpType
ACT = mybir.ActivationFunctionType

P = 128
D = 2048
L = 256
EPS = 1e-6
NRAW = 4
NSPL = 4
POOL_W = (2, 4, 8, 16)
PI_DOWN = 3.1415925
NV = 11
PACE = 1


class Queue:

    def __init__(self, sem):
        self.sem, self.n, self.items = sem, 0, []

    def __call__(self, fn, *waits, inc=True):
        self.items.append((fn, list(flat(waits)), (self.sem, 1) if inc else None))
        self.n += inc
        return (self.sem, self.n)

    def now(self):
        return (self.sem, self.n)

    def play(self, eng):
        seen = {}
        for fn, waits, inc in self.items:
            for sem, val in waits:
                if seen.get(sem.name, 0) < val:
                    eng.wait_ge(sem, val)
                    seen[sem.name] = val
            ins = fn(eng)
            if inc:
                ins.then_inc(*inc)


def flat(waits):
    for w in waits:
        if isinstance(w, list):
            yield from flat(w)
        elif w is not None and w[1] > 0:
            yield w


def consts():
    c = np.zeros((P, 3 * P + 2), np.float32)
    i = np.arange(P)
    c[:, 0:P] = np.eye(P)
    c[:, P:2 * P] = i[:, None] >= i[None, :]
    c[:, 2 * P:3 * P] = 1.0
    c[i, 3 * P + (i // 16) % 2] = 1.0
    s, t = np.arange(L)[:, None], np.arange(L)[None, :]
    m = np.zeros((P, 4, 2, L), np.float32)
    for g, w in enumerate(POOL_W):
        band = ((s <= t) & (s > t - w)) / np.minimum(t + 1, w).astype(np.float64) - (s == t)
        m[:, g] = band.astype(np.float32).reshape(2, P, L).transpose(1, 0, 2)
    return c, m


def build(nc, a, out):
    ctx = ExitStack()

    def sem(name):
        return ctx.enter_context(nc.semaphore(name))

    T, A, V, G, S = (Queue(sem("q_" + n)) for n in ("tensor", "scalar", "vector", "pool", "sync"))

    def sb(name, shape, dt=F32, to=ctx):
        return to.enter_context(nc.sbuf_tensor(name, shape, dt))

    dma_count = {}

    def dma(name, dst, src, *waits):
        if name not in dma_count:
            dma_count[name] = [sem("d_" + name), 0]
        rec = dma_count[name]
        rec[1] += 16
        s = rec[0]
        S.items.append((lambda e: e.dma_start(dst, src).then_inc(s, 16), list(flat(waits)), None))
        return (s, rec[1])

    def row(ap, n):
        return ap.rearrange("(a n) -> a n", a=1).to_broadcast([P, n])

    def everything():
        return [q.now() for q in (T, A, V, G)]

    X = sb("X", [P, 2, D])
    XTH, XTL = sb("XTH", [P, 16, L], F32R), sb("XTL", [P, 16, L], F32R)
    RAW = [sb(f"RAW{i}", [P, 2, 512]) for i in range(NRAW)]
    WH = [sb(f"WH{i}", [P, 2, 512], F32R) for i in range(NSPL)]
    WL = [sb(f"WL{i}", [P, 2, 512], F32R) for i in range(NSPL)]
    YAH, YAL = sb("YAH", [P, 8, L], F32R), sb("YAL", [P, 8, L], F32R)
    CST = sb("CST", [P, 3 * P + 2])
    VEC = sb("VEC", [P, 110])
    DWT = sb("DWT", [P, 6, 34])
    ST = sb("ST", [P, 160])
    GB = [sb(f"GB{i}", [P, 512]) for i in range(2)]
    JK = sb("JK", [P, 512])
    IDENT, TRI, ONES, PAR = CST[:, 0:P], CST[:, P:2 * P], CST[:, 2 * P:3 * P], CST[:, 3 * P:3 * P + 2]
    ACC = ctx.enter_context(nc.psum_tensor("ACC", [P, 4, 512], F32))
    TB = [ctx.enter_context(nc.psum_tensor(f"TB{i}", [P, 512], F32)) for i in range(4)]

    st_used = [0]

    def stat(n):
        st_used[0] += n
        return ST[:, st_used[0] - n:st_used[0]]

    bank_free = [[] for _ in TB]
    bank_next = [0]

    def bank():
        i = bank_next[0] % 4
        bank_next[0] += 1
        assert bank_free[i] is not None
        free, bank_free[i] = bank_free[i], None
        return i, TB[i], free

    def bank_done(i, *evs):
        bank_free[i] = list(evs)

    side = deque()

    def side_step():
        while side:
            try:
                next(side[0])
                return
            except StopIteration:
                side.popleft()

    def side_drain(gen):
        while gen in side:
            side_step()

    def later(gen, first=False):
        side.appendleft(gen) if first else side.append(gen)
        return gen

    w_in1, w_in2 = a["w_in"][0], a["w_in_2"][0]
    wg2 = a["w_gate_2"][0]
    wbr = [a["w_branch"][0, n] for n in range(3)]
    plan = []

    def planned(w, nk, c0, n=512):
        plan.append((w, nk, c0, n))

    def plan_branch(gate, g0, w, nk, wide):
        if wide:
            for c in range(4):
                planned(gate, 16, g0 + 512 * c)
            for c in range(4):
                planned(w, nk, 512 * c)
        else:
            for c in range(4):
                planned(gate, 16, g0 + 512 * c)
                planned(w, nk, 512 * c)

    def plan_mlp(wi, wo):
        for j in range(9):
            if j < 8:
                for b in range(2):
                    planned(wi, 16, 1024 * j + 512 * b)
            if j > 0:
                for c in range(4):
                    planned(wo[1024 * (j - 1):1024 * j, :], 8, 512 * c)

    GATE0 = 6144
    for c in (4, 5, 2, 3, 0, 1):
        planned(w_in1, 16, 512 * c)
    plan_branch(w_in1, GATE0, wbr[0], 8, True)
    for c in range(6, 12):
        planned(w_in1, 16, 512 * c)
    for c in range(2):
        planned(a["s5_w_glu"][0], 8, 512 * c)
    plan_branch(w_in1, GATE0 + 2 * D, wbr[2], 8, True)
    plan_branch(w_in1, GATE0 + D, wbr[1], 8, True)
    for c in range(4):
        planned(a["w_out"][0], 16, 512 * c)
    plan_mlp(a["w_mlp_in"][0], a["w_mlp_out"][0])
    ZC0 = 2048
    for c in range(3):
        planned(w_in2, 16, 512 * c)
    for c in range(5):
        planned(w_in2, 16, ZC0 + 512 * c, 512 if c < 4 else 256)
    planned(w_in2, 16, 1536)
    plan_branch(wg2, D, a["w_b_out_2"][0], 4, False)
    plan_branch(wg2, 2 * D, a["w_c_out_2"][0], 6, False)
    plan_branch(wg2, 0, a["w_a_out_2"][0], 6, True)
    for c in range(4):
        planned(a["w_o_2"][0], 16, 512 * c)
    plan_mlp(a["w_up_2"][0], a["w_down_2"][0])

    units = [(w, 2 * i, c0, n) for w, nk, c0, n in plan for i in range(nk // 2)]
    landed, split, used = {}, {}, {}
    sent, cut = [0], [0]

    def send(upto_u):
        while sent[0] < min(upto_u, len(units)):
            u = sent[0]
            w, k, c0, n = units[u]
            src = w[k * P:(k + 2) * P, c0:c0 + n].rearrange("(t p) n -> p t n", p=P)
            landed[u] = dma(f"raw{u % NRAW}", RAW[u % NRAW][:, :, 0:n], src, split.get(u - NRAW))
            sent[0] += 1

    def cut_units(upto_u):
        while cut[0] < min(upto_u, len(units)):
            u = cut[0]
            send(u + 1)
            n = units[u][3]
            r, h, l = (b[:, :, 0:n] for b in (RAW[u % NRAW], WH[u % NSPL], WL[u % NSPL]))
            ev = A(lambda e, h=h, r=r: e.activation(h, r, ACT.Copy), landed[u], used.get(u - NSPL))
            split[u] = V(lambda e, l=l, r=r, h=h: e.tensor_tensor(l, r, h, ALU.subtract),
                         ev, used.get(u - NSPL))
            cut[0] += 1
            send(u + 1 + NRAW)

    acc_free = [[], []]
    at = {"unit": 0, "block": 0}

    pace = [1]

    def product(w, nk, c0, xh, xl, ready, n=512):
        s = at["block"] % 2
        pw, pk, pc, pn = plan[at["block"]]
        assert (pk, pc, pn) == (nk, c0, n) and pw.tensor.name == w.tensor.name
        at["block"] += 1
        ev = None
        for i in range(nk // 2):
            u = at["unit"]
            at["unit"] += 1
            cut_units(u + NSPL - 1)
            h, l = WH[u % NSPL], WL[u % NSPL]

            def mm(e, i=i, h=h, l=l):
                for half in range(2):
                    for t in range(2):
                        k = 2 * i + t
                        xs = slice(half * P, half * P + P)
                        for m, (p, q) in enumerate(((xh, h), (xh, l), (xl, h))):
                            ins = e.matmul(ACC[:, 2 * s + half, 0:n], p[:, k, xs], q[:, t, 0:n],
                                           start=(k == 0 and m == 0), stop=(k == nk - 1 and m == 2))
                return ins

            while ready is not None and len(ready) <= i:
                assert side
                side_step()
            ev = used[u] = T(mm, split[u], ready[i] if ready else None, acc_free[s] if i == 0 else None)
            for _ in range(pace[0]):
                side_step()
        return s, ev

    def turning(evs, src, kts, yh, yl, *waits, free=None, gain=None, wait=0):
        for _ in range(wait):
            yield
        for k in range(0, kts, 2):
            b, t, bf = bank()

            def tr(e, k=k, t=t):
                for m in range(2):
                    for half in range(2):
                        ins = e.transpose(t[:, m * L + half * P:m * L + half * P + P], src(k + m, half), IDENT)
                return ins

            ev = T(tr, bf, *waits)
            tv = t[:, :].rearrange("p (m t) -> p m t", m=2)
            if gain is None:
                e1 = A(lambda e, k=k, tv=tv: e.activation(yh[:, k:k + 2, :], tv, ACT.Copy), ev, free)
                e2 = V(lambda e, k=k, tv=tv: e.tensor_tensor(yl[:, k:k + 2, :], tv, yh[:, k:k + 2, :], ALU.subtract),
                       e1, free)
            else:
                for m in range(2):
                    e1 = A(lambda e, k=k + m, tv=tv[:, m, :]: e.activation(yh[:, k, :], tv, ACT.Copy, scale=gain(k)),
                           ev, free)
                for m in range(2):
                    e2 = V(lambda e, k=k + m, tv=tv[:, m, :]: e.scalar_tensor_tensor(
                        out=yl[:, k, :], in0=tv, scalar=gain(k), in1=yh[:, k, :], op0=ALU.mult, op1=ALU.subtract),
                        e1, free)
            bank_done(b, e2)
            evs.append(e2)
            yield

    def turn(src, kts, yh, yl, *waits, **kw):
        evs = []
        for _ in turning(evs, src, kts, yh, yl, *waits, **kw):
            pass
        return evs

    def x_turning(evs, x, gain, blocks, free):
        for c in range(4):
            yield from turning(evs, lambda k, half, c=c: x[:, half, 512 * c + k * P:512 * c + k * P + P], 4,
                               XTH[:, 4 * c:4 * c + 4, :], XTL[:, 4 * c:4 * c + 4, :], blocks[c], free=free,
                               gain=lambda k, c=c: gain[:, 4 * c + k:4 * c + k + 1])

    def begin(gen, steps):
        for _ in range(steps):
            next(gen)
        return later(gen, first=True)

    jk = [None]

    def squares(x, ss, c, ev):
        for half in range(2):
            jk[0] = A(lambda e, half=half: e.activation(JK[:, :], x[:, half, 512 * c:512 * c + 512], ACT.Square,
                                                        accum_out=ss[:, half, c:c + 1]), ev, jk[0])
        return jk[0]

    def sum_stat(n):
        return stat(2 * n).rearrange("p (h c) -> p h c", h=2)

    def root(ss, width, ev):
        tot, rs = stat(2), stat(2)
        ev = V(lambda e: e.tensor_reduce(tot, ss, mybir.AxisListType.X, ALU.add), ev)
        return rs, finish_rms(tot, rs, width, ev)

    def finish_rms(ss, rs, width, *waits):
        ev = V(lambda e: e.tensor_scalar(ss, ss, 1.0 / width, EPS, ALU.mult, ALU.add), *waits)
        ev = A(lambda e: e.activation(ss, ss, ACT.Sqrt), ev)
        return V(lambda e: e.reciprocal(rs, ss), ev)

    gb_used = [0]
    gb_free = [None, None]

    def gate_branch(gate, g0, bias, rs, w, nk, yready, merged, SG, sg_ready, first, mfree, wide, last=None, add=None):
        res = []
        sg_free = {}
        at_gates = {}
        add = add or G

        def do_gate(c):
            i = gb_used[0] % 2
            gb_used[0] += 1
            eb = dma(f"gb{i}", GB[i][:, :], row(bias[512 * c:512 * c + 512], 512), gb_free[i])
            s, ev = product(gate, 16, g0 + 512 * c, XTH, XTL, None)
            if c == 0:
                sg_free["start"] = sg_ready()
            sg = SG[:, :, 512 * c:512 * c + 512] if wide else SG
            for half in range(2):
                e1 = V(lambda e, half=half: e.scalar_tensor_tensor(
                    out=sg[:, half, :], in0=ACC[:, 2 * s + half, :], scalar=rs[0][:, half:half + 1], in1=GB[i][:, :],
                    op0=ALU.mult, op1=ALU.add), ev, eb, rs[1], sg_free["start"], sg_free.get(c if wide else 0))
            acc_free[s] = [e1]
            gb_free[i] = e1
            at_gates["done"] = ev
            return A(lambda e: e.activation(sg, sg, ACT.Sigmoid), e1)

        def do_branch(c, es):
            s, ev = product(w, nk, 512 * c, YAH, YAL, yready() if c == 0 else None)
            if c == 0 and callable(mfree):
                mf.append(mfree())
            sg = SG[:, :, 512 * c:512 * c + 512] if wide else SG
            m = merged[:, :, 512 * c:512 * c + 512]
            av = ACC[:, 2 * s:2 * s + 2, :]
            if first:
                e1 = V(lambda e: e.tensor_tensor(m, av, sg, ALU.mult), ev, es, mf)
                acc_free[s] = [e1]
            else:
                e0 = V(lambda e: e.tensor_tensor(sg, av, sg, ALU.mult), ev, es)
                acc_free[s] = [e0]
                e1 = add(lambda e: e.tensor_tensor(m, m, sg, ALU.add), e0, mf)
            sg_free[c if wide else 0] = e1
            res.append(e1)
            if last:
                last(c, e1, at_gates["done"])
            return ev

        mf = [] if callable(mfree) else [mfree]
        if wide:
            es = [do_gate(c) for c in range(4)]
            for c in range(4):
                ev = do_branch(c, es[c])
        else:
            for c in range(4):
                e = do_gate(c)
                ev = do_branch(c, e)
        return res, ev

    def residual_product(w, x, ready, xready, ss):
        evs = []
        for c in range(4):
            s, ev = product(w, 16, 512 * c, XTH, XTL, ready if c == 0 else None)
            xv = x[:, :, 512 * c:512 * c + 512]
            e1 = V(lambda e, s=s, xv=xv: e.tensor_tensor(xv, xv, ACC[:, 2 * s:2 * s + 2, :], ALU.add),
                   ev, xready() if callable(xready) else xready)
            acc_free[s] = [e1]
            evs.append(e1)
            esq = squares(x, ss, c, e1)
        return evs, ev, esq

    def mlp(tag, wi, wo, x, ready, rs, xready, done):
        with ExitStack() as sc:
            fence = everything()
            YBH, YBL = sb("YBH" + tag, [P, 8, L], F32R, sc), sb("YBL" + tag, [P, 8, L], F32R, sc)
            HB = [sb(f"HB{i}" + tag, [P, 2, 512], F32, sc) for i in range(2)]
            hb_free = [fence, fence]
            Y = [(YAH, YAL), (YBH, YBL)]
            y_free = [fence, fence]
            hready, gens = {}, {}

            def hidden(j, b, e2):
                yh, yl = Y[j % 2]
                yield from turning(hready[j], lambda k, half: HB[b][:, half, k * P:k * P + P], 4,
                                   yh[:, 4 * b:4 * b + 4, :], yl[:, 4 * b:4 * b + 4, :], e2, free=y_free[j % 2], wait=1)
                hb_free[b] = T.now()

            for j in range(9):
                if j < 8:
                    hready[j] = []
                    for b in range(2):
                        s, ev = product(wi, 16, 1024 * j + 512 * b, XTH, XTL, ready if j + b == 0 else None)
                        if (j - 1, b) in gens:
                            side_drain(gens[j - 1, b])
                        hb = HB[b]
                        for half in range(2):
                            e1 = A(lambda e, s=s, hb=hb, half=half: e.activation(
                                hb[:, half, :], ACC[:, 2 * s + half, :], ACT.Relu, scale=rs[0][:, half:half + 1]),
                                ev, hb_free[b], rs[1])
                        acc_free[s] = [e1]
                        e2 = A(lambda e, hb=hb: e.activation(hb[:, :, :], hb[:, :, :], ACT.Square), e1)
                        gens[j, b] = later(hidden(j, b, e2))
                    xlast = ev
                if j > 0:
                    wj = wo[1024 * (j - 1):1024 * j, :]
                    yh, yl = Y[(j - 1) % 2]
                    for c in range(4):
                        s, ev = product(wj, 8, 512 * c, yh, yl, hready[j - 1] if c == 0 else None)
                        xv = x[:, :, 512 * c:512 * c + 512]
                        e1 = V(lambda e, s=s, xv=xv: e.tensor_tensor(xv, xv, ACC[:, 2 * s:2 * s + 2, :], ALU.add),
                               ev, xready)
                        acc_free[s] = [e1]
                        if j == 8:
                            done(c, e1, xlast)
                    y_free[(j - 1) % 2] = ev

    x0 = a["x"][0].rearrange("(h p) n -> p h n", p=P)
    ld_xc = []
    for c in range(4):
        cs = slice(512 * c, 512 * c + 512)
        ld_xc.append(dma(f"x{c}", X[:, :, cs], x0[:, :, cs]))
        if c == 0:
            ld_c = dma("cst", CST[:, :], a["cst"])

    one = ExitStack()
    XIN = sb("XIN", [P, 2, 1024], to=one)
    s5 = ExitStack()
    CT = sb("CT", [P, 2, 8, P], to=s5)
    SS = sb("SS", [P, 2, 16, L], to=s5)
    AP = sb("AP", [P, 3, 32, 16], to=s5)
    TMP = sb("TMP", [P, 2, 2, 256], to=s5)
    PR = sb("PR", [P, 24, 32], to=s5)
    GR = sb("GR", [P, 4096], to=s5)
    VG = GR[:, 0:2048].rearrange("p (a n) -> p a n", a=2)
    WS = GR[:, 2048:3072].rearrange("p (g s) -> p g s", g=8)
    UG1 = sb("UG1", [P, 2, 512], to=s5)
    UG = [GR[:, 3072:4096].rearrange("p (a n) -> p a n", a=2), UG1[:, :, :]]
    SGA = GR[:, :].rearrange("p (a n) -> p a n", a=2)
    VST = sb("VST", [110, P], to=s5)
    S5ST = sb("S5ST", [32, 3, P], to=s5)
    LDT = sb("LDT", [32, 2], to=s5)
    pool = SS[:, :, :, :].rearrange("p a j t -> p (a j t)")
    BRI = pool[:, 0:1024].rearrange("p (a j h) -> p a j h", a=2, j=32)
    EX = pool[:, 1024:3072].rearrange("p (a j g h) -> p a j g h", a=2, j=32, g=2)
    CRI = pool[:, 3072:4096].rearrange("p (a q s) -> p a q s", a=2, q=8)
    CX = pool[:, 4096:6144].rearrange("p (a q g s) -> p a q g s", a=2, q=8, g=2)
    GW = pool[:, 6144:7168].rearrange("p (g s) -> p g s", g=8)
    DB = pool[:, 7168:8192]
    DWS = GR[0:34, 0:768]
    GMG = GR[:, 3072:4096]

    r0 = 0
    for name, n in (("norm1_g", 16), ("norm2_g", 16), ("g_mix_2", 16), ("g_mlp_2", 16), ("gm_b_s", 8),
                    ("ln_g_a_2", 6), ("ln_b_a_2", 6), ("b_dw_a_2", 6), ("pool_scale_2", 4), ("final_g", 16)):
        v = a[name] if name == "final_g" else a[name][0]
        src = v if name == "gm_b_s" else v.rearrange("(r p) -> r p", p=P)
        ld_v = dma("vec", VST[r0:r0 + n, :], src)
        r0 += n
    V_N1, V_N2, V_MIX, V_MLP, V_GB, V_LG, V_LB, V_DB, V_PS, V_FIN = 0, 16, 32, 48, 64, 72, 78, 84, 90, 94
    dma("s5p", S5ST[:, 0, :], a["s5_lambda_re"][0].rearrange("(j g) p -> j (g p)", g=2))
    dma("s5p", S5ST[:, 1, :], a["s5_lambda_im"][0].rearrange("(j g) p -> j (g p)", g=2))
    ld_s = dma("s5p", LDT[:, :], a["s5_log_dt"][0].rearrange("(j g) -> j g", g=2))
    send(NRAW)
    dma("dw", DWS[0:31, :], a["w_dw_a_2"][0])
    ld_dw = dma("dw", DWS[31:34, :], a["w_dw_c_2"][0])
    for i, n in enumerate(("s5_b_re", "s5_b_im")):
        ld_b = dma("s5b", BRI[:, i, :, :], a[n][0].rearrange("(j g) p h -> (g p) j h", g=2))
    for i, n in enumerate(("s5_c_re", "s5_c_im")):
        ld_cc = dma("s5c", CRI[:, i, :, :], a[n][0].rearrange("(q g) h p -> (g h) q p", q=8))
    ld_gw = dma("gw", GW, a["gm_w_s"][0].rearrange("g t s -> t g s"))
    ld_d = dma("sd", DB, row(a["s5_d"][0], 1024))
    ld_gmg = dma("gmg", GMG, row(a["gm_norm_g"][0], 1024))

    b, t, bf = bank()
    ev = T(lambda e, t=t: e.transpose(t[:, 0:110], VST[:, :], IDENT[0:110, 0:110]), ld_v, ld_c, bf)
    ev_vec = V(lambda e, t=t: e.tensor_copy(VEC[:, :], t[:, 0:110]), ev)
    bank_done(b, ev_vec)

    ready, ss0 = [], sum_stat(4)
    x_gen = begin(x_turning(ready, X, VEC[:, V_N1:V_N1 + 16], [[e, ev_vec] for e in ld_xc], None), 4)
    gain_x2 = stat(16)
    ev_gx = V(lambda e: e.tensor_tensor(gain_x2, VEC[:, V_FIN:V_FIN + 16], VEC[:, V_MIX:V_MIX + 16], ALU.mult), ev_vec)
    for c in range(4):
        ev = squares(X, ss0, c, ld_xc[c])
    rs0 = root(ss0, D, ev)
    pv = {}

    def pr(i):
        return PR[:, i, :]

    def vtt(o, x, y, op, *w):
        return V(lambda e: e.tensor_tensor(o, x, y, op), *w)

    def vts(o, x, s1, s2, o1, o2, *w):
        return V(lambda e: e.tensor_scalar(o, x, s1, s2, o1, o2), *w)

    def vstt(o, x, s, y, o1, o2, *w):
        return V(lambda e: e.scalar_tensor_tensor(out=o, in0=x, scalar=s, in1=y, op0=o1, op1=o2), *w)

    def prep():
        ev = V(lambda e: e.tensor_copy(S5ST[:, 2, :].rearrange("j (g p) -> j g p", g=2),
                                       LDT[:, :].unsqueeze(2).to_broadcast([32, 2, 64])), ld_s)
        b, t, bf = bank()

        def tr3(e, t=t):
            for i in range(3):
                ins = e.transpose(t[:, 32 * i:32 * i + 32], S5ST[:, i, :], IDENT[0:32, 0:32])
            return ins

        ev = T(tr3, ev, bf)
        ev = V(lambda e, t=t: e.tensor_copy(PR[:, 0:3, :], t[:, 0:96].rearrange("p (i j) -> p i j", i=3)), ev)
        bank_done(b, ev)

        ev = A(lambda e: e.activation(pr(3), pr(2), ACT.Exp), ev)
        ev = vtt(pr(4), pr(0), pr(3), ALU.mult, ev)
        ev_m = A(lambda e: e.activation(pr(5), pr(4), ACT.Exp), ev)
        ev = vtt(pr(6), pr(1), pr(3), ALU.mult, ev)
        MAGIC = 12582912.0
        ev = vts(pr(7), pr(6), 1.0 / (2 * np.pi), MAGIC, ALU.mult, ALU.add, ev)
        ev = vts(pr(7), pr(7), MAGIC, None, ALU.subtract, ALU.bypass, ev)
        c1 = 6.28125
        c2 = 0.0019350051879882812
        c3 = 2 * np.pi - c1 - c2
        ev = vstt(pr(8), pr(7), -c1, pr(6), ALU.mult, ALU.add, ev)
        ev = vstt(pr(8), pr(7), -c2, pr(8), ALU.mult, ALU.add, ev)
        ev = vstt(pr(8), pr(7), -c3, pr(8), ALU.mult, ALU.add, ev)
        yield
        ev = vts(pr(8), pr(8), PI_DOWN, -PI_DOWN, ALU.min, ALU.max, ev)
        ev_sn = A(lambda e: e.activation(pr(9), pr(8), ACT.Sin), ev)
        ev = A(lambda e: e.activation(pr(10), pr(8), ACT.Abs), ev)
        ev = vts(pr(10), pr(10), -1.0, float(np.pi / 2), ALU.mult, ALU.add, ev)
        ev = A(lambda e: e.activation(pr(10), pr(10), ACT.Sin), ev)
        ev_are = vtt(AP[:, 0, :, 0], pr(5), pr(10), ALU.mult, ev, ev_m)
        ev_aim = vtt(AP[:, 2, :, 0], pr(5), pr(9), ALU.mult, ev_sn)
        ar, ai = AP[:, 0, :, 0], AP[:, 2, :, 0]
        yield
        e1 = vtt(pr(13), pr(0), pr(0), ALU.mult)
        e2 = vtt(pr(14), pr(1), pr(1), ALU.mult)
        e1 = vtt(pr(13), pr(13), pr(14), ALU.add, e2)
        e1 = V(lambda e: e.reciprocal(pr(14), pr(13)), e1)
        e2 = vts(pr(15), ar, 1.0, None, ALU.subtract, ALU.bypass, ev_are)
        e3 = vtt(pr(16), pr(15), pr(0), ALU.mult, e2)
        e4 = vtt(pr(17), ai, pr(1), ALU.mult, ev_aim)
        e5 = vtt(pr(18), ai, pr(0), ALU.mult, e4)
        e6 = vtt(pr(21), pr(15), pr(1), ALU.mult, e5)
        e3 = vtt(pr(19), pr(16), pr(17), ALU.add, e6)
        e4 = vtt(pr(20), pr(18), pr(21), ALU.subtract, e6)
        e3 = vtt(pr(19), pr(19), pr(14), ALU.mult, e4)
        ev_k = vtt(pr(20), pr(20), pr(14), ALU.mult, e4)

        yield
        ev_ez = G(lambda e: e.memset(EX, 0.0))
        kre = pr(19).unsqueeze(2).to_broadcast([P, 32, 16])
        kim = pr(20).unsqueeze(2).to_broadcast([P, 32, 16])
        t0 = TMP[:, 0, :, :].rearrange("p a (j h) -> p (a j) h", h=16)
        t1 = TMP[:, 1, :, :].rearrange("p a (j h) -> p (a j) h", h=16)
        ev_e = ev_ez
        for i in range(2):
            e1 = G(lambda e, i=i: e.tensor_tensor(t0, BRI[:, i, :, :], kre, ALU.mult), ev_k, ld_b, ev_e)
            e2 = G(lambda e, i=i: e.tensor_tensor(t1, BRI[:, 1 - i, :, :], kim, ALU.mult), ev_k, ld_b, ev_e)
            for g in range(2):
                q = slice(64 * g, 64 * g + 64)
                ev_e = V(lambda e, i=i, g=g, q=q: e.tensor_tensor(EX[q, i, :, g, :], t0[q], t1[q],
                                                                  ALU.subtract if i == 0 else ALU.add), e1, e2, ev_ez)
        yield
        for i in range(2):
            for g in range(2):
                if i == 0:
                    ev_c = V(lambda e, g=g: e.tensor_scalar(CX[:, 0, :, g, :], CRI[:, 0, :, :], PAR[:, g:g + 1], None,
                                                            ALU.mult), ld_cc, ld_c)
                else:
                    ev_c = V(lambda e, g=g: e.tensor_scalar(CX[:, 1, :, g, :], CRI[:, 1, :, :], PAR[:, g:g + 1], -1.0,
                                                            ALU.mult, ALU.mult), ld_cc, ld_c)
        yield
        u0 = TMP[:, 0, :, :].rearrange("p a n -> p (a n)")
        u1 = TMP[:, 1, :, :].rearrange("p a n -> p (a n)")
        ev = [ev_aim, ev_e]
        for n in (1, 2, 4, 8):
            re, im = AP[:, 0, :, 0:n], AP[:, 2, :, 0:n]
            mr = AP[:, 0, :, n - 1:n].to_broadcast([P, 32, n])
            mi = AP[:, 2, :, n - 1:n].to_broadcast([P, 32, n])
            yield
            v0 = u0[:, 0:32 * n].rearrange("p (j n) -> p j n", n=n)
            v1 = u1[:, 0:32 * n].rearrange("p (j n) -> p j n", n=n)
            e1 = vtt(v0, re, mr, ALU.mult, ev)
            e1 = vtt(v1, im, mi, ALU.mult, ev)
            e1 = vtt(AP[:, 0, :, n:2 * n], v0, v1, ALU.subtract, e1)
            e2 = vtt(v0, re, mi, ALU.mult, e1)
            e2 = vtt(v1, im, mr, ALU.mult, e1)
            ev = vtt(AP[:, 2, :, n:2 * n], v0, v1, ALU.add, e2)
        ev_ap = vts(AP[:, 1, :, :], AP[:, 2, :, :], -1.0, None, ALU.mult, ALU.bypass, ev)

        pv.update(ap=ev_ap, e=ev_e, c=ev_c)
        yield
        ev_gw = G(lambda e: e.affine_select(out=GW, in_=GW, compare_op=ALU.is_ge, fill=0.0, base=0,
                                            pattern=[[0, 8], [-1, P]], channel_multiplier=1), ld_gw)
        for g4 in range(2):
            b, t, bf = bank()

            def tr4(e, t=t, g4=g4):
                for g in range(4):
                    ins = e.transpose(t[:, g * P:g * P + P], GW[:, 4 * g4 + g, :], IDENT)
                return ins

            ev = T(tr4, ev_gw, bf)
            ev_ws = V(lambda e, t=t, g4=g4: e.tensor_copy(WS[:, 4 * g4:4 * g4 + 4, :],
                                                          t[:, :].rearrange("p (g s) -> p g s", g=4)), ev)
            bank_done(b, ev_ws)
            yield
        b, t, bf = bank()

        def tr6(e, t=t):
            for c in range(6):
                ins = e.transpose(t[:, 34 * c:34 * c + 34], DWS[:, c * P:c * P + P], IDENT[0:34, 0:34])
            return ins

        ev_dw_t = T(tr6, ld_dw, bf)
        ev_dw = V(lambda e, t=t: e.tensor_copy(DWT[:, :, :], t[:, 0:204].rearrange("p (c k) -> p c k", c=6)), ev_dw_t)
        bank_done(b, ev_dw)
        pv.update(ws=ev_ws, gw=ev_gw, dw=ev_dw, dwt=ev_dw_t)


    BT = X[:, 0, :].rearrange("p (a q s) -> p a q s", a=2, q=8)
    UT = X[:, 1, :].rearrange("p (q t) -> p q t", q=8)

    def s5_turn(src, dst, *waits):
        for i in range(2):
            for q4 in range(2):
                b, t, bf = bank()

                def tr(e, t=t, i=i, q4=q4):
                    for q in range(4):
                        ins = e.transpose(t[:, q * P:q * P + P], src(i, 4 * q4 + q), IDENT)
                    return ins

                ev = T(tr, bf, *waits)
                ev = A(lambda e, t=t, i=i, q4=q4: e.activation(
                    dst[:, i, 4 * q4:4 * q4 + 4, :], t[:, :].rearrange("p (q s) -> p q s", q=4), ACT.Copy), ev)
                bank_done(b, ev)
        return ev

    ev_s5 = {}

    def s5_run():
        yield from prep()
        ev_e, ev_c, ev_ap, ev_ws, ev_gw = (pv[k] for k in ("e", "c", "ap", "ws", "gw"))
        while "in" not in ev_s5:
            yield
        ev_x_read = ready
        ev_bt = s5_turn(lambda i, q: EX[:, i, 4 * q:4 * q + 4, :, :].rearrange("p j g h -> p (j g h)"), BT, ev_e, ev_x_read)
        yield
        ev_ct = s5_turn(lambda i, q: CX[:, i, q, :, :].rearrange("p g s -> p (g s)"), CT, ev_c)
        yield
        for k in range(0, 8, 2):
            b, t, bf = bank()

            def tr(e, t=t, k=k):
                for m in range(2):
                    for half in range(2):
                        ins = e.transpose(t[:, m * L + half * P:m * L + half * P + P],
                                          XIN[:, half, (k + m) * P:(k + m) * P + P], IDENT)
                return ins

            ev = T(tr, bf, ev_s5["in"])
            ev_u = A(lambda e, t=t, k=k: e.activation(UT[:, k:k + 2, :], t[:, :].rearrange("p (m t) -> p m t", m=2),
                                                      ACT.Copy), ev)
            bank_done(b, ev_u)
        yield
        for half in range(2):
            ev_dx = G(lambda e, half=half: e.tensor_tensor(XIN[:, half, :], XIN[:, half, :], DB, ALU.mult),
                      ld_d, T.now(), ev_s5["in"])
        yield
        ev_free = [ev_dx, ev_ct, ev_bt, ev_e, ev_c, ev_ws, ev_gw]
        Sv = SS[:, :, :, :].rearrange("p a j (c i) -> p a j c i", i=16)
        for r in range(2):
            for jj in range(16):
                j = 16 * r + jj
                q, i = j // 4, j % 4
                b, t, bf = bank()
                rows = slice(32 * i, 32 * i + 32)

                def mm(e, t=t, q=q, rows=rows):
                    for ri in range(2):
                        ins = e.matmul(t[:, ri * L:ri * L + L], BT[rows, ri, q, :], UT[rows, q, :],
                                       start=True, stop=True)
                    return ins

                ev = T(mm, bf, ev_bt, ev_u)
                ev_bu = A(lambda e, t=t, jj=jj: e.activation(SS[:, :, jj, :], t[:, :].rearrange("p (a t) -> p a t", a=2),
                                                             ACT.Copy), ev, ev_free)
                bank_done(b, ev_bu)
                if jj % 4 == 3:
                    yield
            if r == 1:
                ev_s5["x_free"] = T.now()
            parts = [(V, 0, NV, 0), (G, NV, 16, NV * 16)]
            last = {}

            def step(k, dst, src, rr, ii, shape, j0, j1, tk):
                n = 1
                for d in shape[1:]:
                    n *= d
                tv = []
                for z in range(2):
                    f = TMP[:, z, :, tk:tk + n]
                    tv.append(f if len(shape) == 2 else f.rearrange("p a (j c) -> p a j c", c=shape[2]))
                Q = parts[k][0]
                w = [last.get(k), ev_bu, ev_ap]
                Q(lambda e: e.tensor_tensor(tv[0], src, rr, ALU.mult), w)
                e1 = Q(lambda e: e.tensor_tensor(tv[1], src[:, ::-1], ii, ALU.mult), w)
                e1 = Q(lambda e: e.tensor_tensor(dst, dst, tv[0], ALU.add), e1)
                last[k] = Q(lambda e: e.tensor_tensor(dst, dst, tv[1], ALU.add), e1)

            def coef(j0, j1, p, n):
                js = slice(16 * r + j0, 16 * r + j1)
                if n is None:
                    return (AP[:, 0, js, p].unsqueeze(1).to_broadcast([P, 2, j1 - j0]), AP[:, 1:3, js, p])
                rr = AP[:, 0, js, p].unsqueeze(1).unsqueeze(3).to_broadcast([P, 2, j1 - j0, n])
                ii = AP[:, 1:3, js, p].unsqueeze(3).to_broadcast([P, 2, j1 - j0, n])
                return rr, ii

            for i in range(1, 16):
                for k, (Q, j0, j1, tk) in enumerate(parts):
                    rr, ii = coef(j0, j1, 0, 16)
                    step(k, Sv[:, :, j0:j1, :, i], Sv[:, :, j0:j1, :, i - 1], rr, ii, (2, j1 - j0, 16), j0, j1, tk)
                yield
            for c in range(1, 16):
                for k, (Q, j0, j1, tk) in enumerate(parts):
                    rr, ii = coef(j0, j1, 15, None)
                    step(k, Sv[:, :, j0:j1, c, 15], Sv[:, :, j0:j1, c - 1, 15], rr, ii, (2, j1 - j0), j0, j1, tk)
                if c % 3 == 0:
                    yield
            for i in range(15):
                for k, (Q, j0, j1, tk) in enumerate(parts):
                    rr, ii = coef(j0, j1, i, 15)
                    step(k, Sv[:, :, j0:j1, 1:16, i], Sv[:, :, j0:j1, 0:15, 15], rr, ii, (2, j1 - j0, 15), j0, j1, tk)
                yield
            for half in range(2):
                b, t, bf = bank()

                def mm(e, t=t, half=half, r=r):
                    for jj in range(16):
                        j = 16 * r + jj
                        q, i = j // 4, j % 4
                        for ri in range(2):
                            ins = e.matmul(t[:, 32 * jj:32 * jj + 32], SS[:, ri, jj, half * P:half * P + P],
                                           CT[:, ri, q, 32 * i:32 * i + 32], start=(ri == 0), stop=(ri == 1))
                    return ins

                ev = T(mm, bf, [last[0], last[1]], ev_ct)
                ev_y = V(lambda e, t=t, half=half, r=r: e.tensor_tensor(
                    XIN[:, half, 512 * r:512 * r + 512], t[:, :], XIN[:, half, 512 * r:512 * r + 512], ALU.add), ev, ev_dx)
                bank_done(b, ev_y)
            ev_free = [ev_y, ev]
            yield
        ev_s5["y"] = A(lambda e: e.activation(XIN[:, :, :], XIN[:, :, :], ACT.Gelu_apprx_tanh), ev_y)

    s5_gen = later(s5_run())
    for c in range(2):
        s, ev = product(w_in1, 16, 512 * (4 + c), XTH, XTL, ready if c == 0 else None)
        for half in range(2):
            e1 = A(lambda e, s=s, c=c, half=half: e.activation(
                XIN[:, half, 512 * c:512 * c + 512], ACC[:, 2 * s + half, :], ACT.Copy, scale=rs0[0][:, half:half + 1]),
                ev, rs0[1])
        acc_free[s] = [e1]
    ev_s5["in"] = e1

    ssv = sum_stat(2)
    for c in range(2):
        s, ev = product(w_in1, 16, 512 * (2 + c), XTH, XTL, None)
        while "dwt" not in pv:
            side_step()
        for half in range(2):
            e1 = A(lambda e, s=s, c=c, half=half: e.activation(
                VG[:, half, 512 * c:512 * c + 512], ACC[:, 2 * s + half, :], ACT.Gelu_apprx_tanh,
                scale=rs0[0][:, half:half + 1]), ev, pv["dwt"], rs0[1])
        acc_free[s] = [e1]
        esq = squares(VG, ssv, c, e1)
    rsv = root(ssv, 1024, esq)
    for half in range(2):
        ev_vn = vstt(VG[:, half, :], VG[:, half, :], rsv[0][:, half:half + 1], GMG, ALU.mult, ALU.mult, rsv[1], ld_gmg)
    ya = []

    def gmlp(c, ev_ug):
        yield
        for half in range(2):
            b, t, bf = bank()

            def mm(e, t=t, half=half):
                for g in range(4):
                    ins = e.matmul(t[:, g * P:g * P + P], WS[:, 4 * c + g, :],
                                   VG[:, half, (4 * c + g) * P:(4 * c + g) * P + P], start=True, stop=True)
                return ins

            ev = T(mm, bf, ev_vn, pv["ws"])
            for g in range(4):
                ug = UG[c][:, half, g * P:g * P + P]
                e1 = vstt(ug, t[:, g * P:g * P + P], VEC[:, V_GB + 4 * c + g:V_GB + 4 * c + g + 1], ug,
                          ALU.add, ALU.mult, ev, ev_ug)
            bank_done(b, e1)
            yield
        yield from turning(ya, lambda k, half: UG[c][:, half, k * P:k * P + P], 4, YAH[:, 4 * c:4 * c + 4, :],
                           YAL[:, 4 * c:4 * c + 4, :], e1, wait=1)

    gm_gens = []
    for c in range(2):
        s, ev = product(w_in1, 16, 512 * c, XTH, XTL, None)
        for half in range(2):
            e1 = A(lambda e, s=s, c=c, half=half: e.activation(
                UG[c][:, half, :], ACC[:, 2 * s + half, :], ACT.Gelu_apprx_tanh, scale=rs0[0][:, half:half + 1]), ev, ev_vn)
        acc_free[s] = [e1]
        gm_gens.append(later(gmlp(c, e1), first=True))

    bg1 = a["b_gate"][0]

    def gmlp_done():
        for g in reversed(gm_gens):
            while g in side:
                side_step()
        return [T.now(), A.now(), V.now()]

    def merged_free():
        while "x_free" not in ev_s5:
            side_step()
        return ev_s5["x_free"]

    pace[0] = PACE
    res, ev_ya = gate_branch(w_in1, GATE0, bg1[0], rs0, wbr[0], 8, lambda: ya, X, SGA, gmlp_done, True, merged_free, True)
    s, ev = product(w_in1, 16, 512 * 6, XTH, XTL, None)
    side_drain(s5_gen)
    pace[0] = 1
    fence = everything()
    s5.close()

    QKV = sb("QKV", [P, 2, 3072], to=one)
    QT = sb("QT", [P, 8, L], to=one)
    KT = sb("KT", [P, 8, L], to=one)
    SG = sb("SG", [P, 2, D], to=one)
    BGL = sb("BGL", [P, 1024], to=one)
    ld_bgl = dma("bgl", BGL[:, :], row(a["s5_b_glu"][0], 1024), fence)
    gt = []
    gt_gen = later(turning(gt, lambda k, half: XIN[:, half, k * P:k * P + P], 8, YAH, YAL, ev_s5["y"], free=ev_ya, wait=4))
    for c in range(6):
        if c > 0:
            s, ev = product(w_in1, 16, 512 * (6 + c), XTH, XTL, None)
        for half in range(2):
            e1 = A(lambda e, s=s, c=c, half=half: e.activation(
                QKV[:, half, 512 * c:512 * c + 512], ACC[:, 2 * s + half, :], ACT.Copy, scale=rs0[0][:, half:half + 1]),
                ev, fence)
        acc_free[s] = [e1]
    side_drain(gt_gen)
    ev_qkv = e1

    ev_at = {}
    HW = 384
    pool2 = QKV[:, :, 0:D]
    ZSb, SPb = QKV[:, 0, 0:4 * HW], QKV[:, 1, 0:4 * HW]

    def attention():
        for src, dst in ((0, QT), (1024, KT)):
            for h in range(0, 8, 2):
                b, t, bf = bank()

                def tr(e, t=t, src=src, h=h):
                    for m in range(2):
                        for half in range(2):
                            ins = e.transpose(t[:, m * L + half * P:m * L + half * P + P],
                                              QKV[:, half, src + (h + m) * P:src + (h + m) * P + P], IDENT)
                    return ins

                ev = T(tr, bf, ev_qkv)
                ev_t = A(lambda e, t=t, dst=dst, h=h: e.activation(
                    dst[:, h:h + 2, :], t[:, :].rearrange("p (m t) -> p m t", m=2), ACT.Copy), ev, fence)
                bank_done(b, ev_t)
                yield
        free = [ev]
        for hg in range(2):
            for hh in range(4):
                h = 4 * hg + hh
                b, t, bf = bank()

                def mm(e, t=t, h=h):
                    e.matmul(t[:, 0:L], KT[:, h, 0:P], QT[:, h, :], start=True, stop=True)
                    return e.matmul(t[:, L:HW], KT[:, h, P:L], QT[:, h, P:L], start=True, stop=True)

                ev = T(mm, bf, ev_t)
                ev_z = A(lambda e, t=t, hh=hh: e.activation(ZSb[:, hh * HW:hh * HW + HW], t[:, 0:HW], ACT.Copy,
                                                            scale=128.0 ** -0.5), ev, free)
                bank_done(b, ev_z)
            yield
            e1 = A(lambda e: e.activation(SPb, ZSb, ACT.Abs), ev_z, free)
            e1 = A(lambda e: e.activation(SPb, SPb, ACT.Exp, scale=-1.0), e1)
            e1 = A(lambda e: e.activation(SPb, SPb, ACT.Ln, bias=1.0), e1)
            yield
            e1 = vstt(SPb, ZSb, 0.0, SPb, ALU.max, ALU.add, e1)
            yield
            for buf, fill in ((SPb, 0.0), (ZSb, -1e30)):
                for d in (0, 2):
                    v = buf.rearrange("p (h b c) -> p h b c", h=4, b=3)[:, :, d, :]
                    ev_m = G(lambda e, v=v, fill=fill: e.affine_select(
                        out=v, in_=v, compare_op=ALU.is_gt, fill=fill, base=0, pattern=[[0, 4], [1, P]],
                        channel_multiplier=-1), e1)
            yield
            for hh in range(4):
                sp = SPb[:, hh * HW:hh * HW + HW]
                b, t, bf = bank()

                def mm(e, t=t, sp=sp):
                    e.matmul(t[:, 0:P], TRI, sp[:, 0:P], start=True, stop=True)
                    e.matmul(t[:, P:L], TRI, sp[:, P:L], start=True, stop=False)
                    e.matmul(t[:, P:L], ONES, sp[:, L:HW], start=False, stop=True)
                    return e.matmul(t[:, L:HW], TRI, sp[:, L:HW], start=True, stop=True)

                ev = T(mm, bf, ev_m)
                zs = ZSb[:, hh * HW:hh * HW + HW]
                e2 = vtt(zs, zs, t[:, 0:HW], ALU.subtract, ev, ev_m)
                bank_done(b, e2)
            yield
            e2 = A(lambda e: e.activation(ZSb, ZSb, ACT.Exp), e2)
            yield
            for hp in range(2):
                b, t, bf = bank()

                def mm(e, t=t, hp=hp, hg=hg):
                    for m in range(2):
                        hh = 2 * hp + m
                        vc = D + (4 * hg + hh) * P
                        w = ZSb[:, hh * HW:hh * HW + HW]
                        e.matmul(t[:, m * L:m * L + P], QKV[:, 0, vc:vc + P], w[:, 0:P], start=True, stop=True)
                        e.matmul(t[:, m * L + P:m * L + L], QKV[:, 0, vc:vc + P], w[:, P:L], start=True, stop=False)
                        ins = e.matmul(t[:, m * L + P:m * L + L], QKV[:, 1, vc:vc + P], w[:, L:HW],
                                       start=False, stop=True)
                    return ins

                ev = T(mm, bf, e2)
                k = 4 * hg + 2 * hp
                tv = t[:, :].rearrange("p (m t) -> p m t", m=2)
                e3 = A(lambda e, k=k, tv=tv: e.activation(YAH[:, k:k + 2, :], tv, ACT.Copy), ev, ev_at["free"])
                e4 = vtt(YAL[:, k:k + 2, :], tv, YAH[:, k:k + 2, :], ALU.subtract, e3, ev_at["free"])
                bank_done(b, e4)
                ev_at.setdefault("y", []).append(e4)
            free = [ev, e2]
            yield

    at_gen = attention()
    for c in range(2):
        s, ev = product(a["s5_w_glu"][0], 8, 512 * c, YAH, YAL, gt if c == 0 else None)
        sg = SG[:, :, 512 * c:512 * c + 512]
        for half in range(2):
            e1 = vtt(sg[:, half, :], ACC[:, 2 * s + half, :], BGL[:, 512 * c:512 * c + 512], ALU.add, ev, ld_bgl, fence)
        acc_free[s] = [e1]
        e1 = A(lambda e, sg=sg: e.activation(sg, sg, ACT.Sigmoid), e1)
        xi = XIN[:, :, 512 * c:512 * c + 512]
        ev_yb = G(lambda e, xi=xi, sg=sg: e.tensor_tensor(xi, xi, sg, ALU.mult), e1, gt)
    ev_at["free"] = ev
    side.append(at_gen)

    def yc_ready():
        side_drain(at_gen)
        return ev_at["y"]

    res, ev_yc = gate_branch(w_in1, GATE0 + 2 * D, bg1[2], rs0, wbr[2], 8, yc_ready, X, SG, lambda: [ev_yb], False, res, True)
    yb = []
    yb_gen = later(turning(yb, lambda k, half: XIN[:, half, k * P:k * P + P], 8, YAH, YAL, ev_yb, free=ev_yc, wait=2))

    def yb_ready():
        side_drain(yb_gen)
        return yb

    mready = []

    def merged_turner(src, out):
        def go(c, ev, gates_done):
            later(turning(out, lambda k, half: src[:, half, 512 * c + k * P:512 * c + k * P + P], 4,
                          XTH[:, 4 * c:4 * c + 4, :], XTL[:, 4 * c:4 * c + 4, :], ev, free=gates_done, wait=1))
        return go

    gate_branch(w_in1, GATE0 + D, bg1[1], rs0, wbr[1], 8, yb_ready, X, SG, lambda: [A.now(), G.now()], False, res, True,
                last=merged_turner(X, mready), add=V)
    fence = everything()
    one.close()

    def x_again():
        while len(mready) < 8:
            yield
        ld_x.append(dma("x0", X[:, :, :], x0, T.now()))

    ld_x = []
    later(x_again())
    ss1 = sum_stat(4)

    def x_loaded():
        while not ld_x:
            side_step()
        return ld_x

    xr, ev_xt, esq = residual_product(a["w_out"][0], X, mready, x_loaded, ss1)
    rs1 = root(ss1, D, esq)

    ready, ready2 = [], []
    begin(x_turning(ready, X, VEC[:, V_N2:V_N2 + 16], xr, ev_xt), 4)
    ss2, ss3 = sum_stat(4), sum_stat(4)
    x1 = []

    def mlp1_done(c, ev, xt_free):
        x1.append(ev)
        sq2.append(squares(X, ss2, c, ev))
        later(turning(ready2, lambda k, half: X[:, half, 512 * c + k * P:512 * c + k * P + P], 4,
                      XTH[:, 4 * c:4 * c + 4, :], XTL[:, 4 * c:4 * c + 4, :], ev, ev_gx, free=xt_free, wait=1,
                      gain=lambda k: gain_x2[:, 4 * c + k:4 * c + k + 1]))

    sq2 = []
    mlp("1", a["w_mlp_in"][0], a["w_mlp_out"][0], X, ready, rs1, xr, mlp1_done)
    rs2 = root(ss2, D, sq2[-1])
    ready = ready2

    two = ExitStack()
    fence = everything()
    MG = sb("MG", [P, 2, D], to=two)
    ZA = MG[:, :, :].rearrange("p a n -> p (a n)")[:, 0:3072].rearrange("p (a n) -> p a n", a=2)
    ZB = MG[:, :, :].rearrange("p a n -> p (a n)")[:, 3072:4096].rearrange("p (a n) -> p a n", a=2)
    ZCb = sb("ZCb", [P, 2 * 2304], to=two)
    ZC = ZCb[:, :].rearrange("p (a n) -> p a n", a=2)
    SG2 = ZCb[:, 0:2 * D].rearrange("p (a n) -> p a n", a=2)
    UA = sb("UA", [P, 6, 30 + L], to=two)
    CA = sb("CA", [P, 6, L], to=two)
    VT = sb("VT", [P, 2, 768], to=two)
    PC = sb("PC", [P, 6, 2 + L], to=two)
    GBT = sb("GBT", [P, 6, L], to=two)
    PM = sb("PM", [P, 4, 2, L], to=two)
    PT = sb("PT", [P, 4, L], to=two)
    WG = sb("WG", [P, 4, P], to=two)
    BG = VT[:, :, :].rearrange("p a n -> p (a n)")
    FG = ZCb[:, 0:D]
    ld_fg = dma("fg", FG, row(a["final_g"], D), fence)
    ld_bg = dma("bglu2", BG, row(a["b_glu_2"][0], 1536), fence)
    ld_pm = dma("pm", PM[:, :, :, :], a["pmat"], fence)
    ld_wg = dma("wgrp", WG[:, :, :], a["w_pool_grp_2"][0].rearrange("g c d -> c g d"), fence)
    ev_pad = G(lambda e: e.memset(UA[:, :, 0:30], 0.0), fence)
    ev_pad = G(lambda e: e.memset(PC[:, :, 0:2], 0.0), fence)

    x2 = {}

    def close_block1():
        while len(ready) < 8:
            yield
        read = T.now()
        for half in range(2):
            ev = vstt(X[:, half, :], X[:, half, :], rs2[0][:, half:half + 1], FG, ALU.mult, ALU.mult, rs2[1], ld_fg, read)
        x2["fg"] = ev
        yield
        for c in range(4):
            e1 = squares(X, ss3, c, ev)
            yield
        r3, e1 = root(ss3, D, e1)
        r23 = stat(2)
        x2["rs"] = (r23, vtt(r23, r3, rs2[0], ALU.mult, e1))

    x2_gen = later(close_block1())
    for c in range(3):
        s, ev = product(w_in2, 16, 512 * c, XTH, XTL, ready if c == 0 else None)
        if c == 0:
            side_drain(x2_gen)
            rsb, xr = x2["rs"], x2["fg"]
        for half in range(2):
            e1 = vstt(ZA[:, half, 512 * c:512 * c + 512], ACC[:, 2 * s + half, :], rsb[0][:, half:half + 1],
                      BG[:, 512 * c:512 * c + 512], ALU.mult, ALU.add, ev, ld_bg, fence, rsb[1])
        acc_free[s] = [e1]
    e1 = A(lambda e: e.activation(ZA[:, :, 768:1536], ZA[:, :, 768:1536], ACT.Sigmoid), e1)
    ev_ua = G(lambda e: e.tensor_tensor(ZA[:, :, 0:768], ZA[:, :, 0:768], ZA[:, :, 768:1536], ALU.mult), e1)

    def plain_turn(src, k0, n, dst, *waits):
        b, t, bf = bank()

        def tr(e):
            for m in range(n):
                for half in range(2):
                    ins = e.transpose(t[:, m * L + half * P:m * L + half * P + P], src(k0 + m, half), IDENT)
            return ins

        ev = T(tr, bf, *waits)
        ev = A(lambda e: e.activation(dst, t[:, 0:n * L].rearrange("p (m t) -> p m t", m=n), ACT.Copy), ev, fence)
        bank_done(b, ev)
        return ev

    ya2 = []
    va = {}

    def conv_a():
        yield
        yield
        for k in range(0, 6, 2):
            ev_t = plain_turn(lambda k, half: ZA[:, half, k * P:k * P + P], k, 2, UA[:, k:k + 2, 30:30 + L], ev_ua)
            yield
        va["za_read"] = T.now()
        prev = [None] * 6
        for k in range(31):
            for c in range(6):
                tap = DWT[:, c, k:k + 1]
                if k == 0:
                    prev[c] = vts(CA[:, c, :], UA[:, c, 0:L], tap, VEC[:, V_DB + c:V_DB + c + 1], ALU.mult, ALU.add,
                                  ev_t, ev_pad, fence)
                else:
                    prev[c] = vstt(CA[:, c, :], UA[:, c, k:k + L], tap, CA[:, c, :], ALU.mult, ALU.add, prev[c])
                if c == 2:
                    yield
            yield
        for half in range(2):
            for c0, n in ((0, 4), (4, 2)):
                b, t, bf = bank()

                def tr(e, t=t, c0=c0, n=n, half=half):
                    for m in range(n):
                        ins = e.transpose(t[:, m * P:m * P + P], CA[:, c0 + m, half * P:half * P + P], IDENT)
                    return ins

                ev = T(tr, bf, prev)
                e1 = A(lambda e, t=t, c0=c0, n=n, half=half: e.activation(
                    VT[:, half, c0 * P:(c0 + n) * P], t[:, 0:n * P], ACT.Copy), ev, acc_bg)
                bank_done(b, e1)
            yield
        e1 = [e1]
        for half in range(2):
            bs, mv, rs = stat(12), stat(2), stat(1)
            for q in range(2):
                e2 = V(lambda e, half=half, q=q, bs=bs: e.bn_stats(bs[:, 6 * q:6 * q + 6],
                                                                   VT[:, half, 384 * q:384 * q + 384]), e1)
            e2 = V(lambda e, bs=bs, mv=mv: e.bn_aggr(mv, bs.rearrange("p (q s) -> p q s", q=2)), e2)
            e2 = vts(rs, mv[:, 1:2], EPS, None, ALU.add, ALU.bypass, e2)
            e2 = A(lambda e, rs=rs: e.activation(rs, rs, ACT.Sqrt), e2)
            e2 = V(lambda e, rs=rs: e.reciprocal(rs, rs), e2)
            ev_ln = vts(VT[:, half, :], VT[:, half, :], mv[:, 0:1], rs, ALU.subtract, ALU.mult, e2)
            yield
        for k in range(0, 6, 2):
            b, t, bf = bank()

            def tr(e, t=t, k=k):
                for m in range(2):
                    for half in range(2):
                        ins = e.transpose(t[:, m * L + half * P:m * L + half * P + P],
                                          VT[:, half, (k + m) * P:(k + m) * P + P], IDENT)
                return ins

            ev = T(tr, bf, ev_ln)
            for m in range(2):
                e1 = vts(CA[:, k + m, :], t[:, m * L:m * L + L], VEC[:, V_LG + k + m:V_LG + k + m + 1],
                         VEC[:, V_LB + k + m:V_LB + k + m + 1], ALU.mult, ALU.add, ev)
            bank_done(b, e1)
            e1 = A(lambda e, k=k: e.activation(UA[:, k:k + 2, 0:L], CA[:, k:k + 2, :], ACT.Sigmoid), e1)
            va["v"] = vtt(CA[:, k:k + 2, :], CA[:, k:k + 2, :], UA[:, k:k + 2, 0:L], ALU.mult, e1)
            yield

    def place(src, n, free, *waits):
        evs = []
        for k in range(0, n, 2):
            e1 = A(lambda e, k=k: e.activation(YAH[:, k:k + 2, :], src[:, k:k + 2, :], ACT.Copy), free, *waits)
            evs.append(vtt(YAL[:, k:k + 2, :], src[:, k:k + 2, :], YAH[:, k:k + 2, :], ALU.subtract, e1, free))
        return evs

    acc_bg = e1
    va_gen = later(conv_a())

    for c in range(5):
        n = 512 if c < 4 else 256
        s, ev = product(w_in2, 16, ZC0 + 512 * c, XTH, XTL, None, n=n)
        for half in range(2):
            e1 = A(lambda e, s=s, c=c, n=n, half=half: e.activation(
                ZC[:, half, 512 * c:512 * c + n], ACC[:, 2 * s + half, 0:n], ACT.Copy, scale=rsb[0][:, half:half + 1]),
                ev, fence, xr)
        acc_free[s] = [e1]
    ev_zc = e1
    ev_p = G(lambda e: e.tensor_tensor(ZC[:, :, 768:1536], ZC[:, :, 768:1536], ZC[:, :, 1536:2304], ALU.mult), ev_zc)
    vc = {}

    def conv_c():
        yield
        yield
        for k in range(0, 6, 2):
            ev_g = plain_turn(lambda k, half: ZC[:, half, k * P:k * P + P], k, 2, GBT[:, k:k + 2, :], ev_zc)
            yield
        for k in range(0, 6, 2):
            ev_t = plain_turn(lambda k, half: ZC[:, half, 768 + k * P:768 + k * P + P], k, 2, PC[:, k:k + 2, 2:2 + L], ev_p)
            yield
        vc["read"] = [T.now(), ev_p]
        prev = [None] * 6
        for tap in range(3):
            for c in range(6):
                w = DWT[:, c, 31 + tap:32 + tap]
                if tap == 0:
                    prev[c] = vts(WGC[:, c, :], PC[:, c, 0:L], w, None, ALU.mult, ALU.bypass, ev_t, ev_pad, fence)
                else:
                    prev[c] = vstt(WGC[:, c, :], PC[:, c, tap:tap + L], w, WGC[:, c, :], ALU.mult, ALU.add, prev[c])
                if c % 3 == 2:
                    yield
        vc["v"] = G(lambda e: e.tensor_tensor(GBT[:, :, :], GBT[:, :, :], WGC[:, :, :], ALU.mult), prev, ev_g)

    WGC = sb("WGC", [P, 6, L], to=two)
    vc_gen = later(conv_c(), first=True)
    s, ev = product(w_in2, 16, 1536, XTH, XTL, None)
    for half in range(2):
        ev_zb = A(lambda e, s=s, half=half: e.activation(ZB[:, half, :], ACC[:, 2 * s + half, :], ACT.Copy,
                                                         scale=rsb[0][:, half:half + 1]), ev, fence)
    acc_free[s] = [ev_zb]
    yb2 = []
    vb = {}

    def pools():
        yield
        for g in range(0, 4, 2):
            b, t, bf = bank()

            def mm(e, t=t, g=g):
                for m in range(2):
                    for half in range(2):
                        ins = e.matmul(t[:, m * L:m * L + L], ZB[:, half, (g + m) * P:(g + m) * P + P],
                                       PM[:, g + m, half, :], start=(half == 0), stop=(half == 1))
                return ins

            ev = T(mm, bf, ev_zb, ld_pm)
            e2 = A(lambda e, t=t, g=g: e.activation(PT[:, g:g + 2, :], t[:, :].rearrange("p (m t) -> p m t", m=2), ACT.Copy),
                   ev, fence)
            bank_done(b, e2)
            yield
        vb["read"] = T.now()
        yield
        for g in range(0, 4, 2):
            b, t, bf = bank()

            def mm(e, t=t, g=g):
                for m in range(2):
                    ins = e.matmul(t[:, m * L:m * L + L], WG[:, g + m, :], PT[:, g + m, :], start=True, stop=True)
                return ins

            ev = T(mm, bf, e2, ld_wg)
            for m in range(2):
                sc_ = VEC[:, V_PS + g + m:V_PS + g + m + 1]
                e3 = A(lambda e, t=t, g=g, m=m, sc_=sc_: e.activation(YAH[:, g + m, :], t[:, m * L:m * L + L], ACT.Copy,
                                                                      scale=sc_), ev, fence)
            for m in range(2):
                sc_ = VEC[:, V_PS + g + m:V_PS + g + m + 1]
                e4 = vstt(YAL[:, g + m, :], t[:, m * L:m * L + L], sc_, YAH[:, g + m, :], ALU.mult, ALU.subtract, e3, fence)
            bank_done(b, e4)
            yb2.append(e4)
            yield

    vb_gen = later(pools(), first=True)

    def sg2_free():
        side_drain(vb_gen)
        while vc_gen in side and "read" not in vc:
            side_step()
        return [vc["read"], ev_zc]

    def mg_free():
        while "za_read" not in va:
            side_step()
        return [va["za_read"], vb["read"]]

    bg2 = a["b_gate_2"][0].rearrange("(n d) -> n d", n=3)
    SGB = SG2[:, :, 0:512]
    res, ev_b = gate_branch(wg2, D, bg2[1], rsb, a["w_b_out_2"][0], 4, lambda: yb2, MG, SGB, sg2_free, True, mg_free, False)

    def yc2():
        side_drain(vc_gen) if vc_gen in side else None
        return place(GBT, 6, ev_b, vc["v"])

    res, ev_c2 = gate_branch(wg2, 2 * D, bg2[2], rsb, a["w_c_out_2"][0], 6, yc2, MG, SGB, lambda: [G.now()], False, res, False)

    def ya2_ready():
        side_drain(va_gen)
        return place(CA, 6, ev_c2, va["v"])

    mready2 = []
    gate_branch(wg2, 0, bg2[0], rsb, a["w_a_out_2"][0], 6, ya2_ready, MG, SG2, lambda: [A.now(), G.now()], False, res, True,
                last=merged_turner(MG, mready2), add=V)
    ss4 = sum_stat(4)
    xr, ev_xt, esq = residual_product(a["w_o_2"][0], X, mready2, xr, ss4)
    two.close()
    rs4 = root(ss4, D, esq)
    ready, sq5 = [], []
    begin(x_turning(ready, X, VEC[:, V_MLP:V_MLP + 16], xr, ev_xt), 4)
    ss5 = sum_stat(4)
    x5 = []

    def mlp2_done(c, ev, xt_free):
        x5.append(ev)
        sq5.append(squares(X, ss5, c, ev))

    with ExitStack() as sc:
        FG2 = sb("FG2", [P, D], F32, sc)
        ld_fg = dma("fg2", FG2[:, :], row(a["g_final_2"], D), everything())
        mlp("2", a["w_up_2"][0], a["w_down_2"][0], X, ready, rs4, xr, mlp2_done)
        rs5 = root(ss5, D, sq5[-1])
        o = out[0].rearrange("(h p) n -> h p n", p=P)
        stores = []
        for half in range(2):
            for c in range(2):
                cs = slice(1024 * c, 1024 * c + 1024)
                ev = vstt(X[:, half, cs], X[:, half, cs], rs5[0][:, half:half + 1], FG2[:, cs], ALU.mult, ALU.mult,
                          rs5[1], ld_fg)
                stores.append(dma(f"out{half}{c}", o[half, :, cs], X[:, half, cs], ev))
    assert at["block"] == len(plan) and at["unit"] == len(units)
    for st in stores:
        S.items.append((lambda e, st=st: e.wait_ge(*st), [], None))

    block = ctx.enter_context(nc.Block())

    @block.sync
    def _(eng):
        S.play(eng)

    @block.tensor
    def _(eng):
        T.play(eng)

    @block.scalar
    def _(eng):
        A.play(eng)

    @block.vector
    def _(eng):
        V.play(eng)

    @block.gpsimd
    def _(eng):
        G.play(eng)

    ctx.close()


_INS = ["x", "norm1_g", "w_in", "b_gate", "gm_norm_g", "gm_w_s", "gm_b_s", "s5_lambda_re", "s5_lambda_im", "s5_log_dt",
        "s5_b_re", "s5_b_im", "s5_c_re", "s5_c_im", "s5_d", "s5_w_glu", "s5_b_glu", "w_branch", "w_out", "norm2_g",
        "w_mlp_in", "w_mlp_out", "final_g", "g_mix_2", "w_in_2", "w_gate_2", "b_gate_2", "b_glu_2", "w_dw_a_2",
        "b_dw_a_2", "ln_g_a_2", "ln_b_a_2", "w_a_out_2", "w_pool_grp_2", "pool_scale_2", "w_b_out_2", "w_dw_c_2",
        "w_c_out_2", "w_o_2", "g_mlp_2", "w_up_2", "w_down_2", "g_final_2"]


def kernel(**inputs):
    import numpy as _np
    import concourse.bacc as _bacc
    from concourse import mybir as _mybir
    from concourse.bass_utils import run_bass_kernel_spmd as _run

    nc = _bacc.Bacc("TRN2", target_bir_lowering=False, num_devices=1)
    arrays, aps = {}, {}
    cst, pmat = consts()
    for name in _INS + ["cst", "pmat"]:
        v = {"cst": cst, "pmat": pmat}.get(name)
        v = _np.ascontiguousarray(inputs[name] if v is None else v)
        arrays[f"in_{name}_dram"] = v
        aps[name] = nc.dram_tensor(f"in_{name}_dram", v.shape, _mybir.dt.from_np(v.dtype), kind="ExternalInput").ap()
    out = nc.dram_tensor("out_0_dram", (1, L, D), F32, kind="ExternalOutput").ap()
    build(nc, aps, out)
    r = _run(nc, [arrays], core_ids=[0])
    return r.results[0]["out_0_dram"]
```

```python
from collections import deque
from contextlib import ExitStack

import numpy as np
import concourse.bass as bass
from concourse import mybir

F32 = mybir.dt.float32
F32R = mybir.dt.float32r
ALU = mybir.AluOpType
ACT = mybir.ActivationFunctionType

P = 128
D = 2048
L = 256
EPS = 1e-6
NRAW = 4
NSPL = 4
POOL_W = (2, 4, 8, 16)
PI_DOWN = 3.1415925
VECS = ("norm1_g", "norm2_g", "g_mix_2", "g_mlp_2", "gm_b_s", "ln_g_a_2", "ln_b_a_2", "b_dw_a_2", "pool_scale_2", "final_g",
        "s5_d")
NVEC = 118
PACE_V, PACE_G, PACE_2 = 0.85, 0.9, 0.75
EARLY = 3
DEFER = 1


class Queue:

    def __init__(self, sem):
        self.sem, self.n, self.items = sem, 0, []

    def __call__(self, fn, *waits, inc=True):
        self.items.append((fn, list(flat(waits)), (self.sem, 1) if inc else None))
        self.n += inc
        return (self.sem, self.n)

    def now(self):
        return (self.sem, self.n)

    def play(self, eng):
        seen = {}
        for fn, waits, inc in self.items:
            for sem, val in waits:
                if seen.get(sem.name, 0) < val:
                    eng.wait_ge(sem, val)
                    seen[sem.name] = val
            ins = fn(eng)
            if inc:
                ins.then_inc(*inc)


def flat(waits):
    for w in waits:
        if isinstance(w, list):
            yield from flat(w)
        elif w is not None and w[1] > 0:
            yield w


def consts():
    c = np.zeros((P, 3 * P), np.float32)
    i = np.arange(P)
    c[:, 0:P] = np.eye(P)
    c[:, P:2 * P] = i[:, None] >= i[None, :]
    c[:, 2 * P:3 * P] = 1.0
    s, t = np.arange(L)[:, None], np.arange(L)[None, :]
    m = np.zeros((P, 4, 2, L), np.float32)
    for g, w in enumerate(POOL_W):
        band = ((s <= t) & (s > t - w)) / np.minimum(t + 1, w).astype(np.float64) - (s == t)
        m[:, g] = band.astype(np.float32).reshape(2, P, L).transpose(1, 0, 2)
    return c, m


def build(nc, a, out):
    ctx = ExitStack()

    def sem(name):
        return ctx.enter_context(nc.semaphore(name))

    T, A, V, G, S = (Queue(sem("q_" + n)) for n in ("tensor", "scalar", "vector", "pool", "sync"))

    def sb(name, shape, dt=F32, to=ctx):
        return to.enter_context(nc.sbuf_tensor(name, shape, dt))

    dma_count = {}

    def dma(name, dst, src, *waits):
        if name not in dma_count:
            dma_count[name] = [sem("d_" + name), 0]
        rec = dma_count[name]
        rec[1] += 16
        s = rec[0]
        S.items.append((lambda e: e.dma_start(dst, src).then_inc(s, 16), list(flat(waits)), None))
        return (s, rec[1])

    waiting, unissued = deque(), deque()

    def dma_later(name, pieces):
        evs = []
        assert name not in dma_count
        s = sem("d_" + name)
        dma_count[name] = [s, 16 * len(pieces)]
        for n, (dst, src) in enumerate(pieces):
            waiting.append((lambda e, dst=dst, src=src: e.dma_start(dst, src).then_inc(s, 16), [], None))
            evs.append((s, 16 * n + 16))
            unissued.append(evs[-1])
        return evs

    def issued(*evs):
        return not any(e in unissued for e in flat(evs))

    def row(ap, n):
        return ap.rearrange("(a n) -> a n", a=1).to_broadcast([P, n])

    def everything():
        return [q.now() for q in (T, A, V, G)]

    X = sb("X", [P, 2, D])
    XTH, XTL = sb("XTH", [P, 16, L], F32R), sb("XTL", [P, 16, L], F32R)
    RAW = [sb(f"RAW{i}", [P, 2, 512]) for i in range(NRAW)]
    WH = [sb(f"WH{i}", [P, 2, 512], F32R) for i in range(NSPL)]
    WL = [sb(f"WL{i}", [P, 2, 512], F32R) for i in range(NSPL)]
    YAH, YAL = sb("YAH", [P, 8, L], F32R), sb("YAL", [P, 8, L], F32R)
    CST = sb("CST", [P, 3 * P])
    VEC = sb("VEC", [P, NVEC])
    DWT = sb("DWT", [P, 6, 34])
    ST = sb("ST", [P, 160])
    GB = [sb(f"GB{i}", [P, 512]) for i in range(2)]
    JK = sb("JK", [P, 512])
    IDENT, TRI, ONES = CST[:, 0:P], CST[:, P:2 * P], CST[:, 2 * P:3 * P]
    ACC = ctx.enter_context(nc.psum_tensor("ACC", [P, 4, 512], F32))
    TB = [ctx.enter_context(nc.psum_tensor(f"TB{i}", [P, 512], F32)) for i in range(4)]

    st_used = [0]

    def stat(n):
        st_used[0] += n
        return ST[:, st_used[0] - n:st_used[0]]

    bank_free = [[] for _ in TB]
    bank_next = [0]

    def bank():
        i = bank_next[0] % 4
        bank_next[0] += 1
        assert bank_free[i] is not None
        free, bank_free[i] = bank_free[i], None
        return i, TB[i], free

    def bank_done(i, *evs):
        bank_free[i] = list(evs)

    side = deque()

    def side_step():
        while side:
            try:
                next(side[0])
                return
            except StopIteration:
                side.popleft()

    def side_drain(gen):
        while gen in side:
            side_step()

    def later(gen, first=False):
        side.appendleft(gen) if first else side.append(gen)
        return gen

    w_in1, w_in2 = a["w_in"][0], a["w_in_2"][0]
    wg2 = a["w_gate_2"][0]
    wbr = [a["w_branch"][0, n] for n in range(3)]
    plan = []

    def planned(w, nk, c0, n=512):
        plan.append((w, nk, c0, n))

    def plan_gates(gate, g0, cols):
        for c in cols:
            planned(gate, 16, g0 + 512 * c)

    def plan_branch(gate, g0, w, nk, first=0):
        plan_gates(gate, g0, range(first, 4))
        for c in range(4):
            planned(w, nk, 512 * c)

    def plan_mlp(wi, wo):
        for j in range(9):
            if j < 8:
                for b in range(2):
                    planned(wi, 16, 1024 * j + 512 * b)
            if j > 0:
                for c in range(4):
                    planned(wo[1024 * (j - 1):1024 * j, :], 8, 512 * c)

    GATE0 = 6144
    for c in (4, 5, 2, 3, 0, 1):
        planned(w_in1, 16, 512 * c)
    plan_branch(w_in1, GATE0, wbr[0], 8)
    plan_gates(w_in1, GATE0 + D, range(EARLY))
    for c in range(6, 12):
        planned(w_in1, 16, 512 * c)
    for c in range(2):
        planned(a["s5_w_glu"][0], 8, 512 * c)
    plan_branch(w_in1, GATE0 + 2 * D, wbr[2], 8)
    plan_branch(w_in1, GATE0 + D, wbr[1], 8, EARLY)
    for c in range(4):
        planned(a["w_out"][0], 16, 512 * c)
    plan_mlp(a["w_mlp_in"][0], a["w_mlp_out"][0])
    ZC0 = 2048
    for c in range(3):
        planned(w_in2, 16, 512 * c)
    for c in range(5):
        planned(w_in2, 16, ZC0 + 512 * c, 512 if c < 4 else 256)
    planned(w_in2, 16, 1536)
    plan_branch(wg2, D, a["w_b_out_2"][0], 4)
    plan_branch(wg2, 2 * D, a["w_c_out_2"][0], 6)
    plan_branch(wg2, 0, a["w_a_out_2"][0], 6)
    for c in range(4):
        planned(a["w_o_2"][0], 16, 512 * c)
    plan_mlp(a["w_up_2"][0], a["w_down_2"][0])

    units = [(w, 2 * i, c0, n) for w, nk, c0, n in plan for i in range(nk // 2)]
    landed, split, used = {}, {}, {}
    sent, cut = [0], [0]

    def send(upto_u):
        while sent[0] < min(upto_u, len(units)):
            u = sent[0]
            w, k, c0, n = units[u]
            src = w[k * P:(k + 2) * P, c0:c0 + n].rearrange("(t p) n -> p t n", p=P)
            if waiting:
                S.items.append(waiting.popleft())
                unissued.popleft()
            landed[u] = dma(f"raw{u % NRAW}", RAW[u % NRAW][:, :, 0:n], src, split.get(u - NRAW))
            sent[0] += 1

    def cut_units(upto_u):
        while cut[0] < min(upto_u, len(units)):
            u = cut[0]
            send(u + 1)
            n = units[u][3]
            r, h, l = (b[:, :, 0:n] for b in (RAW[u % NRAW], WH[u % NSPL], WL[u % NSPL]))
            ev = A(lambda e, h=h, r=r: e.activation(h, r, ACT.Copy), landed[u], used.get(u - NSPL))
            split[u] = V(lambda e, l=l, r=r, h=h: e.tensor_tensor(l, r, h, ALU.subtract),
                         ev, used.get(u - NSPL))
            cut[0] += 1
            send(u + 1 + NRAW)

    acc_free = [[], []]
    at = {"unit": 0, "block": 0}

    deferred = []

    def take_deferred():
        for _ in range(len(deferred)):
            deferred.pop(0)()

    lanes = []

    def lane_step(lane):
        try:
            next(lane[0])
        except StopIteration:
            lanes.remove(lane)

    def lane(gen, pace):
        lanes.append([gen, pace, 0])
        return lanes[-1]

    def lanes_drain():
        while lanes:
            lane_step(lanes[0])

    def product(w, nk, c0, xh, xl, ready, n=512):
        s = at["block"] % 2
        pw, pk, pc, pn = plan[at["block"]]
        assert (pk, pc, pn) == (nk, c0, n) and pw.tensor.name == w.tensor.name
        at["block"] += 1
        ev = None
        for i in range(nk // 2):
            u = at["unit"]
            at["unit"] += 1
            cut_units(u + NSPL - 1)
            h, l = WH[u % NSPL], WL[u % NSPL]

            def mm(e, i=i, h=h, l=l):
                for half in range(2):
                    for t in range(2):
                        k = 2 * i + t
                        xs = slice(half * P, half * P + P)
                        for m, (p, q) in enumerate(((xh, h), (xh, l), (xl, h))):
                            ins = e.matmul(ACC[:, 2 * s + half, 0:n], p[:, k, xs], q[:, t, 0:n],
                                           start=(k == 0 and m == 0), stop=(k == nk - 1 and m == 2))
                return ins

            if i >= min(DEFER, nk // 2 - 1) or ready is not None:
                take_deferred()
            while ready is not None and len(ready) <= i:
                assert side
                side_step()
            ev = used[u] = T(mm, split[u], ready[i] if ready else None, acc_free[s] if i == 0 else None)
            side_step()
            for x in list(lanes):
                x[2] += x[1]
                while x[2] >= 1 and x in lanes:
                    x[2] -= 1
                    lane_step(x)
        return s, ev

    def turning(evs, src, kts, yh, yl, *waits, free=None, gain=None, wait=0):
        for _ in range(wait):
            yield
        for k in range(0, kts, 2):
            b, t, bf = bank()

            def tr(e, k=k, t=t):
                for m in range(2):
                    for half in range(2):
                        ins = e.transpose(t[:, m * L + half * P:m * L + half * P + P], src(k + m, half), IDENT)
                return ins

            ev = T(tr, bf, *waits)
            tv = t[:, :].rearrange("p (m t) -> p m t", m=2)
            if gain is None:
                e1 = A(lambda e, k=k, tv=tv: e.activation(yh[:, k:k + 2, :], tv, ACT.Copy), ev, free)
                e2 = V(lambda e, k=k, tv=tv: e.tensor_tensor(yl[:, k:k + 2, :], tv, yh[:, k:k + 2, :], ALU.subtract),
                       e1, free)
            else:
                for m in range(2):
                    e1 = A(lambda e, k=k + m, tv=tv[:, m, :]: e.activation(yh[:, k, :], tv, ACT.Copy, scale=gain(k)),
                           ev, free)
                for m in range(2):
                    e2 = V(lambda e, k=k + m, tv=tv[:, m, :]: e.scalar_tensor_tensor(
                        out=yl[:, k, :], in0=tv, scalar=gain(k), in1=yh[:, k, :], op0=ALU.mult, op1=ALU.subtract),
                        e1, free)
            bank_done(b, e2)
            evs.append(e2)
            yield

    def placing(evs, src, n, free, *waits):
        for k in range(0, n, 2):
            e1 = A(lambda e, k=k: e.activation(YAH[:, k:k + 2, :], src[:, k:k + 2, :], ACT.Copy), free, *waits)
            evs.append(V(lambda e, k=k: e.tensor_tensor(YAL[:, k:k + 2, :], src[:, k:k + 2, :], YAH[:, k:k + 2, :],
                                                        ALU.subtract), e1, free))
            yield

    def x_turning(evs, x, gain, blocks, free):
        for c in range(4):
            yield from turning(evs, lambda k, half, c=c: x[:, half, 512 * c + k * P:512 * c + k * P + P], 4,
                               XTH[:, 4 * c:4 * c + 4, :], XTL[:, 4 * c:4 * c + 4, :], blocks[c], free=free,
                               gain=lambda k, c=c: gain[:, 4 * c + k:4 * c + k + 1])

    def begin(gen, steps):
        for _ in range(steps):
            next(gen)
        return later(gen, first=True)

    jk = [None]

    def squares(x, ss, c, ev):
        for half in range(2):
            jk[0] = A(lambda e, half=half: e.activation(JK[:, :], x[:, half, 512 * c:512 * c + 512], ACT.Square,
                                                        accum_out=ss[:, half, c:c + 1]), ev, jk[0])
        return jk[0]

    def sum_stat(n):
        return stat(2 * n).rearrange("p (h c) -> p h c", h=2)

    def root(ss, width, ev):
        tot, rs = stat(2), stat(2)
        ev = V(lambda e: e.tensor_reduce(tot, ss, mybir.AxisListType.X, ALU.add), ev)
        return rs, finish_rms(tot, rs, width, ev)

    def finish_rms(ss, rs, width, *waits):
        ev = V(lambda e: e.tensor_scalar(ss, ss, 1.0 / width, EPS, ALU.mult, ALU.add), *waits)
        ev = A(lambda e: e.activation(ss, ss, ACT.Sqrt), ev)
        return V(lambda e: e.reciprocal(rs, ss), ev)

    gb_used = [0]
    gb_free = [None, None]

    def gates(gate, g0, bias, rs, SG, sg_ready, cols, es=None):
        es, start = [] if es is None else es, []
        for c in cols:
            i = gb_used[0] % 2
            gb_used[0] += 1
            eb = dma(f"gb{i}", GB[i][:, :], row(bias[512 * c:512 * c + 512], 512), gb_free[i])
            s, ev = product(gate, 16, g0 + 512 * c, XTH, XTL, None)

            def result(c=c, s=s, i=i, ev=ev, eb=eb):
                if c == cols[0]:
                    start.append(sg_ready())
                sg = SG[:, :, 512 * c:512 * c + 512]
                for half in range(2):
                    e1 = V(lambda e, half=half: e.scalar_tensor_tensor(
                        out=sg[:, half, :], in0=ACC[:, 2 * s + half, :], scalar=rs[0][:, half:half + 1], in1=GB[i][:, :],
                        op0=ALU.mult, op1=ALU.add), ev, eb, rs[1], start)
                acc_free[s] = [e1]
                gb_free[i] = e1
                deferred.append(lambda: es.append(A(lambda e: e.activation(sg, sg, ACT.Sigmoid), e1)))

            deferred.append(result)
        return es, ev

    def branch(es, w, nk, yready, merged, SG, first, mfree, last=None, add=None):
        res, mf = [], []
        for c in range(4):
            s, ev = product(w, nk, 512 * c, YAH, YAL, yready() if c == 0 else None)

            def result(c=c, s=s, ev=ev):
                if c == 0:
                    mf.append(mfree() if callable(mfree) else mfree)
                sg = SG[:, :, 512 * c:512 * c + 512]
                m = merged[:, :, 512 * c:512 * c + 512]
                av = ACC[:, 2 * s:2 * s + 2, :]
                if first:
                    e1 = V(lambda e: e.tensor_tensor(m, av, sg, ALU.mult), ev, es[c], mf)
                    acc_free[s] = [e1]
                else:
                    e0 = V(lambda e: e.tensor_tensor(sg, av, sg, ALU.mult), ev, es[c])
                    acc_free[s] = [e0]
                    e1 = (add or G)(lambda e: e.tensor_tensor(m, m, sg, ALU.add), e0, mf)
                res.append(e1)
                if last:
                    last(c, e1)

            deferred.append(result)
        return res, ev

    def residual_product(w, x, ready, xready, ss):
        evs = []
        for c in range(4):
            s, ev = product(w, 16, 512 * c, XTH, XTL, ready if c == 0 else None)
            xv = x[:, :, 512 * c:512 * c + 512]
            e1 = V(lambda e, s=s, xv=xv: e.tensor_tensor(xv, xv, ACC[:, 2 * s:2 * s + 2, :], ALU.add),
                   ev, xready() if callable(xready) else xready)
            acc_free[s] = [e1]
            evs.append(e1)
            if c < 3:
                squares(x, ss, c, e1)
        return evs, ev

    def mlp(tag, wi, wo, x, ready, rs, xready, done):
        with ExitStack() as sc:
            fence = everything()
            YBH, YBL = sb("YBH" + tag, [P, 8, L], F32R, sc), sb("YBL" + tag, [P, 8, L], F32R, sc)
            HB = [sb(f"HB{i}" + tag, [P, 2, 512], F32, sc) for i in range(2)]
            hb_free = [fence, fence]
            Y = [(YAH, YAL), (YBH, YBL)]
            y_free = [fence, fence]
            hready, gens = {}, {}

            def hidden(j, b, e2):
                yh, yl = Y[j % 2]
                yield from turning(hready[j], lambda k, half: HB[b][:, half, k * P:k * P + P], 4,
                                   yh[:, 4 * b:4 * b + 4, :], yl[:, 4 * b:4 * b + 4, :], e2, free=y_free[j % 2], wait=1)
                hb_free[b] = T.now()

            for j in range(9):
                if j < 8:
                    hready[j] = []
                    for b in range(2):
                        s, ev = product(wi, 16, 1024 * j + 512 * b, XTH, XTL, ready if j + b == 0 else None)
                        if (j - 1, b) in gens:
                            side_drain(gens[j - 1, b])
                        hb = HB[b]
                        for half in range(2):
                            e1 = A(lambda e, s=s, hb=hb, half=half: e.activation(
                                hb[:, half, :], ACC[:, 2 * s + half, :], ACT.Relu, scale=rs[0][:, half:half + 1]),
                                ev, hb_free[b], rs[1])
                        acc_free[s] = [e1]
                        e2 = A(lambda e, hb=hb: e.activation(hb[:, :, :], hb[:, :, :], ACT.Square), e1)
                        gens[j, b] = later(hidden(j, b, e2))
                    xlast = ev
                if j > 0:
                    wj = wo[1024 * (j - 1):1024 * j, :]
                    yh, yl = Y[(j - 1) % 2]
                    for c in range(4):
                        s, ev = product(wj, 8, 512 * c, yh, yl, hready[j - 1] if c == 0 else None)
                        xv = x[:, :, 512 * c:512 * c + 512]
                        e1 = V(lambda e, s=s, xv=xv: e.tensor_tensor(xv, xv, ACC[:, 2 * s:2 * s + 2, :], ALU.add),
                               ev, xready)
                        acc_free[s] = [e1]
                        if j == 8:
                            done(c, e1, xlast)
                    y_free[(j - 1) % 2] = ev

    x0 = a["x"][0].rearrange("(h p) n -> p h n", p=P)

    one = ExitStack()
    UT = sb("UT", [P, 8, L], to=one)
    GR = sb("GR", [P, 4096], to=one)
    s5 = ExitStack()
    CT = sb("CT", [P, 2, 1024], to=s5)
    SS = sb("SS", [P, 2, 16, L], to=s5)
    AP = sb("AP", [P, 3, 32, 16], to=s5)
    TMP = sb("TMP", [P, 2, 2, 256], to=s5)
    PR = sb("PR", [P, 24, 32], to=s5)
    VG = GR[:, 0:2048].rearrange("p (a n) -> p a n", a=2)
    WS = GR[:, 2048:3072].rearrange("p (g s) -> p g s", g=8)
    GMG = GR[:, 3072:4096]
    UG1 = sb("UG1", [P, 2, 512], to=s5)
    UG = [GR[:, 3072:4096].rearrange("p (a n) -> p a n", a=2), UG1[:, :, :]]
    SGA = GR[:, :].rearrange("p (a n) -> p a n", a=2)
    pool = SS[:, :, :, :].rearrange("p a j t -> p (a j t)")
    XS = pool[:, 0:4096].rearrange("p (a n) -> p a n", a=2)
    XST = pool[:, 4096:8192].rearrange("p (k t) -> p k t", k=16)
    BT = X[:, 0, :].rearrange("p (a q s) -> p a q s", a=2, q=8)
    XIN = X[:, 1, :].rearrange("p (a n) -> p a n", a=2)

    ld_vec = dma("vec", VEC[:, :], a["vecs"])
    ld_xt = [dma_later(f"xt{k}", [(XST[:, 2 * k:2 * k + 2, :],
                                   a["x_t"][2 * P * k:2 * P * (k + 1), :].rearrange("(k p) t -> p k t", p=P))])[0]
             for k in range(8)]
    ld_s = dma_later("s5p", [(PR[:, 0:3, :], a["s5_p"])])
    ld_x0 = [dma_later(f"x{k}", [(XS[:, :, 256 * k:256 * k + 256], x0[:, :, 256 * k:256 * k + 256])])[0] for k in range(8)]
    ld_c = dma_later("cst", [(CST[:, :], a["cst"])])
    ld_bt = dma_later("s5b", [(X[:, 0, 512 * k:512 * k + 512], a["s5_bt"][:, 512 * k:512 * k + 512]) for k in range(4)])
    ld_gmg = dma_later("gmg", [(GMG, row(a["gm_norm_g"][0], 1024))])
    ld_gw = dma_later("gw", [(WS[:, 4 * k:4 * k + 4, :], a["gm_wt"][:, 4 * k:4 * k + 4, :]) for k in range(2)])
    ld_cc = dma_later("s5c", [(CT[:, k, :], a["s5_ct"][:, k, :]) for k in range(2)])
    ld_dw = dma_later("dw", [(DWT[:, :, :], a["taps"])])
    send(NRAW)

    V_N1, V_N2, V_MIX, V_MLP, V_GB, V_LG, V_LB, V_DB, V_PS, V_FIN, V_SD = 0, 16, 32, 48, 64, 72, 78, 84, 90, 94, 110

    def x_split(evs):
        for k in range(16):
            g = VEC[:, V_N1 + k:V_N1 + k + 1]
            e1 = A(lambda e, k=k, g=g: e.activation(XTH[:, k, :], XST[:, k, :], ACT.Copy, scale=g), ld_xt[k // 2], ld_vec)
            e1 = V(lambda e, k=k, g=g: e.scalar_tensor_tensor(out=XTL[:, k, :], in0=XST[:, k, :], scalar=g,
                                                              in1=XTH[:, k, :], op0=ALU.mult, op1=ALU.subtract), e1)
            if k % 2:
                evs.append(e1)
                yield

    ready, ss0 = [], sum_stat(4)
    begin(x_split(ready), 1)
    gain_x2 = stat(16)
    rs0 = []

    def x_norm():
        for c in range(4):
            while not issued(ld_x0[2 * c:2 * c + 2]):
                yield
            ev = squares(XS, ss0, c, ld_x0[2 * c:2 * c + 2])
            yield
        rs0.extend(root(ss0, D, ev))

    pv = {}

    def pr(i):
        return PR[:, i, :]

    def vtt(o, x, y, op, *w):
        return V(lambda e: e.tensor_tensor(o, x, y, op), *w)

    def vts(o, x, s1, s2, o1, o2, *w):
        return V(lambda e: e.tensor_scalar(o, x, s1, s2, o1, o2), *w)

    def vstt(o, x, s, y, o1, o2, *w):
        return V(lambda e: e.scalar_tensor_tensor(out=o, in0=x, scalar=s, in1=y, op0=o1, op1=o2), *w)

    def s5_parameters():
        while not issued(ld_s):
            yield
        ev = A(lambda e: e.activation(pr(3), pr(2), ACT.Exp), ld_s)
        ev = vtt(pr(4), pr(0), pr(3), ALU.mult, ev, ld_s)
        ev_m = A(lambda e: e.activation(pr(5), pr(4), ACT.Exp), ev)
        ev = vtt(pr(6), pr(1), pr(3), ALU.mult, ev)
        MAGIC = 12582912.0
        ev = vts(pr(7), pr(6), 1.0 / (2 * np.pi), MAGIC, ALU.mult, ALU.add, ev)
        ev = vts(pr(7), pr(7), MAGIC, None, ALU.subtract, ALU.bypass, ev)
        c1 = 6.28125
        c2 = 0.0019350051879882812
        c3 = 2 * np.pi - c1 - c2
        ev = vstt(pr(8), pr(7), -c1, pr(6), ALU.mult, ALU.add, ev)
        ev = vstt(pr(8), pr(7), -c2, pr(8), ALU.mult, ALU.add, ev)
        ev = vstt(pr(8), pr(7), -c3, pr(8), ALU.mult, ALU.add, ev)
        yield
        ev = vts(pr(8), pr(8), PI_DOWN, -PI_DOWN, ALU.min, ALU.max, ev)
        ev_sn = A(lambda e: e.activation(pr(9), pr(8), ACT.Sin), ev)
        ev = A(lambda e: e.activation(pr(10), pr(8), ACT.Abs), ev)
        ev = vts(pr(10), pr(10), -1.0, float(np.pi / 2), ALU.mult, ALU.add, ev)
        ev = A(lambda e: e.activation(pr(10), pr(10), ACT.Sin), ev)
        ev_are = vtt(AP[:, 0, :, 0], pr(5), pr(10), ALU.mult, ev, ev_m)
        ev_aim = vtt(AP[:, 2, :, 0], pr(5), pr(9), ALU.mult, ev_sn)
        ar, ai = AP[:, 0, :, 0], AP[:, 2, :, 0]
        yield
        e1 = vtt(pr(13), pr(0), pr(0), ALU.mult)
        e2 = vtt(pr(14), pr(1), pr(1), ALU.mult)
        e1 = vtt(pr(13), pr(13), pr(14), ALU.add, e2)
        e1 = V(lambda e: e.reciprocal(pr(14), pr(13)), e1)
        e2 = vts(pr(15), ar, 1.0, None, ALU.subtract, ALU.bypass, ev_are)
        e3 = vtt(pr(16), pr(15), pr(0), ALU.mult, e2)
        e4 = vtt(pr(17), ai, pr(1), ALU.mult, ev_aim)
        e5 = vtt(pr(18), ai, pr(0), ALU.mult, e4)
        e6 = vtt(pr(21), pr(15), pr(1), ALU.mult, e5)
        e3 = vtt(pr(19), pr(16), pr(17), ALU.add, e6)
        e4 = vtt(pr(20), pr(18), pr(21), ALU.subtract, e6)
        e3 = vtt(pr(19), pr(19), pr(14), ALU.mult, e4)
        ev_k = vtt(pr(20), pr(20), pr(14), ALU.mult, e4)

        yield
        pv.update(are=ev_are, aim=ev_aim, k=ev_k)

    def s5_matrices():
        pv["gx"] = vtt(gain_x2, VEC[:, V_FIN:V_FIN + 16], VEC[:, V_MIX:V_MIX + 16], ALU.mult, ld_vec)
        kre = pr(19).unsqueeze(2).to_broadcast([P, 32, 32])
        kim = pr(20).unsqueeze(2).to_broadcast([P, 32, 32])
        cr, ci = (CT[:, i, :].rearrange("p (j c) -> p j c", c=32) for i in range(2))
        z = [pool[:, 1024 * i:1024 * i + 1024].rearrange("p (j c) -> p j c", c=32) for i in range(4)]
        free = [rs0[1], ready]
        u0 = TMP[:, 0, :, :].rearrange("p a n -> p (a n)")
        u1 = TMP[:, 1, :, :].rearrange("p a n -> p (a n)")
        ev = pv["aim"]
        for n in (1, 2, 4, 8):
            re, im = AP[:, 0, :, 0:n], AP[:, 2, :, 0:n]
            mr = AP[:, 0, :, n - 1:n].to_broadcast([P, 32, n])
            mi = AP[:, 2, :, n - 1:n].to_broadcast([P, 32, n])
            yield
            v0 = u0[:, 0:32 * n].rearrange("p (j n) -> p j n", n=n)
            v1 = u1[:, 0:32 * n].rearrange("p (j n) -> p j n", n=n)
            e1 = vtt(v0, re, mr, ALU.mult, ev)
            e1 = vtt(v1, im, mi, ALU.mult, ev)
            e1 = vtt(AP[:, 0, :, n:2 * n], v0, v1, ALU.subtract, e1)
            e2 = vtt(v0, re, mi, ALU.mult, e1)
            e2 = vtt(v1, im, mr, ALU.mult, e1)
            ev = vtt(AP[:, 2, :, n:2 * n], v0, v1, ALU.add, e2)
        ev_ap = vts(AP[:, 1, :, :], AP[:, 2, :, :], -1.0, None, ALU.mult, ALU.bypass, ev)

        while not issued(ld_cc, ld_gw):
            yield
        e1 = G(lambda e: e.tensor_tensor(z[0], cr, kre, ALU.mult), pv["k"], ld_cc, free)
        e1 = G(lambda e: e.tensor_tensor(z[1], ci, kim, ALU.mult), e1)
        e1 = G(lambda e: e.tensor_tensor(z[2], cr, kim, ALU.mult), e1)
        ev_z = G(lambda e: e.tensor_tensor(z[3], ci, kre, ALU.mult), e1)
        pv["ws"] = G(lambda e: e.affine_select(out=WS, in_=WS, compare_op=ALU.is_ge, fill=0.0, base=0,
                                               pattern=[[0, 8], [1, P]], channel_multiplier=-1), ld_gw)
        yield
        for _ in range(3):
            yield
        e1 = vtt(cr, z[0], z[1], ALU.subtract, ev_z)
        ev_c = vstt(ci, z[2], -1.0, z[3], ALU.mult, ALU.subtract, ev_z)
        pv.update(ap=ev_ap, c=ev_c)

    ev_s5 = {}

    def s5_run():
        while not rs0 or "k" not in pv:
            yield
        yield from s5_matrices()
        while "in" not in ev_s5:
            yield
        for k in range(0, 8, 2):
            b, t, bf = bank()

            def tr(e, t=t, k=k):
                for m in range(2):
                    for half in range(2):
                        ins = e.transpose(t[:, m * L + half * P:m * L + half * P + P],
                                          XIN[:, half, (k + m) * P:(k + m) * P + P], IDENT)
                return ins

            ev = T(tr, bf, ev_s5["in"], ld_c)
            ev_u = A(lambda e, t=t, k=k: e.activation(UT[:, k:k + 2, :], t[:, :].rearrange("p (m t) -> p m t", m=2),
                                                      ACT.Copy), ev)
            bank_done(b, ev_u)
        yield
        s5_lanes.append(lane(s5_scan(V, 0, (0, 16), ev_u), PACE_V))
        s5_lanes.append(lane(s5_scan(G, 8, (8, 24), ev_u), PACE_G))

    s5_lanes, s5_read, s5_y = [], [], []

    def s5_scan(Q, o, bases, ev_u):
        ev_free = [pv["c"], rs0[1], ready]
        Sv = SS[:, :, o:o + 8, :].rearrange("p a j (c i) -> p a j c i", i=16)
        for base in bases:
            js = slice(base, base + 8)
            for jj in range(8):
                q, i = (base + jj) // 4, jj % 4
                b, t, bf = bank()
                rows = slice(32 * i, 32 * i + 32)

                def mm(e, t=t, q=q, rows=rows):
                    for ri in range(2):
                        ins = e.matmul(t[:, ri * L:ri * L + L], BT[rows, ri, q, :], UT[rows, q, :],
                                       start=True, stop=True)
                    return ins

                ev = T(mm, bf, ld_bt, ev_u)
                ev_bu = A(lambda e, t=t, jj=jj: e.activation(
                    SS[:, :, o + jj, :], t[:, :].rearrange("p (a t) -> p a t", a=2), ACT.Copy), ev, ev_free)
                bank_done(b, ev_bu)
                if jj % 2:
                    yield
            if base == bases[-1]:
                s5_read.append(T.now())

            def step(last, dst, src, rr, ii, shape):
                n = 8 * (shape[2] if len(shape) == 3 else 1)
                tv = []
                for z in range(2):
                    f = TMP[:, z, :, 16 * o:16 * o + n]
                    tv.append(f if len(shape) == 2 else f.rearrange("p a (j c) -> p a j c", c=shape[2]))
                w = [last, ev_bu, pv["ap"]]
                Q(lambda e: e.tensor_tensor(tv[0], src, rr, ALU.mult), w)
                e1 = Q(lambda e: e.tensor_tensor(tv[1], src[:, ::-1], ii, ALU.mult), w)
                e1 = Q(lambda e: e.tensor_tensor(dst, dst, tv[0], ALU.add), e1)
                return Q(lambda e: e.tensor_tensor(dst, dst, tv[1], ALU.add), e1)

            def coef(p, n):
                if n is None:
                    return AP[:, 0, js, p].unsqueeze(1).to_broadcast([P, 2, 8]), AP[:, 1:3, js, p]
                return (AP[:, 0, js, p].unsqueeze(1).unsqueeze(3).to_broadcast([P, 2, 8, n]),
                        AP[:, 1:3, js, p].unsqueeze(3).to_broadcast([P, 2, 8, n]))

            last = None
            rr, ii = coef(0, 16)
            for i in range(1, 16):
                last = step(last, Sv[:, :, :, :, i], Sv[:, :, :, :, i - 1], rr, ii, (2, 8, 16))
                yield
            rr, ii = coef(15, None)
            for c in range(1, 16):
                last = step(last, Sv[:, :, :, c, 15], Sv[:, :, :, c - 1, 15], rr, ii, (2, 8))
                if c % 3 == 0:
                    yield
            for i in range(15):
                rr, ii = coef(i, 15)
                last = step(last, Sv[:, :, :, 1:16, i], Sv[:, :, :, 0:15, 15], rr, ii, (2, 8, 15))
                yield
            b, t, bf = bank()

            def mm(e, t=t, base=base):
                for m in range(2):
                    for i in range(4):
                        j = 4 * m + i
                        for ri in range(2):
                            ins = e.matmul(t[32 * i:32 * i + 32, m * L:m * L + L],
                                           CT[:, ri, 32 * (base + j):32 * (base + j) + 32],
                                           SS[:, ri, o + j, :], start=(ri == 0), stop=(ri == 1))
                return ins

            ev = T(mm, bf, last, pv["c"])
            for m in range(2):
                q = base // 4 + m
                ev_y = vstt(UT[:, q, :], UT[:, q, :], VEC[:, V_SD + q:V_SD + q + 1], t[:, m * L:m * L + L],
                            ALU.mult, ALU.add, ev)
            bank_done(b, ev_y)
            ev_free = ev
            yield
        s5_y.append(ev_y)

    later(s5_parameters())
    later(x_norm())

    def s5_input(c, s, ev):
        while not rs0:
            yield
        for half in range(2):
            e1 = A(lambda e, half=half: e.activation(XIN[:, half, 512 * c:512 * c + 512], ACC[:, 2 * s + half, :], ACT.Copy,
                                                     scale=rs0[0][:, half:half + 1]), ev, rs0[1])
        acc_free[s] = [e1]
        ev_s5[c] = e1

    for c in range(2):
        s, ev = product(w_in1, 16, 512 * (4 + c), XTH, XTL, ready if c == 0 else None)
        if c == 0:
            in_gen = later(s5_input(c, s, ev))
            lane(s5_run(), 1)
        else:
            side_drain(in_gen)
            for _ in s5_input(c, s, ev):
                pass
    ev_s5["in"] = ev_s5[1]

    ssv = sum_stat(2)
    for c in range(2):
        s, ev = product(w_in1, 16, 512 * (2 + c), XTH, XTL, None)
        for half in range(2):
            e1 = A(lambda e, s=s, c=c, half=half: e.activation(
                VG[:, half, 512 * c:512 * c + 512], ACC[:, 2 * s + half, :], ACT.Gelu_apprx_tanh,
                scale=rs0[0][:, half:half + 1]), ev, rs0[1])
        acc_free[s] = [e1]
        esq = squares(VG, ssv, c, e1)
    vn = []

    def v_norm():
        tot, rs = stat(2), stat(2)
        yield
        ev = V(lambda e: e.tensor_reduce(tot, ssv, mybir.AxisListType.X, ALU.add), esq)
        ev = vts(tot, tot, 1.0 / 1024, EPS, ALU.mult, ALU.add, ev)
        ev = A(lambda e: e.activation(tot, tot, ACT.Sqrt), ev)
        yield
        ev = V(lambda e: e.reciprocal(rs, tot), ev)
        for half in range(2):
            e1 = vstt(VG[:, half, :], VG[:, half, :], rs[:, half:half + 1], GMG, ALU.mult, ALU.mult, ev, ld_gmg)
            yield
        vn.append(e1)

    vn_gen = later(v_norm(), first=True)
    ya = []

    def gmlp(c, ev_ug):
        yield
        for half in range(2):
            b, t, bf = bank()

            def mm(e, t=t, half=half):
                for g in range(4):
                    ins = e.matmul(t[:, g * P:g * P + P], WS[:, 4 * c + g, :],
                                   VG[:, half, (4 * c + g) * P:(4 * c + g) * P + P], start=True, stop=True)
                return ins

            ev = T(mm, bf, vn, pv["ws"])
            for g in range(4):
                ug = UG[c][:, half, g * P:g * P + P]
                e1 = vstt(ug, t[:, g * P:g * P + P], VEC[:, V_GB + 4 * c + g:V_GB + 4 * c + g + 1], ug,
                          ALU.add, ALU.mult, ev, ev_ug)
            bank_done(b, e1)
            yield
        yield from turning(ya, lambda k, half: UG[c][:, half, k * P:k * P + P], 4, YAH[:, 4 * c:4 * c + 4, :],
                           YAL[:, 4 * c:4 * c + 4, :], e1, wait=1)

    gm_gens = []
    for c in range(2):
        s, ev = product(w_in1, 16, 512 * c, XTH, XTL, None)
        side_drain(vn_gen)
        for half in range(2):
            e1 = A(lambda e, s=s, c=c, half=half: e.activation(
                UG[c][:, half, :], ACC[:, 2 * s + half, :], ACT.Gelu_apprx_tanh, scale=rs0[0][:, half:half + 1]), ev, vn)
        acc_free[s] = [e1]
        gm_gens.append(later(gmlp(c, e1), first=True))

    bg1 = a["b_gate"][0]

    def gmlp_done():
        for g in reversed(gm_gens):
            while g in side:
                side_step()
        return [T.now(), A.now(), V.now()]

    def merged_free():
        while len(s5_read) < 2:
            for x in list(lanes):
                lane_step(x)
        for x in s5_lanes:
            x[1] = PACE_2
        return s5_read

    es, _ = gates(w_in1, GATE0, bg1[0], rs0, SGA, gmlp_done, range(4))
    res, ev_ya = branch(es, wbr[0], 8, lambda: ya, X, SGA, True, merged_free)
    esb, _ = gates(w_in1, GATE0 + D, bg1[1], rs0, SGA, lambda: res, range(EARLY))
    s, ev = product(w_in1, 16, 512 * 6, XTH, XTL, None)
    lanes_drain()
    ev_s5["y"] = A(lambda e: e.activation(UT[:, :, :], UT[:, :, :], ACT.Gelu_apprx_tanh), s5_y)
    fence = everything()
    s5.close()

    QKV = sb("QKV", [P, 2, 3072], to=one)
    QT = sb("QT", [P, 8, L], to=one)
    KT = sb("KT", [P, 8, L], to=one)
    SG = sb("SG", [P, 2, D], to=one)
    BGL = sb("BGL", [P, 1024], to=one)
    ld_bgl = dma("bgl", BGL[:, :], row(a["s5_b_glu"][0], 1024), fence)
    gt = []
    gt_gen = later(placing(gt, UT, 8, ev_ya, ev_s5["y"]))
    for c in range(6):
        if c > 0:
            s, ev = product(w_in1, 16, 512 * (6 + c), XTH, XTL, None)
        for half in range(2):
            e1 = A(lambda e, s=s, c=c, half=half: e.activation(
                QKV[:, half, 512 * c:512 * c + 512], ACC[:, 2 * s + half, :], ACT.Copy, scale=rs0[0][:, half:half + 1]),
                ev, fence)
        acc_free[s] = [e1]
    side_drain(gt_gen)
    ev_qkv = e1

    ev_at = {}
    HW = 384
    ZSb, SPb = QKV[:, 0, 0:4 * HW], QKV[:, 1, 0:4 * HW]

    def attention():
        for src, dst in ((0, QT), (1024, KT)):
            for h in range(0, 8, 2):
                b, t, bf = bank()

                def tr(e, t=t, src=src, h=h):
                    for m in range(2):
                        for half in range(2):
                            ins = e.transpose(t[:, m * L + half * P:m * L + half * P + P],
                                              QKV[:, half, src + (h + m) * P:src + (h + m) * P + P], IDENT)
                    return ins

                ev = T(tr, bf, ev_qkv)
                ev_t = A(lambda e, t=t, dst=dst, h=h: e.activation(
                    dst[:, h:h + 2, :], t[:, :].rearrange("p (m t) -> p m t", m=2), ACT.Copy), ev, fence)
                bank_done(b, ev_t)
                yield
        free = [ev]
        for hg in range(2):
            for hh in range(4):
                h = 4 * hg + hh
                b, t, bf = bank()

                def mm(e, t=t, h=h):
                    e.matmul(t[:, 0:L], KT[:, h, 0:P], QT[:, h, :], start=True, stop=True)
                    return e.matmul(t[:, L:HW], KT[:, h, P:L], QT[:, h, P:L], start=True, stop=True)

                ev = T(mm, bf, ev_t)
                ev_z = A(lambda e, t=t, hh=hh: e.activation(ZSb[:, hh * HW:hh * HW + HW], t[:, 0:HW], ACT.Copy,
                                                            scale=128.0 ** -0.5), ev, free)
                bank_done(b, ev_z)
            yield
            e1 = A(lambda e: e.activation(SPb, ZSb, ACT.Abs), ev_z, free)
            yield
            e1 = A(lambda e: e.activation(SPb, SPb, ACT.Exp, scale=-1.0), e1)
            e1 = A(lambda e: e.activation(SPb, SPb, ACT.Ln, bias=1.0), e1)
            yield
            e1 = vstt(SPb, ZSb, 0.0, SPb, ALU.max, ALU.add, e1)
            yield
            for buf, fill in ((SPb, 0.0), (ZSb, -1e30)):
                for d in (0, 2):
                    v = buf.rearrange("p (h b c) -> p h b c", h=4, b=3)[:, :, d, :]
                    ev_m = G(lambda e, v=v, fill=fill: e.affine_select(
                        out=v, in_=v, compare_op=ALU.is_gt, fill=fill, base=0, pattern=[[0, 4], [1, P]],
                        channel_multiplier=-1), e1)
            yield
            yield
            for hh in range(4):
                sp = SPb[:, hh * HW:hh * HW + HW]
                b, t, bf = bank()

                def mm(e, t=t, sp=sp):
                    e.matmul(t[:, 0:P], TRI, sp[:, 0:P], start=True, stop=True)
                    e.matmul(t[:, P:L], TRI, sp[:, P:L], start=True, stop=False)
                    e.matmul(t[:, P:L], ONES, sp[:, L:HW], start=False, stop=True)
                    return e.matmul(t[:, L:HW], TRI, sp[:, L:HW], start=True, stop=True)

                ev = T(mm, bf, ev_m)
                zs = ZSb[:, hh * HW:hh * HW + HW]
                e2 = vtt(zs, zs, t[:, 0:HW], ALU.subtract, ev, ev_m)
                bank_done(b, e2)
            yield
            e2 = A(lambda e: e.activation(ZSb, ZSb, ACT.Exp), e2)
            yield
            for hp in range(2):
                b, t, bf = bank()

                def mm(e, t=t, hp=hp, hg=hg):
                    for m in range(2):
                        hh = 2 * hp + m
                        vc = D + (4 * hg + hh) * P
                        w = ZSb[:, hh * HW:hh * HW + HW]
                        e.matmul(t[:, m * L:m * L + P], QKV[:, 0, vc:vc + P], w[:, 0:P], start=True, stop=True)
                        e.matmul(t[:, m * L + P:m * L + L], QKV[:, 0, vc:vc + P], w[:, P:L], start=True, stop=False)
                        ins = e.matmul(t[:, m * L + P:m * L + L], QKV[:, 1, vc:vc + P], w[:, L:HW],
                                       start=False, stop=True)
                    return ins

                ev = T(mm, bf, e2)
                k = 4 * hg + 2 * hp
                tv = t[:, :].rearrange("p (m t) -> p m t", m=2)
                e3 = A(lambda e, k=k, tv=tv: e.activation(YAH[:, k:k + 2, :], tv, ACT.Copy), ev, ev_at["free"])
                e4 = vtt(YAL[:, k:k + 2, :], tv, YAH[:, k:k + 2, :], ALU.subtract, e3, ev_at["free"])
                bank_done(b, e4)
                ev_at.setdefault("y", []).append(e4)
            free = [ev, e2]
            yield

    at_gen = attention()
    for c in range(2):
        s, ev = product(a["s5_w_glu"][0], 8, 512 * c, YAH, YAL, gt if c == 0 else None)
        sg = SG[:, :, 512 * c:512 * c + 512]
        for half in range(2):
            e1 = vtt(sg[:, half, :], ACC[:, 2 * s + half, :], BGL[:, 512 * c:512 * c + 512], ALU.add, ev, ld_bgl, fence)
        acc_free[s] = [e1]
        ev_sg = A(lambda e, sg=sg: e.activation(sg, sg, ACT.Sigmoid), e1)
    ev_at["free"] = ev
    glu = {}

    def glu_gate():
        yield
        for k in range(0, 8, 2):
            b, t, bf = bank()

            def tr(e, t=t, k=k):
                for m in range(2):
                    for half in range(2):
                        ins = e.transpose(t[:, m * L + half * P:m * L + half * P + P],
                                          SG[:, half, (k + m) * P:(k + m) * P + P], IDENT)
                return ins

            ev = T(tr, bf, ev_sg)
            glu["y"] = vtt(UT[:, k:k + 2, :], UT[:, k:k + 2, :], t[:, :].rearrange("p (m t) -> p m t", m=2), ALU.mult,
                           ev, gt)
            bank_done(b, glu["y"])
            yield
        glu["read"] = T.now()

    glu_gen = later(glu_gate())
    later(at_gen)

    def sg_read():
        side_drain(glu_gen)
        return [glu["read"]]

    def yc_ready():
        side_drain(at_gen)
        return ev_at["y"]

    es, _ = gates(w_in1, GATE0 + 2 * D, bg1[2], rs0, SG, sg_read, range(4))
    res, ev_yc = branch(es, wbr[2], 8, yc_ready, X, SG, False, res)
    yb = []
    yb_gen = later(placing(yb, UT, 8, ev_yc, glu["y"]))

    def yb_ready():
        side_drain(yb_gen)
        return yb

    mready = []

    def merged_turner(src, out, gates_done):
        def go(c, ev):
            later(turning(out, lambda k, half: src[:, half, 512 * c + k * P:512 * c + k * P + P], 4,
                          XTH[:, 4 * c:4 * c + 4, :], XTL[:, 4 * c:4 * c + 4, :], ev, free=gates_done, wait=1))
        return go

    _, ev = gates(w_in1, GATE0 + D, bg1[1], rs0, SGA, lambda: None, range(EARLY, 4), es=esb)
    branch(esb, wbr[1], 8, yb_ready, X, SGA, False, res, last=merged_turner(X, mready, ev), add=V)
    while deferred:
        take_deferred()
    fence = everything()
    one.close()

    def x_again():
        while len(mready) < 8:
            yield
        ld_x.append(dma("x", X[:, :, :], x0, T.now()))

    ld_x = []
    later(x_again())
    ss1 = sum_stat(4)

    def x_loaded():
        while not ld_x:
            side_step()
        return ld_x

    xr, ev_xt = residual_product(a["w_out"][0], X, mready, x_loaded, ss1)

    ready, ready2 = [], []
    begin(x_turning(ready, X, VEC[:, V_N2:V_N2 + 16], xr, ev_xt), 4)
    rs1 = root(ss1, D, squares(X, ss1, 3, xr[3]))
    ss2, ss3 = sum_stat(4), sum_stat(4)
    x1 = []

    def mlp1_done(c, ev, xt_free):
        x1.append(ev)
        sq2.append(squares(X, ss2, c, ev))
        later(turning(ready2, lambda k, half: X[:, half, 512 * c + k * P:512 * c + k * P + P], 4,
                      XTH[:, 4 * c:4 * c + 4, :], XTL[:, 4 * c:4 * c + 4, :], ev, pv["gx"], free=xt_free, wait=1,
                      gain=lambda k: gain_x2[:, 4 * c + k:4 * c + k + 1]))

    sq2 = []
    mlp("1", a["w_mlp_in"][0], a["w_mlp_out"][0], X, ready, rs1, xr, mlp1_done)
    rs2 = root(ss2, D, sq2[-1])
    ready = ready2

    two = ExitStack()
    fence = everything()
    MG = sb("MG", [P, 2, D], to=two)
    ZA = MG[:, :, :].rearrange("p a n -> p (a n)")[:, 0:3072].rearrange("p (a n) -> p a n", a=2)
    ZB = MG[:, :, :].rearrange("p a n -> p (a n)")[:, 3072:4096].rearrange("p (a n) -> p a n", a=2)
    ZCb = sb("ZCb", [P, 2 * 2304], to=two)
    ZC = ZCb[:, :].rearrange("p (a n) -> p a n", a=2)
    SG2 = ZCb[:, 0:2 * D].rearrange("p (a n) -> p a n", a=2)
    UA = sb("UA", [P, 6, 30 + L], to=two)
    CA = sb("CA", [P, 6, L], to=two)
    VT = sb("VT", [P, 2, 768], to=two)
    PC = sb("PC", [P, 6, 2 + L], to=two)
    GBT = sb("GBT", [P, 6, L], to=two)
    PM = sb("PM", [P, 4, 2, L], to=two)
    PT = sb("PT", [P, 4, L], to=two)
    WG = sb("WG", [P, 4, P], to=two)
    BG = VT[:, :, :].rearrange("p a n -> p (a n)")
    FG = ZCb[:, 0:D]
    ld_fg = dma("fg", FG, row(a["final_g"], D), fence)
    ld_bg = dma("bglu2", BG, row(a["b_glu_2"][0], 1536), fence)
    ld_pm = dma("pm", PM[:, :, :, :], a["pmat"], fence)
    ld_wg = dma("wgrp", WG[:, :, :], a["w_pool_grp_2"][0].rearrange("g c d -> c g d"), fence)
    ev_pad = G(lambda e: e.memset(UA[:, :, 0:30], 0.0), fence)
    ev_pad = G(lambda e: e.memset(PC[:, :, 0:2], 0.0), fence)

    x2 = {}

    def close_block1():
        while len(ready) < 8:
            yield
        read = T.now()
        for half in range(2):
            ev = vstt(X[:, half, :], X[:, half, :], rs2[0][:, half:half + 1], FG, ALU.mult, ALU.mult, rs2[1], ld_fg, read)
        x2["fg"] = ev
        yield
        for c in range(4):
            e1 = squares(X, ss3, c, ev)
            yield
        r3, e1 = root(ss3, D, e1)
        r23 = stat(2)
        x2["rs"] = (r23, vtt(r23, r3, rs2[0], ALU.mult, e1))

    x2_gen = later(close_block1())
    for c in range(3):
        s, ev = product(w_in2, 16, 512 * c, XTH, XTL, ready if c == 0 else None)
        if c == 0:
            side_drain(x2_gen)
            rsb, xr = x2["rs"], x2["fg"]
        for half in range(2):
            e1 = vstt(ZA[:, half, 512 * c:512 * c + 512], ACC[:, 2 * s + half, :], rsb[0][:, half:half + 1],
                      BG[:, 512 * c:512 * c + 512], ALU.mult, ALU.add, ev, ld_bg, fence, rsb[1])
        acc_free[s] = [e1]
    bg_read = e1
    e1 = A(lambda e: e.activation(ZA[:, :, 768:1536], ZA[:, :, 768:1536], ACT.Sigmoid), e1)
    ev_ua = G(lambda e: e.tensor_tensor(ZA[:, :, 0:768], ZA[:, :, 0:768], ZA[:, :, 768:1536], ALU.mult), e1)

    def plain_turn(src, k0, n, dst, *waits):
        b, t, bf = bank()

        def tr(e):
            for m in range(n):
                for half in range(2):
                    ins = e.transpose(t[:, m * L + half * P:m * L + half * P + P], src(k0 + m, half), IDENT)
            return ins

        ev = T(tr, bf, *waits)
        ev = A(lambda e: e.activation(dst, t[:, 0:n * L].rearrange("p (m t) -> p m t", m=n), ACT.Copy), ev, fence)
        bank_done(b, ev)
        return ev

    ya2 = []
    va = {}

    def conv_a():
        yield
        yield
        for k in range(0, 6, 2):
            ev_t = plain_turn(lambda k, half: ZA[:, half, k * P:k * P + P], k, 2, UA[:, k:k + 2, 30:30 + L], ev_ua)
            yield
        va["za_read"] = T.now()
        prev = [None] * 6
        for k in range(31):
            for c in range(6):
                tap = DWT[:, c, k:k + 1]
                if k == 0:
                    prev[c] = vts(CA[:, c, :], UA[:, c, 0:L], tap, VEC[:, V_DB + c:V_DB + c + 1], ALU.mult, ALU.add,
                                  ev_t, ev_pad, fence, ld_dw)
                else:
                    prev[c] = vstt(CA[:, c, :], UA[:, c, k:k + L], tap, CA[:, c, :], ALU.mult, ALU.add, prev[c])
                if c in (1, 3):
                    yield
            yield
        yield
        for half in range(2):
            for c0, n in ((0, 4), (4, 2)):
                b, t, bf = bank()

                def tr(e, t=t, c0=c0, n=n, half=half):
                    for m in range(n):
                        ins = e.transpose(t[:, m * P:m * P + P], CA[:, c0 + m, half * P:half * P + P], IDENT)
                    return ins

                ev = T(tr, bf, prev)
                e1 = A(lambda e, t=t, c0=c0, n=n, half=half: e.activation(
                    VT[:, half, c0 * P:(c0 + n) * P], t[:, 0:n * P], ACT.Copy), ev, bg_read)
                bank_done(b, e1)
            yield
        e1 = [e1]
        yield
        for half in range(2):
            bs, mv, rs = stat(12), stat(2), stat(1)
            for q in range(2):
                e2 = V(lambda e, half=half, q=q, bs=bs: e.bn_stats(bs[:, 6 * q:6 * q + 6],
                                                                   VT[:, half, 384 * q:384 * q + 384]), e1)
            e2 = V(lambda e, bs=bs, mv=mv: e.bn_aggr(mv, bs.rearrange("p (q s) -> p q s", q=2)), e2)
            e2 = vts(rs, mv[:, 1:2], EPS, None, ALU.add, ALU.bypass, e2)
            e2 = A(lambda e, rs=rs: e.activation(rs, rs, ACT.Sqrt), e2)
            yield
            yield
            e2 = V(lambda e, rs=rs: e.reciprocal(rs, rs), e2)
            ev_ln = vts(VT[:, half, :], VT[:, half, :], mv[:, 0:1], rs, ALU.subtract, ALU.mult, e2)
            yield
        for k in range(0, 6, 2):
            b, t, bf = bank()

            def tr(e, t=t, k=k):
                for m in range(2):
                    for half in range(2):
                        ins = e.transpose(t[:, m * L + half * P:m * L + half * P + P],
                                          VT[:, half, (k + m) * P:(k + m) * P + P], IDENT)
                return ins

            ev = T(tr, bf, ev_ln)
            for m in range(2):
                e1 = vts(CA[:, k + m, :], t[:, m * L:m * L + L], VEC[:, V_LG + k + m:V_LG + k + m + 1],
                         VEC[:, V_LB + k + m:V_LB + k + m + 1], ALU.mult, ALU.add, ev)
            bank_done(b, e1)
            e1 = A(lambda e, k=k: e.activation(UA[:, k:k + 2, 0:L], CA[:, k:k + 2, :], ACT.Sigmoid), e1)
            va["v"] = vtt(CA[:, k:k + 2, :], CA[:, k:k + 2, :], UA[:, k:k + 2, 0:L], ALU.mult, e1)
            yield

    later(conv_a())

    for c in range(5):
        n = 512 if c < 4 else 256
        s, ev = product(w_in2, 16, ZC0 + 512 * c, XTH, XTL, None, n=n)
        for half in range(2):
            e1 = A(lambda e, s=s, c=c, n=n, half=half: e.activation(
                ZC[:, half, 512 * c:512 * c + n], ACC[:, 2 * s + half, 0:n], ACT.Copy, scale=rsb[0][:, half:half + 1]),
                ev, fence, xr)
        acc_free[s] = [e1]
    ev_zc = e1
    ev_p = G(lambda e: e.tensor_tensor(ZC[:, :, 768:1536], ZC[:, :, 768:1536], ZC[:, :, 1536:2304], ALU.mult), ev_zc)
    vc = {}

    def conv_c():
        yield
        yield
        for k in range(0, 6, 2):
            ev_g = plain_turn(lambda k, half: ZC[:, half, k * P:k * P + P], k, 2, GBT[:, k:k + 2, :], ev_zc)
            yield
        for k in range(0, 6, 2):
            ev_t = plain_turn(lambda k, half: ZC[:, half, 768 + k * P:768 + k * P + P], k, 2, PC[:, k:k + 2, 2:2 + L], ev_p)
            yield
        vc["read"] = [T.now(), ev_p]
        prev = [None] * 6
        for tap in range(3):
            for c in range(6):
                w = DWT[:, c, 31 + tap:32 + tap]
                if tap == 0:
                    prev[c] = vts(WGC[:, c, :], PC[:, c, 0:L], w, None, ALU.mult, ALU.bypass, ev_t, ev_pad, fence, ld_dw)
                else:
                    prev[c] = vstt(WGC[:, c, :], PC[:, c, tap:tap + L], w, WGC[:, c, :], ALU.mult, ALU.add, prev[c])
                if c % 3 == 2:
                    yield
        vc["v"] = G(lambda e: e.tensor_tensor(GBT[:, :, :], GBT[:, :, :], WGC[:, :, :], ALU.mult), prev, ev_g)

    WGC = sb("WGC", [P, 6, L], to=two)
    vc_gen = later(conv_c(), first=True)
    s, ev = product(w_in2, 16, 1536, XTH, XTL, None)
    for half in range(2):
        ev_zb = A(lambda e, s=s, half=half: e.activation(ZB[:, half, :], ACC[:, 2 * s + half, :], ACT.Copy,
                                                         scale=rsb[0][:, half:half + 1]), ev, fence)
    acc_free[s] = [ev_zb]
    yb2 = []
    vb = {}

    def pools():
        yield
        for g in range(0, 4, 2):
            b, t, bf = bank()

            def mm(e, t=t, g=g):
                for m in range(2):
                    for half in range(2):
                        ins = e.matmul(t[:, m * L:m * L + L], ZB[:, half, (g + m) * P:(g + m) * P + P],
                                       PM[:, g + m, half, :], start=(half == 0), stop=(half == 1))
                return ins

            ev = T(mm, bf, ev_zb, ld_pm)
            e2 = A(lambda e, t=t, g=g: e.activation(PT[:, g:g + 2, :], t[:, :].rearrange("p (m t) -> p m t", m=2), ACT.Copy),
                   ev, fence)
            bank_done(b, e2)
            yield
        vb["read"] = T.now()
        yield
        for g in range(0, 4, 2):
            b, t, bf = bank()

            def mm(e, t=t, g=g):
                for m in range(2):
                    ins = e.matmul(t[:, m * L:m * L + L], WG[:, g + m, :], PT[:, g + m, :], start=True, stop=True)
                return ins

            ev = T(mm, bf, e2, ld_wg)
            for m in range(2):
                sc_ = VEC[:, V_PS + g + m:V_PS + g + m + 1]
                e3 = A(lambda e, t=t, g=g, m=m, sc_=sc_: e.activation(YAH[:, g + m, :], t[:, m * L:m * L + L], ACT.Copy,
                                                                      scale=sc_), ev, fence)
            for m in range(2):
                sc_ = VEC[:, V_PS + g + m:V_PS + g + m + 1]
                e4 = vstt(YAL[:, g + m, :], t[:, m * L:m * L + L], sc_, YAH[:, g + m, :], ALU.mult, ALU.subtract, e3, fence)
            bank_done(b, e4)
            yb2.append(e4)
            yield

    vb_gen = later(pools(), first=True)

    def sg2_free():
        side_drain(vb_gen)
        while vc_gen in side and "read" not in vc:
            side_step()
        return [vc["read"], ev_zc]

    def mg_free():
        while "za_read" not in va:
            side_step()
        return [va["za_read"], vb["read"]]

    bg2 = a["b_gate_2"][0].rearrange("(n d) -> n d", n=3)
    es, _ = gates(wg2, D, bg2[1], rsb, SG2, sg2_free, range(4))
    res, ev_b = branch(es, a["w_b_out_2"][0], 4, lambda: yb2, MG, SG2, True, mg_free)

    yc2 = []

    def place_c():
        while "v" not in vc:
            yield
        yield from placing(yc2, GBT, 6, ev_b, vc["v"])

    yc2_gen = later(place_c(), first=True)

    def yc2_ready():
        side_drain(vc_gen)
        side_drain(yc2_gen)
        return yc2

    es, _ = gates(wg2, 2 * D, bg2[2], rsb, SG2, lambda: res, range(4))
    res, ev_c2 = branch(es, a["w_c_out_2"][0], 6, yc2_ready, MG, SG2, False, res)

    def place_a():
        yield from placing(ya2, CA, 6, ev_c2, va["v"])

    ya2_gen = later(place_a())

    def ya2_ready():
        side_drain(ya2_gen)
        return ya2

    mready2 = []
    es, ev = gates(wg2, 0, bg2[0], rsb, SG2, lambda: res, range(4))
    branch(es, a["w_a_out_2"][0], 6, ya2_ready, MG, SG2, False, res, last=merged_turner(MG, mready2, ev), add=V)
    ss4 = sum_stat(4)
    xr, ev_xt = residual_product(a["w_o_2"][0], X, mready2, xr, ss4)
    two.close()
    ready, sq5 = [], []
    begin(x_turning(ready, X, VEC[:, V_MLP:V_MLP + 16], xr, ev_xt), 4)
    rs4 = root(ss4, D, squares(X, ss4, 3, xr[3]))
    ss5 = sum_stat(4)
    x5 = {}

    def mlp2_done(c, ev, xt_free):
        sq5.append(squares(X, ss5, c, ev))
        if c < 2:
            times_gain(c, sq5[-1])

    def times_gain(c, *waits):
        for half in range(2):
            cs = slice(512 * c, 512 * c + 512)
            x5[half, c // 2] = vtt(X[:, half, cs], X[:, half, cs], FG2[:, cs], ALU.mult, ld_fg, *waits)

    with ExitStack() as sc:
        FG2 = sb("FG2", [P, D], F32, sc)
        ld_fg = dma("fg2", FG2[:, :], row(a["g_final_2"], D), everything())
        mlp("2", a["w_up_2"][0], a["w_down_2"][0], X, ready, rs4, xr, mlp2_done)
        rs5 = root(ss5, D, sq5[-1])
        o = out[0].rearrange("(h p) n -> h p n", p=P)
        stores = []
        for c in range(2):
            cs = slice(1024 * c, 1024 * c + 1024)
            for half in range(2):
                y, r5 = X[:, half, cs], rs5[0][:, half:half + 1]
                if c == 1:
                    ev = vstt(y, y, r5, FG2[:, cs], ALU.mult, ALU.mult, rs5[1], ld_fg)
                elif half == 0:
                    ev = vts(y, y, r5, None, ALU.mult, ALU.bypass, rs5[1], x5[half, c])
                else:
                    ev = A(lambda e, y=y, r5=r5: e.activation(y, y, ACT.Copy, scale=r5), rs5[1], x5[half, c])
                stores.append(dma(f"out{half}{c}", o[half, :, cs], y, ev))
    assert not waiting and at["block"] == len(plan) and at["unit"] == len(units)
    for st in stores:
        S.items.append((lambda e, st=st: e.wait_ge(*st), [], None))

    block = ctx.enter_context(nc.Block())

    @block.sync
    def _(eng):
        S.play(eng)

    @block.tensor
    def _(eng):
        T.play(eng)

    @block.scalar
    def _(eng):
        A.play(eng)

    @block.vector
    def _(eng):
        V.play(eng)

    @block.gpsimd
    def _(eng):
        G.play(eng)

    ctx.close()


_INS = ["x", "w_in", "b_gate", "gm_norm_g", "s5_w_glu", "s5_b_glu", "w_branch", "w_out",
        "w_mlp_in", "w_mlp_out", "final_g", "w_in_2", "w_gate_2", "b_gate_2", "b_glu_2",
        "w_a_out_2", "w_pool_grp_2", "w_b_out_2",
        "w_c_out_2", "w_o_2", "w_up_2", "w_down_2", "g_final_2"]


def layouts(v):
    r = {}
    r["cst"], r["pmat"] = consts()
    r["vecs"] = np.concatenate([v[n].reshape(-1, P) for n in VECS]).T
    r["x_t"] = v["x"][0].T
    r["gm_wt"] = v["gm_w_s"][0].transpose(2, 0, 1)
    taps = np.concatenate([v["w_dw_a_2"][0], v["w_dw_c_2"][0]])
    r["taps"] = taps.reshape(34, 6, P).transpose(2, 1, 0)
    rows = [v["s5_lambda_re"][0], v["s5_lambda_im"][0], np.broadcast_to(v["s5_log_dt"][0][:, None], (64, 64))]
    r["s5_p"] = np.stack([t.reshape(32, P).T for t in rows], 1)
    bt = np.zeros((4, 2, 16, 2, 8, 2, 64), np.float32)
    ct = np.zeros((2, 64, 2, 32, 2, 16), np.float32)
    for i, n in enumerate(("re", "im")):
        b = v["s5_b_" + n][0].reshape(8, 4, 2, 64, 16)
        c = v["s5_c_" + n][0].reshape(32, 2, 16, 64)
        for g in range(2):
            bt[:, g, :, i, :, g, :] = b[:, :, g].transpose(1, 3, 0, 2)
            ct[g, :, i, :, g, :] = c[:, g].transpose(2, 0, 1)
    r["s5_bt"] = bt.reshape(P, 2048)
    r["s5_ct"] = ct.reshape(P, 2, 1024)
    return r


def kernel(**inputs):
    import numpy as _np
    import concourse.bacc as _bacc
    from concourse import mybir as _mybir
    from concourse.bass_utils import run_bass_kernel_spmd as _run

    nc = _bacc.Bacc("TRN2", target_bir_lowering=False, num_devices=1)
    arrays, aps = {}, {}
    inputs = {n: _np.asarray(v) for n, v in inputs.items()}
    placed = layouts(inputs)
    for name in _INS + list(placed):
        v = _np.ascontiguousarray(placed[name] if name in placed else inputs[name])
        arrays[f"in_{name}_dram"] = v
        aps[name] = nc.dram_tensor(f"in_{name}_dram", v.shape, _mybir.dt.from_np(v.dtype), kind="ExternalInput").ap()
    out = nc.dram_tensor("out_0_dram", (1, L, D), F32, kind="ExternalOutput").ap()
    build(nc, aps, out)
    r = _run(nc, [arrays], core_ids=[0])
    return r.results[0]["out_0_dram"]
```
